# Optimizing a Trainium2 kernel written in Bass

```python
import jax, jax.numpy as jnp
from jax import lax
import numpy as np

D_MODEL = 1024
BATCH = 1
SEQ = 2048
DEPTH = 1

MIX_WIDTH = D_MODEL
CONV_WIDTH = MIX_WIDTH // 2
CONV_GROUPS = 8
CONV_K = 3
GMLP_WIDTH = MIX_WIDTH - CONV_WIDTH
GMLP_HEADS = 8
GMLP_HEAD_DIM = GMLP_WIDTH // GMLP_HEADS
CHUNK = 128
IN_COLS = 3 * CONV_WIDTH + 2 * GMLP_WIDTH
MEM_LEN = 256
XA_HEADS = 4
XA_HEAD_DIM = D_MODEL // XA_HEADS
N_GROUPS = 4
EXPERTS_PER_GROUP = 8
N_EXPERTS = N_GROUPS * EXPERTS_PER_GROUP
TOP_K = 2
D_EXPERT = D_MODEL // 2
MOE_BLOCK = 128
EPS = 1e-6

kernel_name = "hymba_conv_gmlp_hmoe_layer"

def rmsnorm(x, g):
    xf = x.astype(jnp.float32)
    y = xf * lax.rsqrt(jnp.mean(xf * xf, axis=-1, keepdims=True) + EPS)
    return (y * g.astype(jnp.float32)).astype(x.dtype)

def hybrid_mixer(h, w_in, conv_w, g_v, w_s, b_s, g_out_conv, g_out_gmlp, w_out):
    B_, S_, _ = h.shape
    proj = h @ w_in
    gate_b, gate_c, xc, u, v = jnp.split(
        proj, [CONV_WIDTH, 2 * CONV_WIDTH, 3 * CONV_WIDTH, 3 * CONV_WIDTH + GMLP_WIDTH], axis=-1)

    z = gate_c * xc
    zc = lax.conv_general_dilated(
        z, conv_w[:, None, :].astype(z.dtype), window_strides=(1,),
        padding=[(CONV_K - 1, 0)], dimension_numbers=('NWC', 'WIO', 'NWC'),
        feature_group_count=CONV_WIDTH)
    y_a = gate_b * zc

    u = jax.nn.gelu(u)
    v = jax.nn.gelu(v).reshape(B_, S_, GMLP_HEADS, GMLP_HEAD_DIM)
    v = rmsnorm(v, g_v.reshape(GMLP_HEADS, GMLP_HEAD_DIM))
    v = v.reshape(B_, S_ // CHUNK, CHUNK, GMLP_HEADS, GMLP_HEAD_DIM)
    causal = jnp.tril(jnp.ones((CHUNK, CHUNK), dtype=bool))
    ws = jnp.where(causal[None], w_s, 0.0).astype(v.dtype)
    s = jnp.einsum('hts,bcshd->bcthd', ws, v) + b_s.T.astype(v.dtype)[:, :, None]
    y_b = u * s.reshape(B_, S_, GMLP_WIDTH)

    y = jnp.concatenate([rmsnorm(y_a, g_out_conv), rmsnorm(y_b, g_out_gmlp)], axis=-1)
    return y @ w_out

def memory_cross_attention(h, mem_n, w_q, w_k, w_v, w_o):
    B_, S_, _ = h.shape
    M_ = mem_n.shape[1]
    q = (h @ w_q).reshape(B_, S_, XA_HEADS, XA_HEAD_DIM)
    k = (mem_n @ w_k).reshape(B_, M_, XA_HEADS, XA_HEAD_DIM)
    v = (mem_n @ w_v).reshape(B_, M_, XA_HEADS, XA_HEAD_DIM)
    scores = jnp.einsum('bshd,bmhd->bhsm', q, k).astype(jnp.float32) * (XA_HEAD_DIM ** -0.5)
    p = jax.nn.softmax(scores, axis=-1).astype(v.dtype)
    o = jnp.einsum('bhsm,bmhd->bshd', p, v).reshape(B_, S_, D_MODEL)
    return o @ w_o

def hierarchical_moe(h, w_grp, b_grp, w_rt, b_rt, w_gate, w_up, w_down):
    B_, S_, D_ = h.shape
    T = B_ * S_
    xt = h.reshape(T, D_)
    grp_prob = jax.nn.softmax((xt @ w_grp).astype(jnp.float32) + b_grp.astype(jnp.float32), axis=-1)
    grp_p, grp_idx = lax.top_k(grp_prob, 1)
    exp_logits = ((xt @ w_rt).astype(jnp.float32) + b_rt.astype(jnp.float32)).reshape(
        T, N_GROUPS, EXPERTS_PER_GROUP)
    in_grp = jnp.take_along_axis(exp_logits, grp_idx[:, :, None], axis=1)[:, 0]
    top_logit, top_local = lax.top_k(in_grp, TOP_K)
    gates = jax.nn.softmax(top_logit, axis=-1) * grp_p
    expert = grp_idx * EXPERTS_PER_GROUP + top_local

    A = T * TOP_K
    e_flat = expert.reshape(A)
    g_flat = gates.reshape(A)
    tok = jnp.repeat(jnp.arange(T, dtype=jnp.int32), TOP_K)
    order = jnp.argsort(e_flat)
    e_sorted = e_flat[order]
    tok_sorted = tok[order]
    g_sorted = g_flat[order]
    counts = jnp.bincount(e_flat, length=N_EXPERTS)
    starts = jnp.cumsum(counts) - counts
    padded = ((counts + MOE_BLOCK - 1) // MOE_BLOCK) * MOE_BLOCK
    pad_ends = jnp.cumsum(padded)
    pad_starts = pad_ends - padded
    dest = pad_starts[e_sorted] + jnp.arange(A, dtype=jnp.int32) - starts[e_sorted]
    n_blocks = (A + MOE_BLOCK - 1) // MOE_BLOCK + N_EXPERTS
    cap = n_blocks * MOE_BLOCK
    buf = jnp.zeros((cap, D_), xt.dtype).at[dest].set(xt[tok_sorted])
    block_start = jnp.arange(n_blocks, dtype=jnp.int32) * MOE_BLOCK
    block_expert = jnp.minimum(jnp.searchsorted(pad_ends, block_start, side='right'), N_EXPERTS - 1)

    def expert_block(args):
        xb, e = args
        return (jax.nn.silu(xb @ w_gate[e]) * (xb @ w_up[e])) @ w_down[e]

    y_buf = lax.map(expert_block, (buf.reshape(n_blocks, MOE_BLOCK, D_), block_expert)).reshape(cap, D_)
    y_assign = y_buf[dest] * g_sorted[:, None].astype(y_buf.dtype)
    out = jnp.zeros((T, D_), y_buf.dtype).at[tok_sorted].add(y_assign)
    return out.reshape(B_, S_, D_)

def setup_inputs(seed: int = 0) -> dict:
    key = jax.random.key(seed)
    ks = jax.random.split(key, 32)
    f32 = jnp.float32

    def nrm(k, shape, fan_in):
        return jax.random.normal(k, shape, f32) * (fan_in ** -0.5)

    def gain(k, shape):
        return 1.0 + 0.01 * jax.random.normal(k, shape, f32)

    L = DEPTH
    return {
        "x": jax.random.normal(ks[0], (BATCH, SEQ, D_MODEL), f32),
        "mem": jax.random.normal(ks[1], (BATCH, MEM_LEN, D_MODEL), f32),
        "g_mix": gain(ks[2], (L, D_MODEL)),
        "w_in": nrm(ks[3], (L, D_MODEL, IN_COLS), D_MODEL),
        "conv_w": nrm(ks[4], (L, CONV_K, CONV_WIDTH), CONV_K),
        "g_v": gain(ks[5], (L, GMLP_WIDTH)),
        "w_s": nrm(ks[6], (L, GMLP_HEADS, CHUNK, CHUNK), CHUNK),
        "b_s": gain(ks[7], (L, GMLP_HEADS, CHUNK)),
        "g_out_conv": gain(ks[8], (L, CONV_WIDTH)),
        "g_out_gmlp": gain(ks[9], (L, GMLP_WIDTH)),
        "w_out": nrm(ks[10], (L, MIX_WIDTH, D_MODEL), MIX_WIDTH),
        "g_xattn": gain(ks[11], (L, D_MODEL)),
        "g_mem": gain(ks[12], (L, D_MODEL)),
        "w_q": nrm(ks[13], (L, D_MODEL, D_MODEL), D_MODEL),
        "w_k": nrm(ks[14], (L, D_MODEL, D_MODEL), D_MODEL),
        "w_v": nrm(ks[15], (L, D_MODEL, D_MODEL), D_MODEL),
        "w_o": nrm(ks[16], (L, D_MODEL, D_MODEL), D_MODEL),
        "g_ffn": gain(ks[17], (L, D_MODEL)),
        "w_grp": nrm(ks[18], (L, D_MODEL, N_GROUPS), D_MODEL),
        "b_grp": 0.01 * jax.random.normal(ks[19], (L, N_GROUPS), f32),
        "w_rt": nrm(ks[20], (L, D_MODEL, N_EXPERTS), D_MODEL),
        "b_rt": 0.01 * jax.random.normal(ks[21], (L, N_EXPERTS), f32),
        "w_gate": nrm(ks[22], (L, N_EXPERTS, D_MODEL, D_EXPERT), D_MODEL),
        "w_up": nrm(ks[23], (L, N_EXPERTS, D_MODEL, D_EXPERT), D_MODEL),
        "w_down": nrm(ks[24], (L, N_EXPERTS, D_EXPERT, D_MODEL), D_EXPERT),
        "g_final": gain(ks[25], (D_MODEL,)),
    }

def reference(x, mem, g_mix, w_in, conv_w, g_v, w_s, b_s, g_out_conv, g_out_gmlp, w_out,
              g_xattn, g_mem, w_q, w_k, w_v, w_o, g_ffn, w_grp, b_grp, w_rt, b_rt,
              w_gate, w_up, w_down, g_final):
    for l in range(DEPTH):
        x = x + hybrid_mixer(rmsnorm(x, g_mix[l]), w_in[l], conv_w[l], g_v[l], w_s[l], b_s[l],
                             g_out_conv[l], g_out_gmlp[l], w_out[l])
        x = x + memory_cross_attention(rmsnorm(x, g_xattn[l]), rmsnorm(mem, g_mem[l]),
                                       w_q[l], w_k[l], w_v[l], w_o[l])
        x = x + hierarchical_moe(rmsnorm(x, g_ffn[l]), w_grp[l], b_grp[l], w_rt[l], b_rt[l],
                                 w_gate[l], w_up[l], w_down[l])
    return rmsnorm(x, g_final)


_drawn_inputs = setup_inputs


def setup_inputs(seed=0):
    import zlib

    import numpy as np

    out = dict(_drawn_inputs(seed))
    spreads = {}
    factors = {'g_mix': 3.029,
     'g_v': 8.0,
     'b_s': 5.682,
     'g_out_conv': 5.056,
     'g_out_gmlp': 4.956,
     'g_xattn': 8.0,
     'g_mem': 8.0,
     'g_ffn': 3.985,
     'b_grp': 5.406,
     'b_rt': 7.5,
     'g_final': 5.612}
    for name, (base, spread) in spreads.items():
        noise = np.random.default_rng([zlib.crc32(name.encode()), seed]).standard_normal(out[name].shape)
        drawn = base * np.exp(spread * noise) if base else spread * noise
        out[name] = __import__('jax').numpy.asarray(drawn.astype(out[name].dtype))
    for name, factor in factors.items():
        out[name] = (out[name] * factor).astype(out[name].dtype)
    return out
```

```python
from contextlib import ExitStack

import concourse.bass as bass
import concourse.mybir as mybir
import numpy as np

F32 = mybir.dt.float32
F32R = mybir.dt.float32r
BF16 = mybir.dt.bfloat16
I32 = mybir.dt.int32
U32 = mybir.dt.uint32
ALU = mybir.AluOpType
ACT = mybir.ActivationFunctionType
AX = mybir.AxisListType

P = 128
D = 1024
KD = D // P
SEQ = 2048
TILES = SEQ // P
CONV = 512
GMLP = 512
HEADS = 8
HEAD = GMLP // HEADS
CHUNK = 128
CONV_K = 3
MEM = 256
XHEADS = 4
XDIM = D // XHEADS
GROUPS = 4
PER_GROUP = 8
EXPERTS = GROUPS * PER_GROUP
DE = 512
EPS = 1e-6

SUPER = 512
SUPERS = SEQ // SUPER
ST = SUPER // P

SLOT = 2 * P
SLOTS = SEQ * 2 // SLOT + EXPERTS - 1
LISTED = 2 * (SLOTS + 1)

COLS = {}
at = 0
for name, n in (("g_mix", 8), ("g_out_conv", 4), ("g_out_gmlp", 4), ("g_xattn", 8), ("g_ffn", 8),
                ("g_v", 4), ("conv_w", 12)):
    COLS[name] = at
    at += n
GAIN_ROWS = at


def f32(ap):
    return ap.bitcast(F32)


def snap(engine, value):
    return value if isinstance(value, int) else engine.snap(value)


def semaphores(nc, ctx):
    made = []
    ctx.callback(nc.all_engine_barrier)
    ctx.callback(lambda: nc.clear_and_free_semaphores(made))

    def make(name):
        made.append(nc.alloc_semaphore(name))
        return made[-1]
    return make


def wait_apart(engine, passed, *waits):
    waits = [(semaphore, snap(engine, value)) for semaphore, value in waits]
    for semaphore, value in waits:
        engine.wait_ge(semaphore, value)
    engine.sem_inc(passed, 1)


def product(pe, out, ahi, alo, bhi, blo, first, last):
    pe.matmul(out, ahi, bhi, start=first, stop=False)
    pe.matmul(out, ahi, blo, start=False, stop=False)
    return pe.matmul(out, alo, bhi, start=False, stop=last)


class Kept:

    def __init__(self, nc, ctx):
        sb = lambda n, s, d=F32: ctx.enter_context(nc.sbuf_tensor(n, s, d))
        self.ident = sb("ident", [P, P])
        self.ones = sb("ones", [P, 2])
        self.cols = sb("gain_cols", [P, GAIN_ROWS])
        self.logits = sb("logits", [P, TILES, GROUPS + EXPERTS])


class Fold:

    def __init__(self, nc):
        self.nc, self.ctx = nc, ExitStack()

    def __enter__(self):
        sb = lambda n: self.ctx.enter_context(self.nc.sbuf_tensor(n, [P, KD, XHEADS * MEM], F32R))
        self.a_hi, self.a_lo, self.b_hi, self.b_lo = (sb(n) for n in ("A_hi", "A_lo", "B_hi", "B_lo"))
        return self

    def __exit__(self, *exc):
        self.ctx.close()


def setup(nc, keep, ins):
    with ExitStack() as ctx:
        rows = ctx.enter_context(nc.sbuf_tensor("gain_rows", [GAIN_ROWS, P], F32))
        ps = ctx.enter_context(nc.psum_tensor("setup_ps", [P, 512], F32))
        sem = semaphores(nc, ctx)
        loaded = sem("gains_loaded")
        zeroed = sem("ident_zeroed")
        ident_ready = sem("ident_ready")
        turned = sem("gains_turned")
        kept = sem("gains_kept")
        block = ctx.enter_context(nc.Block())

        @block.sync
        def _(sp):
            for name in COLS:
                n = ins[name].shape[1] // P if name != "conv_w" else CONV_K * CONV // P
                src = ins[name].rearrange("a (k p) -> (a k) p", p=P) if name != "conv_w" else \
                    ins[name].rearrange("a j (k p) -> (a j k) p", p=P)
                sp.dma_start(rows[COLS[name]:COLS[name] + n, :], src).then_inc(loaded, 16)

        @block.gpsimd
        def _(pool):
            pool.memset(keep.ident[:], 0.0).then_inc(zeroed, 1)
            pool.memset(keep.ones[:], 1.0).then_inc(zeroed, 1)
            pool.wait_ge(zeroed, 1)
            pool.affine_select(out=keep.ident[:], in_=keep.ident[:], compare_op=ALU.not_equal, fill=1.0,
                               base=0, pattern=[[-1, P]], channel_multiplier=1).then_inc(ident_ready, 1)

        @block.tensor
        def _(pe):
            pe.wait_ge(loaded, 16 * len(COLS))
            pe.wait_ge(ident_ready, 1)
            pe.transpose(ps[:, 0:GAIN_ROWS], rows[:], keep.ident[0:GAIN_ROWS, 0:GAIN_ROWS]).then_inc(turned, 1)

        @block.vector
        def _(dve):
            dve.wait_ge(turned, 1)
            dve.tensor_copy(keep.cols[:], ps[:, 0:GAIN_ROWS]).then_inc(kept, 1)


def mixer(nc, keep, ins, x1):
    UNITS = 4 + 4 * 4
    W_OUT = KD
    PAIR = (4, 6, 0)
    w_in, w_out, x = ins["w_in"], ins["w_out"], ins["x"]
    col = lambda name, k: keep.cols[:, COLS[name] + k:COLS[name] + k + 1]
    with ExitStack() as ctx:
        sb = lambda n, s, d=F32: ctx.enter_context(nc.sbuf_tensor(n, s, d))
        sem = semaphores(nc, ctx)
        bank = ctx.enter_context(nc.psum_tensor("mix_ps", [P, 8, 512], F32))

        wo_hi = sb("wo_hi", [P, KD, D], F32R)
        wo_lo = sb("wo_lo", [P, KD, D], F32R)
        w_raw = sb("w_raw", [P, 2, 1024])
        w_hi = sb("w_hi", [P, 2, 1024], F32R)
        w_lo = sb("w_lo", [P, 2, 1024], F32R)
        xin = sb("xin", [P, 2, D])
        gain = sb("gain_mix", [P, D])
        square = sb("square_out", [P, D], BF16)
        hT_hi = sb("hT_hi", [P, KD, SUPER], F32R)
        hT_lo = sb("hT_lo", [P, KD, SUPER], F32R)
        yT_hi = sb("yT_hi", [P, KD, SUPER], F32R)
        yT_lo = sb("yT_lo", [P, KD, SUPER], F32R)
        v = sb("v", [P, ST, GMLP])
        wsT = sb("wsT", [P, HEADS, CHUNK])
        bias = sb("b_s_rows", [P, HEADS // 2, CHUNK])
        c_sb = sb("c_sb", [P, SUPER])
        z = sb("z", [P, SUPER + CONV_K - 1])
        halo = sb("halo", [P, 4, CONV_K - 1])
        ya = sb("ya", [P, SUPER])
        u_sb = sb("u_sb", [P, SUPER])
        yb = sb("yb", [P, SUPER])
        sq = sb("sq", [P, SUPER])
        sum_a = sb("sum_a", [P, SUPER])
        sum_b = sb("sum_b", [P, SUPER])
        xres = sb("xres", [P, D])
        ssx = sb("ssx", [P, 2])
        rx = sb("rx", [P, 2])
        ssv = sb("ssv", [P, ST, HEADS])
        rv = sb("rv", [P, ST, HEADS])
        ssy = sb("ssy", [P, 2 * ST])
        ry = sb("ry", [P, 2 * ST])
        half = sb("neg_half", [P, HEADS])

        raw_in = [sem(f"w_raw_in{b}") for b in range(2)]
        hi_done, lo_done, unit_used = sem("w_hi_done"), sem("w_lo_done"), sem("w_unit_used")
        ws_in, ws_turned, ws_copied, ws_masked = sem("ws_in"), sem("ws_turned"), sem("ws_copied"), sem("ws_masked")
        pool_passed, sp_passed = sem("pool_passed"), sem("sp_passed")
        const_in, pool_const, halo_zero = sem("const_in"), sem("pool_const"), sem("halo_zero")
        x_in = [sem(f"x_in{b}") for b in range(2)]
        x_sq, x_ms, x_r, x_scaled = sem("x_sq"), sem("x_ms"), sem("x_r"), sem("x_scaled")
        xT_ps, hT_hi_done, hT_lo_done = sem("xT_ps"), sem("hT_hi_done"), sem("hT_lo_done")
        v_gelu, v_sq, v_ss, v_ms, v_r, v_done = [sem(n) for n in (
            "v_gelu", "v_sq", "v_ss", "v_ms", "v_r", "v_done")]
        c_done, z_halo, z_done, conv0, conv1, conv2, ya_done = [sem(n) for n in (
            "c_done", "z_halo", "z_done", "conv0", "conv1", "conv2", "ya_done")]
        u_done, s_ps, t_done, yb_done, halo_kept = [sem(n) for n in (
            "u_done", "s_ps", "t_done", "yb_done", "halo_kept")]
        y_hi, y_lo, y_sq, y_sum = [sem(n) for n in ("y_hi", "y_lo", "y_sq", "y_sum")]
        ssy_ps, ssy_done, ry_ms, ry_done = [sem(n) for n in ("ssy_ps", "ssy_done", "ry_ms", "ry_done")]
        o_ps, o_done, res_in, x1_out = [sem(n) for n in ("o_ps", "o_done", "res_in", "x1_out")]
        block = ctx.enter_context(nc.Block())

        def unit_source(u):
            if u < 4:
                return w_in[0, 2 * u * P:(2 * u + 2) * P, 3 * CONV + GMLP:].rearrange("(k p) n -> p k n", p=P)
            g, which = divmod(u - 4, 4)
            start = {0: CONV, 1: 2 * CONV, 2: 0, 3: 3 * CONV}[which] + g * P
            return w_in[0, :, start:start + P].rearrange("(k p) n -> p k n", p=P)

        def as_unit(tile, u):
            return tile[:, u % 2].rearrange("p (k n) -> p k n", k=2 if u < 4 else KD)

        @block.sync
        def _(sp):
            def load_x(tiles, t):
                row = snap(sp, (tiles + t) * P)
                sp.wait_ge(xT_ps, tiles + t + 1)
                sp.dma_start(xin[:, t % 2], x[0, bass.ds(row, P), :]).then_inc(x_in[t % 2], 16)

            def load_unit(units, u):
                sp.wait_ge(hi_done, units + (u + 1))
                sp.wait_ge(lo_done, units + (u + 1))
                sp.dma_start(as_unit(w_raw, u), unit_source(u)).then_inc(raw_in[u % 2], 16)

            def step(i, last):
                units = snap(sp, i * UNITS + W_OUT)
                units_next = snap(sp, i * UNITS + (W_OUT + UNITS))
                tiles = snap(sp, i * ST)
                tiles_next = snap(sp, i * ST + ST)
                for u in range(2, UNITS):
                    load_unit(units, u)
                    if u == 10 and not last:
                        load_x(tiles_next, 0)
                        load_x(tiles_next, 1)
                for t in range(ST):
                    row = snap(sp, (tiles + t) * P)
                    sp.dma_start(xres[:], x[0, bass.ds(row, P), :]).then_inc(res_in, 16)
                    if t < 2 and not last:
                        load_x(tiles_next, t + 2)
                    if t == 2 and not last:
                        load_unit(units_next, 0)
                        load_unit(units_next, 1)
                    done = snap(sp, (tiles + t) * 16 + 16)
                    both = snap(sp, (tiles + t) * 2 + 5)
                    sp.wait_ge(o_done, both)
                    sp.dma_start(x1[bass.ds(row, P), :], xres[:]).then_inc(x1_out, 16)
                    wait_apart(sp, sp_passed, (x1_out, done))

            sp.dma_start(gain[:], ins["g_mix"].broadcast_to((P, D))).then_inc(const_in, 16)
            for h in range(HEADS):
                sp.dma_start(bias[(h % 2) * HEAD:(h % 2 + 1) * HEAD, h // 2, :],
                             ins["b_s"][0, h:h + 1, :].broadcast_to((HEAD, CHUNK))).then_inc(const_in, 16)
            load_x(0, 0)
            load_x(0, 1)
            sp.dma_start(v[:, 0:2, :].rearrange("p a (h s) -> p (a h) s", s=CHUNK),
                         ins["w_s"][0].rearrange("h t s -> t h s")).then_inc(ws_in, 16)
            load_x(0, 2)
            load_x(0, 3)
            for k in range(W_OUT):
                sp.wait_ge(hi_done, k + 1)
                sp.wait_ge(lo_done, k + 1)
                sp.dma_start(w_raw[:, k % 2], w_out[0, k * P:(k + 1) * P, :]).then_inc(raw_in[k % 2], 16)
            load_unit(W_OUT, 0)
            load_unit(W_OUT, 1)
            with sp.Fori(0, SUPERS - 1) as i:
                step(i, False)
            step(SUPERS - 1, True)

        @block.gpsimd
        def _(pool):
            def inverse_root(ss, out, n, ready, ms, done, k, ahead=0):
                wait_apart(pool, pool_passed, (ready, k + ahead))
                pool.tensor_scalar(out, ss, 1.0 / n, EPS, ALU.mult, ALU.add).then_inc(ms, 1)
                pool.wait_ge(ms, k)
                pool.tensor_tensor(out, out, half[:, 0:out.shape[-1]], ALU.pow).then_inc(done, 1)

            def norm_x(tiles, t):
                pool.wait_ge(x_scaled, tiles + (t + 1))
                inverse_root(ssx[:, t % 2:t % 2 + 1], rx[:, t % 2:t % 2 + 1], D, x_sq, x_ms, x_r, tiles + (t + 1), 1)

            def add_square(target, k, first):
                wait_apart(pool, pool_passed, (y_sum, k), (y_sq, k + 2))
                if first:
                    pool.tensor_copy(target, sq[:]).then_inc(y_sum, 1)
                else:
                    pool.tensor_tensor(target, target, sq[:], ALU.add).then_inc(y_sum, 1)

            def step(i, last):
                groups = snap(pool, i * 4)
                ys = snap(pool, i * 8)
                tiles = snap(pool, i * ST)
                tiles_next = snap(pool, i * ST + ST)
                for t in range(ST):
                    inverse_root(ssv[:, t], rv[:, t], HEAD, v_ss, v_ms, v_r, tiles + (t + 1), 1)
                pool.wait_ge(ssy_ps, snap(pool, i + 1))
                for g in range(4):
                    add_square(sum_a[:], ys + (2 * g + 1), g == 0)
                    pool.wait_ge(u_done, groups + (g + 2))
                    pool.wait_ge(t_done, groups + (g + 3))
                    pool.tensor_tensor(yb[:], yb[:], u_sb[:], ALU.mult).then_inc(yb_done, 1)
                    add_square(sum_b[:], ys + (2 * g + 2), g == 0)
                if not last:
                    norm_x(tiles_next, 0)
                    norm_x(tiles_next, 1)
                n = snap(pool, i + 1)
                inverse_root(ssy[:], ry[:], CONV, ssy_done, ry_ms, ry_done, n)
                if not last:
                    norm_x(tiles_next, 2)
                    norm_x(tiles_next, 3)

            pool.memset(half[:], -0.5).then_inc(pool_const, 1)
            pool.wait_ge(pool_const, 1)
            pool.sem_inc(y_sum, 1)
            pool.sem_inc(yb_done, 1)
            pool.sem_inc(x_r, 2)
            for t in range(ST):
                norm_x(0, t)
            pool.wait_ge(ws_copied, 1)
            pool.affine_select(out=wsT[:], in_=wsT[:], compare_op=ALU.is_ge, fill=0.0, base=0,
                               pattern=[[0, HEADS], [1, CHUNK]], channel_multiplier=-1).then_inc(ws_masked, 1)
            with pool.Fori(0, SUPERS - 1) as i:
                step(i, False)
            step(SUPERS - 1, True)

        @block.scalar
        def _(act):
            def split_raw(out, uses16, u, k):
                act.wait_ge(raw_in[u % 2], uses16)
                act.activation(out, w_raw[:, u % 2], ACT.Copy).then_inc(hi_done, 1)

            def split_unit(units, uses16, u):
                act.wait_ge(unit_used, units + (u + 1 - W_OUT))
                split_raw(w_hi[:, u % 2], uses16 + 16 * (u // 2 + 1), u, None)

            def square_x(tiles, halves16, t):
                act.wait_ge(x_in[t % 2], halves16 + 16 * (t // 2 + 1))
                act.wait_ge(x_r, tiles + (t + 1))
                act.wait_ge(x_sq, tiles + (t + 1))
                act.activation(square[:], xin[:, t % 2], ACT.Square,
                               accum_out=ssx[:, t % 2:t % 2 + 1]).then_inc(x_sq, 1)

            def turn_x(tiles, t):
                act.wait_ge(xT_ps, tiles + (t + 3))
                act.activation(hT_hi[:, :, t * P:(t + 1) * P],
                               bank[:, 2:4, :].rearrange("p b (k n) -> p (b k) n", n=P), ACT.Copy).then_inc(hT_hi_done, 1)

            def keep_y(chunk, tile, ready, k_ready, y_index):
                act.wait_ge(ready, k_ready)
                act.activation(yT_hi[:, chunk], tile[:], ACT.Copy).then_inc(y_hi, 1)
                act.wait_ge(y_sum, y_index + 1)
                act.activation(sq[:], tile[:], ACT.Square).then_inc(y_sq, 1)

            def step(i, last):
                units = snap(act, i * UNITS + W_OUT)
                units_next = snap(act, i * UNITS + (W_OUT + UNITS))
                uses = snap(act, i * (UNITS * 8) + W_OUT * 8)
                uses_next = snap(act, i * (UNITS * 8) + (W_OUT + UNITS) * 8)
                groups = snap(act, i * 4)
                ys = snap(act, i * 8)
                tiles = snap(act, i * ST)
                tiles_next = snap(act, i * ST + ST)
                halves_next = snap(act, (i + 1) * (ST * 8))
                used = snap(act, i * UNITS + 2)
                for u in range(UNITS):
                    g, which = divmod(u - 4, 4)
                    if u == 3:
                        act.wait_ge(s_ps, groups + 1)
                        for t in range(ST):
                            act.wait_ge(unit_used, used + (u + 1))
                            act.activation(v[:, t], bank[:, t], ACT.Gelu_apprx_tanh).then_inc(v_gelu, 1)
                    if u >= 4 and which == 0:
                        act.wait_ge(unit_used, used + (u + 1))
                        act.wait_ge(z_done, groups + (g + 1))
                        act.activation(c_sb[:], bank[:, 4], ACT.Copy).then_inc(c_done, 1)
                        if g:
                            keep_y(4 + g - 1, yb, yb_done, groups + (g + 1), ys + (2 * g - 1))
                    if u >= 4 and which == 3:
                        act.wait_ge(unit_used, used + (u + 1))
                        act.wait_ge(yb_done, groups + (g + 1))
                        act.activation(u_sb[:], bank[:, 7], ACT.Gelu_apprx_tanh).then_inc(u_done, 1)
                        if g == 0:
                            act.wait_ge(o_ps, ys + 1)
                        keep_y(g, ya, ya_done, groups + (g + 2), ys + 2 * g)
                    if u + 2 < UNITS:
                        split_unit(units, uses, u + 2)
                if not last:
                    square_x(tiles_next, halves_next, 0)
                keep_y(7, yb, yb_done, groups + 5, ys + 7)
                if not last:
                    square_x(tiles_next, halves_next, 1)
                    for t in range(ST):
                        turn_x(tiles_next, t)
                        if t < 2:
                            square_x(tiles_next, halves_next, t + 2)
                        if t == 2:
                            split_unit(units_next, uses_next, 0)
                            split_unit(units_next, uses_next, 1)

            act.sem_inc(x_sq, 1)
            act.sem_inc(y_sq, 2)
            act.sem_inc(hi_done, 2)
            act.sem_inc(c_done, 1)
            act.sem_inc(u_done, 1)
            act.sem_inc(hT_hi_done, 1)
            for t in range(ST):
                if t >= 1:
                    turn_x(0, t - 1)
                square_x(0, 0, t)
            turn_x(0, 3)
            for k in range(W_OUT):
                act.wait_ge(raw_in[k % 2], 16 * (k // 2 + 1))
                gain_col = col("g_out_conv", k) if k < 4 else col("g_out_gmlp", k - 4)
                act.activation(wo_hi[:, k], w_raw[:, k % 2], ACT.Copy, scale=gain_col).then_inc(hi_done, 1)
            split_unit(W_OUT, W_OUT * 8, 0)
            split_unit(W_OUT, W_OUT * 8, 1)
            with act.Fori(0, SUPERS - 1) as i:
                step(i, False)
            step(SUPERS - 1, True)

        @block.vector
        def _(dve):
            def split_unit(units, u):
                dve.wait_ge(hi_done, units + (u + 3))
                dve.wait_ge(unit_used, units + (u + 1 - W_OUT))
                dve.tensor_tensor(w_lo[:, u % 2], w_raw[:, u % 2], f32(w_hi[:, u % 2]), ALU.subtract).then_inc(lo_done, 1)

            def scale_x(tiles, t):
                dve.wait_ge(x_r, tiles + (t + 3))
                if t == 0:
                    dve.wait_ge(const_in, 16 * (1 + HEADS))
                dve.scalar_tensor_tensor(xin[:, t % 2], xin[:, t % 2], rx[:, t % 2:t % 2 + 1], gain[:],
                                         ALU.mult, ALU.mult).then_inc(x_scaled, 1)

            def turn_x(tiles, t):
                dve.wait_ge(hT_hi_done, tiles + (t + 2))
                cols = slice(t * P, (t + 1) * P)
                dve.tensor_tensor(hT_lo[:, :, cols], bank[:, 2:4, :].rearrange("p b (k n) -> p (b k) n", n=P),
                                  f32(hT_hi[:, :, cols]), ALU.subtract).then_inc(hT_lo_done, 1)

            def lower_y(chunk, tile, k):
                dve.wait_ge(y_hi, k)
                dve.tensor_tensor(yT_lo[:, chunk], tile[:], f32(yT_hi[:, chunk]), ALU.subtract).then_inc(y_lo, 1)

            def step(i, last):
                units = snap(dve, i * UNITS + W_OUT)
                units_next = snap(dve, i * UNITS + (W_OUT + UNITS))
                used = snap(dve, i * UNITS + 2)
                groups = snap(dve, i * 4)
                ys = snap(dve, i * 8)
                tiles = snap(dve, i * ST)
                tiles_next = snap(dve, i * ST + ST)
                for u in range(UNITS):
                    g, which = divmod(u - 4, 4)
                    if u == 3:
                        for t in range(ST):
                            dve.wait_ge(v_gelu, tiles + (t + 1))
                            dve.wait_ge(v_ss, tiles + (t + 1))
                            dve.tensor_tensor(z[:, 0:GMLP], v[:, t], v[:, t], ALU.mult).then_inc(v_sq, 1)
                            dve.wait_ge(v_sq, tiles + (t + 1))
                            dve.tensor_reduce(ssv[:, t], z[:, 0:GMLP].rearrange("p (h d) -> p h d", d=HEAD),
                                              AX.X, ALU.add).then_inc(v_ss, 1)
                    if u == 4:
                        for t in range(ST):
                            dve.wait_ge(v_r, tiles + (t + 1))
                            heads = v[:, t].rearrange("p (h d) -> p h d", d=HEAD)
                            dve.tensor_tensor(heads, heads, rv[:, t].unsqueeze(2).broadcast_to((P, HEADS, HEAD)),
                                              ALU.mult).then_inc(v_done, 1)
                        dve.wait_ge(v_ss, tiles + (ST + 1))
                    if u >= 8 and which == 0:
                        lower_y(4 + g - 1, yb, ys + 2 * g)
                    if u >= 4 and which == 1:
                        dve.wait_ge(unit_used, used + (u + 1))
                        dve.wait_ge(c_done, groups + (g + 2))
                        dve.wait_ge(halo_kept, groups + (g + 1))
                        dve.tensor_copy(z[:, 0:2], halo[:, g]).then_inc(z_halo, 1)
                        dve.tensor_tensor(z[:, 2:], bank[:, 5], c_sb[:], ALU.mult).then_inc(z_done, 1)
                        dve.wait_ge(z_halo, groups + (g + 1))
                        dve.wait_ge(z_done, groups + (g + 2))
                        dve.wait_ge(y_sq, ys + (2 * g + 1))
                        dve.tensor_scalar(ya[:], z[:, 2:], col("conv_w", 8 + g), None, ALU.mult).then_inc(conv0, 1)
                        dve.wait_ge(conv0, groups + (g + 1))
                        dve.scalar_tensor_tensor(ya[:], z[:, 1:SUPER + 1], col("conv_w", 4 + g), ya[:],
                                                 ALU.mult, ALU.add).then_inc(conv1, 1)
                        dve.wait_ge(conv1, groups + (g + 1))
                        dve.scalar_tensor_tensor(ya[:], z[:, 0:SUPER], col("conv_w", g), ya[:],
                                                 ALU.mult, ALU.add).then_inc(conv2, 1)
                        dve.tensor_copy(halo[:, g], z[:, SUPER:]).then_inc(halo_kept, 1)
                    if u >= 4 and which == 2:
                        dve.wait_ge(unit_used, used + (u + 1))
                        dve.wait_ge(conv2, groups + (g + 1))
                        dve.tensor_tensor(ya[:], bank[:, 6], ya[:], ALU.mult).then_inc(ya_done, 1)
                    if u >= 4 and which == 3:
                        lower_y(g, ya, ys + (2 * g + 1))
                        dve.wait_ge(s_ps, groups + (g + 2))
                        dve.wait_ge(y_sq, ys + (2 * g + 2))
                        dve.scalar_tensor_tensor(
                            yb[:].rearrange("p (t n) -> p t n", n=P), bank[:, g % 2].rearrange("p (t n) -> p t n", n=P),
                            col("g_v", g), bias[:, g].unsqueeze(1).broadcast_to((P, ST, CHUNK)),
                            ALU.mult, ALU.add).then_inc(t_done, 1)
                    if u + 2 < UNITS:
                        split_unit(units, u + 2)
                if not last:
                    scale_x(tiles_next, 0)
                    scale_x(tiles_next, 1)
                lower_y(7, yb, ys + 8)
                n = snap(dve, i + 1)
                dve.wait_ge(ssy_ps, n + 1)
                dve.tensor_copy(ssy[:], bank[:, 2, 0:2 * ST]).then_inc(ssy_done, 1)
                dve.wait_ge(ry_done, n)
                for t in range(ST):
                    if not last:
                        turn_x(tiles_next, t)
                        if t < 2:
                            scale_x(tiles_next, t + 2)
                    res16 = snap(dve, (tiles + t) * 16 + 16)
                    for part in range(2):
                        k = 2 * t + part
                        dve.wait_ge(o_ps, ys + (k + 2))
                        if part == 0:
                            dve.wait_ge(res_in, res16)
                        else:
                            dve.wait_ge(o_done, ys + (k + 3))
                        pair = PAIR[k % 3]
                        dve.scalar_tensor_tensor(
                            xres[:], bank[:, pair:pair + 2].rearrange("p b n -> p (b n)"),
                            ry[:, part * ST + t:part * ST + t + 1], xres[:], ALU.mult, ALU.add).then_inc(o_done, 1)
                    if t == 2 and not last:
                        split_unit(units_next, 0)
                        split_unit(units_next, 1)

            dve.memset(halo[:], 0.0).then_inc(halo_zero, 1)
            dve.wait_ge(halo_zero, 1)
            dve.sem_inc(lo_done, 2)
            dve.sem_inc(z_done, 1)
            dve.sem_inc(ya_done, 1)
            dve.sem_inc(t_done, 2)
            dve.sem_inc(v_ss, 1)
            dve.sem_inc(halo_kept, 1)
            dve.sem_inc(hT_lo_done, 1)
            dve.sem_inc(o_done, 3)
            dve.sem_inc(x_scaled, 2)
            for t in range(ST):
                if t >= 1:
                    turn_x(0, t - 1)
                scale_x(0, t)
            turn_x(0, 3)
            dve.wait_ge(ws_turned, 1)
            dve.tensor_copy(wsT[:], bank[:, 0:2].rearrange("p b (h n) -> p (b h) n", n=CHUNK)).then_inc(ws_copied, 1)
            for k in range(W_OUT):
                gain_col = col("g_out_conv", k) if k < 4 else col("g_out_gmlp", k - 4)
                dve.wait_ge(hi_done, k + 3)
                dve.scalar_tensor_tensor(wo_lo[:, k], w_raw[:, k % 2], gain_col, f32(wo_hi[:, k]),
                                         ALU.mult, ALU.subtract).then_inc(lo_done, 1)
            split_unit(W_OUT, 0)
            split_unit(W_OUT, 1)
            with dve.Fori(0, SUPERS - 1) as i:
                step(i, False)
            step(SUPERS - 1, True)

        @block.tensor
        def _(pe):
            def turn_x(tiles, t):
                pe.wait_ge(x_scaled, tiles + (t + 3))
                pe.wait_ge(hT_hi_done, tiles + (t + 1))
                pe.wait_ge(hT_lo_done, tiles + (t + 1))
                for k in range(KD):
                    mm = pe.transpose(bank[:, 2 + k // 4, (k % 4) * P:(k % 4 + 1) * P],
                                      xin[:, t % 2, k * P:(k + 1) * P], keep.ident[:])
                mm.then_inc(xT_ps, 1)

            def step(i, last):
                units = snap(pe, i * UNITS + W_OUT)
                groups = snap(pe, i * 4)
                ys = snap(pe, i * 8)
                tiles = snap(pe, i * ST)
                tiles_next = snap(pe, i * ST + ST)
                pe.wait_ge(o_done, ys + 3)
                pe.wait_ge(hT_hi_done, tiles + (ST + 1))
                pe.wait_ge(hT_lo_done, tiles + (ST + 1))
                for u in range(UNITS):
                    pe.wait_ge(hi_done, units + (u + 3))
                    pe.wait_ge(lo_done, units + (u + 3))
                    g, which = divmod(u - 4, 4)
                    hi, lo = as_unit(w_hi, u), as_unit(w_lo, u)
                    if u < 4:
                        for kk in range(2):
                            for t in range(ST):
                                k, cols = 2 * u + kk, slice(t * P, (t + 1) * P)
                                mm = product(pe, bank[:, t], hT_hi[:, k, cols], hT_lo[:, k, cols],
                                             hi[:, kk], lo[:, kk], k == 0, k == KD - 1)
                        mm.then_inc(unit_used, 1)
                        continue
                    pe.wait_ge((c_done, z_done, ya_done, u_done)[which], groups + (g + 1))
                    for k in range(KD):
                        mm = product(pe, bank[:, 4 + which], hi[:, k], lo[:, k], hT_hi[:, k], hT_lo[:, k],
                                     k == 0, k == KD - 1)
                    mm.then_inc(unit_used, 1)
                    if which == 3:
                        pe.wait_ge(v_done, tiles + ST)
                        pe.wait_ge(t_done, groups + (g + 1))
                        for t in range(ST):
                            for hh in range(2):
                                h = 2 * g + hh
                                mm = pe.matmul(bank[hh * HEAD:(hh + 1) * HEAD, g % 2, t * P:(t + 1) * P],
                                               v[:, t, h * HEAD:(h + 1) * HEAD], wsT[:, h], start=True, stop=True)
                        mm.then_inc(s_ps, 1)
                pe.wait_ge(y_sum, ys + 9)
                for part, total in enumerate((sum_a, sum_b)):
                    for t in range(ST):
                        mm = pe.matmul(bank[:, 2, part * ST + t:part * ST + t + 1], total[:, t * P:(t + 1) * P],
                                       keep.ones[:, 0:1], start=True, stop=True)
                mm.then_inc(ssy_ps, 1)
                n = snap(pe, i + 1)
                pe.wait_ge(y_hi, ys + 8)
                pe.wait_ge(y_lo, ys + 8)
                for t in range(ST):
                    if not last:
                        if t == 0:
                            pe.wait_ge(ssy_done, n)
                        turn_x(tiles_next, t)
                    cols = slice(t * P, (t + 1) * P)
                    for part in range(2):
                        k = 2 * t + part
                        pair = PAIR[k % 3]
                        pe.wait_ge(o_done, ys + (k + 1))
                        for c in range(4 * part, 4 * part + 4):
                            for n_half in range(2):
                                w = slice(n_half * 512, (n_half + 1) * 512)
                                mm = product(pe, bank[:, pair + n_half], yT_hi[:, c, cols], yT_lo[:, c, cols],
                                             wo_hi[:, c, w], wo_lo[:, c, w], c % 4 == 0, c % 4 == 3)
                        mm.then_inc(o_ps, 1)

            pe.sem_inc(unit_used, 2)
            pe.sem_inc(xT_ps, 2)
            pe.sem_inc(s_ps, 1)
            pe.sem_inc(ssy_ps, 1)
            pe.sem_inc(o_ps, 1)
            pe.wait_ge(ws_in, 16)
            for h in range(HEADS):
                mm = pe.transpose(bank[:, h // 4, (h % 4) * P:(h % 4 + 1) * P], v[:, h // 4, (h % 4) * P:(h % 4 + 1) * P],
                                  keep.ident[:])
            mm.then_inc(ws_turned, 1)
            for t in range(ST):
                turn_x(0, t)
            pe.wait_ge(ws_copied, 1)
            pe.wait_ge(ws_masked, 1)
            with pe.Fori(0, SUPERS - 1) as i:
                step(i, False)
            step(SUPERS - 1, True)


def folding(nc, keep, ins, fold):
    MT = MEM // P
    DC = XDIM // P
    with ExitStack() as ctx:
        sb = lambda n, s, d=F32: ctx.enter_context(nc.sbuf_tensor(n, s, d))
        sem = semaphores(nc, ctx)
        bank = ctx.enter_context(nc.psum_tensor("fold_ps", [P, 8, 512], F32))
        raw = sb("fold_raw", [P, 2, 2048])
        w_hi = sb("fold_w_hi", [P, 2, 2048], F32R)
        w_lo = sb("fold_w_lo", [P, 2, 2048], F32R)
        memT_hi = sb("memT_hi", [P, KD, MEM], F32R)
        memT_lo = sb("memT_lo", [P, KD, MEM], F32R)
        kT_hi, kT_lo = sb("kT_hi", [P, DC, MEM], F32R), sb("kT_lo", [P, DC, MEM], F32R)
        vT_hi, vT_lo = sb("vT_hi", [P, DC, MEM], F32R), sb("vT_lo", [P, DC, MEM], F32R)
        gain = sb("gain_mem", [P, D])
        ssm, rm, half = sb("ssm", [P, MT]), sb("rm", [P, MT]), sb("fold_half", [P, MT])

        mem_in, mem_sq, mem_ms, mem_r, mem_scaled = [sem(n) for n in (
            "mem_in", "mem_sq", "mem_ms", "mem_r", "mem_scaled")]
        mem_ps, mem_hi, mem_lo, half_set = [sem(n) for n in ("mem_ps", "mem_hi", "mem_lo", "half_set")]
        k_in, v_in, q_in, o_in = [sem(n) for n in ("k_in", "v_in", "q_in", "o_in")]
        k_hi, k_lo, v_hi, v_lo, o_hi, o_lo = [sem(n) for n in ("k_hi", "k_lo", "v_hi", "v_lo", "wo_hi_d", "wo_lo_d")]
        k_ps, q_ps, v_ps, a_ps, b_ps = [sem(n) for n in ("k_ps", "q_ps", "v_ps_f", "a_ps", "b_ps")]
        qT_h, qT_l, kT_h, kT_l, vT_h, vT_l = [sem(n) for n in ("qT_h", "qT_l", "kT_h", "kT_l", "vT_h", "vT_l")]
        a_hi, a_lo, b_hi, b_lo = [sem(n) for n in ("a_hi", "a_lo", "b_hi", "b_lo")]
        block = ctx.enter_context(nc.Block())
        col = lambda i: keep.cols[:, COLS["g_xattn"] + i:COLS["g_xattn"] + i + 1]
        mem_raw = raw[:, 0].rearrange("p (t n) -> p t n", t=MT)

        @block.sync
        def _(sp):
            sp.dma_start(mem_raw, ins["mem"][0].rearrange("(t p) n -> p t n", p=P)).then_inc(mem_in, 16)
            sp.dma_start(gain[:], ins["g_mem"].broadcast_to((P, D))).then_inc(mem_in, 16)
            sp.wait_ge(mem_ps, 1)
            by_k = lambda w, h: ins[w][0, :, bass.ds(h * XDIM, XDIM)].rearrange("(k p) n -> p k n", p=P)
            with sp.Fori(0, XHEADS) as h:
                n = sp.snap(h + 1)
                sp.wait_ge(q_ps, n)
                sp.dma_start(raw[:, 0].rearrange("p (k n) -> p k n", k=KD), by_k("w_k", h)).then_inc(k_in, 16)
                sp.wait_ge(o_lo, n)
                sp.dma_start(raw[:, 1].rearrange("p (k n) -> p k n", k=KD), by_k("w_v", h)).then_inc(v_in, 16)
                sp.wait_ge(k_lo, n)
                sp.dma_start(raw[:, 0].rearrange("p (k n) -> p k n", k=KD), by_k("w_q", h)).then_inc(q_in, 16)
                sp.wait_ge(v_lo, n)
                sp.dma_start(raw[:, 1].rearrange("p (c n) -> p c n", c=DC),
                             ins["w_o"][0, bass.ds(h * XDIM, XDIM), :].rearrange("(c p) n -> p c n", p=P)).then_inc(o_in, 16)

        @block.gpsimd
        def _(pool):
            pool.memset(half[:], -0.5).then_inc(half_set, 1)
            pool.wait_ge(mem_sq, MT)
            pool.tensor_scalar(rm[:], ssm[:], 1.0 / D, EPS, ALU.mult, ALU.add).then_inc(mem_ms, 1)
            pool.wait_ge(mem_ms, 1)
            pool.wait_ge(half_set, 1)
            pool.tensor_tensor(rm[:], rm[:], half[:], ALU.pow).then_inc(mem_r, 1)

        @block.scalar
        def _(act):
            act.wait_ge(mem_in, 32)
            for t in range(MT):
                act.activation(raw[:, 1, t * D:(t + 1) * D], mem_raw[:, t], ACT.Square,
                               accum_out=ssm[:, t:t + 1]).then_inc(mem_sq, 1)
            act.wait_ge(mem_ps, 1)
            act.activation(memT_hi[:], bank[:, 0:4].rearrange("p b (k n) -> p (b k) n", n=MEM), ACT.Copy).then_inc(mem_hi, 1)
            with act.Fori(0, XHEADS) as h:
                n = act.snap(h + 1)
                n1 = act.snap(h + 2)
                n16 = act.snap(n * 16)
                act.wait_ge(k_in, n16)
                act.wait_ge(a_ps, n)
                act.activation(w_hi[:, 0], raw[:, 0], ACT.Copy).then_inc(k_hi, 1)
                act.wait_ge(v_in, n16)
                act.wait_ge(b_ps, n)
                act.activation(w_hi[:, 1], raw[:, 1], ACT.Copy).then_inc(v_hi, 1)
                act.wait_ge(k_ps, n)
                act.activation(kT_hi[:], bank[:, 4].rearrange("p (c n) -> p c n", n=MEM), ACT.Copy).then_inc(kT_h, 1)
                act.wait_ge(q_ps, n1)
                act.activation(w_hi[:, 0], bank[:, 0:4].rearrange("p b n -> p (b n)"), ACT.Copy).then_inc(qT_h, 1)
                act.wait_ge(v_ps, n)
                act.activation(vT_hi[:], bank[:, 5].rearrange("p (c n) -> p c n", n=MEM), ACT.Copy).then_inc(vT_h, 1)
                act.wait_ge(o_in, n16)
                act.activation(w_hi[:, 1], raw[:, 1], ACT.Copy).then_inc(o_hi, 1)
                act.wait_ge(a_ps, n1)
                for i in range(KD):
                    mm = act.activation(fold.a_hi[:, i, bass.ds(h * MEM, MEM)], bank[:, 4 + i // 2, (i % 2) * MEM:(i % 2 + 1) * MEM],
                                        ACT.Copy, scale=col(i))
                mm.then_inc(a_hi, 1)
                act.wait_ge(b_ps, n1)
                act.activation(fold.b_hi[:, bass.ds(h * MT, MT), :].rearrange("p m n -> p (m n)"),
                               bank[:, 0:4].rearrange("p b n -> p (b n)"), ACT.Copy).then_inc(b_hi, 1)

        @block.vector
        def _(dve):
            dve.sem_inc(o_lo, 1)
            dve.sem_inc(a_lo, 1)
            dve.sem_inc(b_lo, 1)
            dve.wait_ge(mem_r, 1)
            dve.wait_ge(mem_in, 32)
            for t in range(MT):
                dve.scalar_tensor_tensor(mem_raw[:, t], mem_raw[:, t], rm[:, t:t + 1], gain[:],
                                         ALU.mult, ALU.mult).then_inc(mem_scaled, 1)
            dve.wait_ge(mem_hi, 1)
            dve.tensor_tensor(memT_lo[:], bank[:, 0:4].rearrange("p b (k n) -> p (b k) n", n=MEM), f32(memT_hi[:]),
                              ALU.subtract).then_inc(mem_lo, 1)
            with dve.Fori(0, XHEADS) as h:
                n = dve.snap(h + 1)

                def low(out, of, high, after, done):
                    dve.wait_ge(after, n)
                    return dve.tensor_tensor(out, of, f32(high), ALU.subtract).then_inc(done, 1)

                low(w_lo[:, 0], raw[:, 0], w_hi[:, 0], k_hi, k_lo)
                low(w_lo[:, 1], raw[:, 1], w_hi[:, 1], v_hi, v_lo)
                low(kT_lo[:], bank[:, 4].rearrange("p (c n) -> p c n", n=MEM), kT_hi[:], kT_h, kT_l)
                low(w_lo[:, 0], bank[:, 0:4].rearrange("p b n -> p (b n)"), w_hi[:, 0], qT_h, qT_l)
                low(vT_lo[:], bank[:, 5].rearrange("p (c n) -> p c n", n=MEM), vT_hi[:], vT_h, vT_l)
                low(w_lo[:, 1], raw[:, 1], w_hi[:, 1], o_hi, o_lo)
                dve.wait_ge(a_hi, n)
                for i in range(KD):
                    here = bass.ds(h * MEM, MEM)
                    mm = dve.scalar_tensor_tensor(fold.a_lo[:, i, here], bank[:, 4 + i // 2, (i % 2) * MEM:(i % 2 + 1) * MEM],
                                                  col(i), f32(fold.a_hi[:, i, here]), ALU.mult, ALU.subtract)
                mm.then_inc(a_lo, 1)
                here = bass.ds(h * MT, MT)
                low(fold.b_lo[:, here, :].rearrange("p m n -> p (m n)"), bank[:, 0:4].rearrange("p b n -> p (b n)"),
                    fold.b_hi[:, here, :].rearrange("p m n -> p (m n)"), b_hi, b_lo)

        @block.tensor
        def _(pe):
            pe.sem_inc(q_ps, 1)
            pe.sem_inc(a_ps, 1)
            pe.sem_inc(b_ps, 1)
            pe.wait_ge(mem_scaled, MT)
            for k in range(KD):
                for t in range(MT):
                    c = k * MEM + t * P
                    mm = pe.transpose(bank[:, c // 512, c % 512:c % 512 + P], mem_raw[:, t, k * P:(k + 1) * P], keep.ident[:])
            mm.then_inc(mem_ps, 1)
            pe.wait_ge(mem_lo, 1)
            wide = lambda tile, b: tile[:, b].rearrange("p (k n) -> p k n", k=KD)
            with pe.Fori(0, XHEADS) as h:
                n = pe.snap(h + 1)
                n16 = pe.snap(n * 16)

                def project(b, out, ready, done):
                    pe.wait_ge(ready, n)
                    for c in range(DC):
                        for k in range(KD):
                            cols = slice(c * P, (c + 1) * P)
                            mm = product(pe, bank[:, out, c * MEM:(c + 1) * MEM], wide(w_hi, b)[:, k, cols],
                                         wide(w_lo, b)[:, k, cols], memT_hi[:, k], memT_lo[:, k], k == 0, k == KD - 1)
                    mm.then_inc(done, 1)

                pe.wait_ge(a_lo, n)
                project(0, 4, k_lo, k_ps)
                pe.wait_ge(q_in, n16)
                pe.wait_ge(b_lo, n)
                for c in range(DC):
                    for k in range(KD):
                        mm = pe.transpose(bank[:, 2 * c + k // 4, (k % 4) * P:(k % 4 + 1) * P],
                                          wide(raw, 0)[:, k, c * P:(c + 1) * P], keep.ident[:])
                mm.then_inc(q_ps, 1)
                project(1, 5, v_lo, v_ps)
                pe.wait_ge(kT_l, n)
                pe.wait_ge(qT_l, n)
                pe.wait_ge(vT_l, n)
                for k in range(KD):
                    for c in range(DC):
                        cols = slice(c * D + k * P, c * D + (k + 1) * P)
                        mm = product(pe, bank[:, 4 + k // 2, (k % 2) * MEM:(k % 2 + 1) * MEM], w_hi[:, 0, cols], w_lo[:, 0, cols],
                                     kT_hi[:, c], kT_lo[:, c], c == 0, c == DC - 1)
                mm.then_inc(a_ps, 1)
                n1 = pe.snap(h + 2)
                pe.wait_ge(o_lo, n1)
                for t in range(MT):
                    for nh in range(2):
                        for c in range(DC):
                            cols = slice(c * D + nh * 512, c * D + (nh + 1) * 512)
                            mm = product(pe, bank[:, 2 * t + nh], vT_hi[:, c, t * P:(t + 1) * P], vT_lo[:, c, t * P:(t + 1) * P],
                                         w_hi[:, 1, cols], w_lo[:, 1, cols], c == 0, c == DC - 1)
                mm.then_inc(b_ps, 1)


def xattn(nc, keep, ins, fold, x1, x2, h3):
    with ExitStack() as ctx:
        sb = lambda n, s, d=F32: ctx.enter_context(nc.sbuf_tensor(n, s, d))
        sem = semaphores(nc, ctx)
        bank = ctx.enter_context(nc.psum_tensor("att_ps", [P, 8, 512], F32))
        turned, scored, mixed, prob_ps = (bank[:, b:b + 2].rearrange("p b n -> p (b n)") for b in (0, 2, 4, 6))
        by_k = lambda ap: ap.rearrange("p (k n) -> p k n", n=P)
        xa, xb = sb("xa", [P, D]), sb("xb", [P, D])
        square = sb("att_square", [P, 2, D], BF16)
        xT_hi, xT_lo = sb("xT_hi", [P, KD, P], F32R), sb("xT_lo", [P, KD, P], F32R)
        pT_hi, pT_lo = sb("pT_hi", [P, KD, P], F32R), sb("pT_lo", [P, KD, P], F32R)
        prob = sb("prob", [P, XHEADS * MEM])
        h3_sb = sb("h3_sb", [P, D])
        h3T = sb("h3T", [P, KD, P])
        wr = sb("w_router", [P, KD, GROUPS + EXPERTS])
        ss1, rs1, ss3, r3, half = [sb(n, [P, 1]) for n in ("ss1", "rs1", "ss3", "r3", "att_half")]
        top, shift, total, inv = [sb(n, [P, XHEADS]) for n in ("top", "shift", "total", "inv")]

        wr_in, wr_ready, half_set = sem("wr_in"), sem("wr_ready"), sem("att_half_set")
        xa_in, xb_in, x2_out, h3_out = [sem(n) for n in ("xa_in", "xb_in", "x2_out", "h3_out")]
        sq1, ms1, ms1b, r1_done, sq3, ms3, r3_done = [sem(n) for n in (
            "sq1", "ms1", "ms1b", "r1_done", "sq3", "ms3", "r3_done")]
        t1_ps, xT_h, xT_l, s_ps, max_done, shift_done, exp_done, inv_done, prob_done = [sem(n) for n in (
            "t1_ps", "xT_h", "xT_l", "att_s_ps", "max_done", "shift_done", "exp_done", "inv_done", "prob_done")]
        p_ps, pT_h, pT_l, o_ps, x2_done, h3_done, t3_ps, h3T_done, l_ps, logit_done = [sem(n) for n in (
            "p_ps", "pT_h", "pT_l", "att_o_ps", "x2_done", "h3_done", "t3_ps", "h3T_done", "l_ps", "logit_done")]
        passed, sp_passed = sem("att_pool_passed"), sem("att_sp_passed")
        block = ctx.enter_context(nc.Block())
        W = GROUPS + EXPERTS

        def steps(engine, step):
            step(0)
            step(1)
            with engine.Fori(2, TILES - 1) as i:
                step(i)
            step(TILES - 1)
            step(TILES)

        def has(i, offset):
            return not isinstance(i, int) or 0 <= i + offset < TILES

        @block.sync
        def _(sp):
            sp.dma_start(wr[:, :, 0:GROUPS], ins["w_grp"][0].rearrange("(k p) n -> p k n", p=P)).then_inc(wr_in, 16)
            sp.dma_start(wr[:, :, GROUPS:], ins["w_rt"][0].rearrange("(k p) n -> p k n", p=P)).then_inc(wr_in, 16)
            sp.dma_start(xa[:], x1[0:P, :]).then_inc(xa_in, 16)

            def step(i):
                if has(i, 1):
                    row, n1, n2 = snap(sp, (i + 1) * P), snap(sp, i + 1), snap(sp, i + 2)
                    wait_apart(sp, sp_passed, (t1_ps, n1))
                    wait_apart(sp, sp_passed, (sq1, n2))
                    sp.dma_start(xa[:], x1[bass.ds(row, P), :]).then_inc(xa_in, 16)
                if has(i, -1):
                    row = snap(sp, (i - 1) * P)
                    stored = snap(sp, i * 16)
                    sp.dma_start(xb[:], x1[bass.ds(row, P), :]).then_inc(xb_in, 16)
                    sp.wait_ge(x2_done, snap(sp, i * 1))
                    sp.dma_start(x2[bass.ds(row, P), :], xb[:]).then_inc(x2_out, 16)
                    sp.wait_ge(h3_done, snap(sp, i + 1))
                    sp.dma_start(h3[bass.ds(row, P), :], h3_sb[:]).then_inc(h3_out, 16)
                    wait_apart(sp, sp_passed, (x2_out, stored))

            steps(sp, step)
            sp.wait_ge(h3_out, 16 * TILES)

        @block.gpsimd
        def _(pool):
            pool.memset(half[:], -0.5).then_inc(half_set, 1)
            pool.wait_ge(half_set, 1)

            def root1(j):
                n1, n2 = snap(pool, j + 1), snap(pool, j + 2)
                wait_apart(pool, passed, (sq1, n2), (exp_done, n1))
                pool.tensor_scalar(rs1[:], ss1[:], 1.0 / D, EPS, ALU.mult, ALU.add).then_inc(ms1, 1)
                pool.wait_ge(ms1, n2)
                pool.tensor_tensor(rs1[:], rs1[:], half[:], ALU.pow).then_inc(ms1b, 1)
                wait_apart(pool, passed, (ms1b, n1))
                pool.tensor_scalar(rs1[:], rs1[:], float(XDIM) ** -0.5, None, ALU.mult).then_inc(r1_done, 1)

            def root3(j):
                n1, n2 = snap(pool, j + 1), snap(pool, j + 2)
                wait_apart(pool, passed, (sq3, n2), (h3_done, n1))
                pool.tensor_scalar(r3[:], ss3[:], 1.0 / D, EPS, ALU.mult, ALU.add).then_inc(ms3, 1)
                pool.wait_ge(ms3, n2)
                pool.tensor_tensor(r3[:], r3[:], half[:], ALU.pow).then_inc(r3_done, 1)

            def step(i):
                if has(i, 1):
                    root1(i + 1)
                if has(i, -1):
                    root3(i - 1)

            pool.sem_inc(ms1, 1)
            pool.sem_inc(ms3, 1)
            root1(0)
            steps(pool, step)

        @block.scalar
        def _(act):
            def square1(j):
                act.wait_ge(xa_in, snap(act, j * 16 + 16))
                act.wait_ge(ms1, snap(act, j + 1))
                act.wait_ge(sq1, snap(act, j + 1))
                act.activation(square[:, 0], xa[:], ACT.Square, accum_out=ss1[:]).then_inc(sq1, 1)

            def exps(j):
                n1 = snap(act, j + 1)
                act.wait_ge(shift_done, n1)
                act.wait_ge(p_ps, n1)
                act.wait_ge(inv_done, n1)
                for h in range(XHEADS):
                    cols = slice(h * MEM, (h + 1) * MEM)
                    e = act.activation(prob[:, cols], scored[:, cols], ACT.Exp, bias=shift[:, h:h + 1], scale=rs1[:],
                                       accum_out=total[:, h:h + 1])
                e.then_inc(exp_done, 1)

            def turn1(j):
                act.wait_ge(t1_ps, snap(act, j + 1))
                act.activation(xT_hi[:], by_k(turned), ACT.Copy).then_inc(xT_h, 1)

            def step(i):
                if has(i, 1):
                    square1(i + 1)
                if has(i, 0):
                    exps(i)
                if has(i, 1):
                    turn1(i + 1)
                if has(i, -2):
                    act.wait_ge(t3_ps, snap(act, i - 1))
                    act.activation(h3T[:], by_k(prob_ps), ACT.Copy).then_inc(h3T_done, 1)
                if has(i, -1):
                    act.wait_ge(x2_done, snap(act, i * 1))
                    act.wait_ge(ms3, snap(act, i * 1))
                    act.wait_ge(sq3, snap(act, i * 1))
                    act.activation(square[:, 1], xb[:], ACT.Square, accum_out=ss3[:]).then_inc(sq3, 1)
                if has(i, 0):
                    act.wait_ge(p_ps, snap(act, i + 2))
                    act.activation(pT_hi[:], by_k(prob_ps), ACT.Copy).then_inc(pT_h, 1)

            act.sem_inc(sq1, 1)
            act.sem_inc(sq3, 1)
            act.sem_inc(exp_done, 1)
            act.sem_inc(h3T_done, 2)
            square1(0)
            turn1(0)
            steps(act, step)
            act.wait_ge(t3_ps, TILES)
            act.activation(h3T[:], by_k(prob_ps), ACT.Copy).then_inc(h3T_done, 1)

        @block.vector
        def _(dve):
            def turn1(j):
                dve.wait_ge(xT_h, snap(dve, j + 1))
                dve.tensor_tensor(xT_lo[:], by_k(turned), f32(xT_hi[:]), ALU.subtract).then_inc(xT_l, 1)

            def keep_logits(j):
                dve.wait_ge(l_ps, snap(dve, j + 1))
                dve.tensor_copy(keep.logits[:, bass.ds(j, 1), :], scored[:, 0:W].unsqueeze(1)).then_inc(logit_done, 1)

            def step(i):
                n1, n2 = snap(dve, i + 1), snap(dve, i + 2)
                if has(i, 0):
                    dve.wait_ge(s_ps, n1)
                    dve.tensor_reduce(top[:], scored.rearrange("p (h m) -> p h m", m=MEM), AX.X, ALU.max).then_inc(max_done, 1)
                    dve.wait_ge(max_done, n1)
                    dve.wait_ge(r1_done, n1)
                    dve.tensor_scalar(shift[:], top[:], rs1[:], -1.0, ALU.mult, ALU.mult).then_inc(shift_done, 1)
                if has(i, 1):
                    turn1(i + 1)
                if has(i, 0):
                    dve.wait_ge(exp_done, n2)
                    dve.reciprocal(inv[:], total[:]).then_inc(inv_done, 1)
                    dve.wait_ge(inv_done, n2)
                    heads = prob[:].rearrange("p (h m) -> p h m", m=MEM)
                    dve.tensor_tensor(heads, heads, inv[:].unsqueeze(2).broadcast_to((P, XHEADS, MEM)),
                                      ALU.mult).then_inc(prob_done, 1)
                if has(i, -1):
                    dve.wait_ge(o_ps, snap(dve, i * 1))
                    dve.wait_ge(xb_in, snap(dve, i * 16))
                    dve.tensor_tensor(xb[:], mixed, xb[:], ALU.add).then_inc(x2_done, 1)
                if has(i, -2):
                    keep_logits(i - 2)
                if has(i, 0):
                    dve.wait_ge(pT_h, n1)
                    dve.tensor_tensor(pT_lo[:], by_k(prob_ps), f32(pT_hi[:]), ALU.subtract).then_inc(pT_l, 1)
                if has(i, -1):
                    dve.wait_ge(r3_done, snap(dve, i * 1))
                    dve.wait_ge(x2_done, snap(dve, i * 1))
                    if has(i, -2):
                        dve.wait_ge(h3_out, snap(dve, i * 16 - 16))
                        dve.wait_ge(t3_ps, snap(dve, i - 1))
                    dve.tensor_scalar(h3_sb[:], xb[:], r3[:], None, ALU.mult).then_inc(h3_done, 1)

            dve.sem_inc(xT_l, 1)
            dve.sem_inc(inv_done, 1)
            dve.sem_inc(pT_l, 1)
            dve.sem_inc(h3_done, 1)
            dve.sem_inc(logit_done, 3)
            dve.wait_ge(wr_in, 32)
            gain = keep.cols[:, COLS["g_ffn"]:COLS["g_ffn"] + KD]
            dve.tensor_tensor(wr[:], wr[:], gain.unsqueeze(2).broadcast_to((P, KD, W)), ALU.mult).then_inc(wr_ready, 1)
            turn1(0)
            steps(dve, step)
            keep_logits(TILES - 1)

        @block.tensor
        def _(pe):
            def turn(out, of, done):
                for k in range(KD):
                    mm = pe.transpose(out[:, k * P:(k + 1) * P], of[:, k * P:(k + 1) * P], keep.ident[:])
                mm.then_inc(done, 1)

            def turn1(j):
                pe.wait_ge(xa_in, snap(pe, j * 16 + 16))
                pe.wait_ge(xT_l, snap(pe, j + 1))
                turn(turned, xa, t1_ps)

            def times(out, a_hi, a_lo, b_hi, b_lo, done):
                for k in range(KD):
                    for nh in range(2):
                        cols = slice(nh * 512, (nh + 1) * 512)
                        mm = product(pe, out[:, cols], a_hi[:, k], a_lo[:, k], b_hi[:, k, cols], b_lo[:, k, cols],
                                     k == 0, k == KD - 1)
                mm.then_inc(done, 1)

            def turn3(j):
                pe.wait_ge(h3_done, snap(pe, j + 2))
                pe.wait_ge(pT_l, snap(pe, j + 3) if has(j, 1) else TILES + 1)
                turn(prob_ps, h3_sb, t3_ps)

            def route(j):
                pe.wait_ge(h3T_done, snap(pe, j + 3))
                pe.wait_ge(exp_done, snap(pe, j + 4) if has(j, 2) else TILES + 1)
                for k in range(KD):
                    mm = pe.matmul(scored[:, 0:W], h3T[:, k], wr[:, k], start=(k == 0), stop=(k == KD - 1))
                mm.then_inc(l_ps, 1)

            def step(i):
                if has(i, 0):
                    pe.wait_ge(xT_l, snap(pe, i + 2))
                    pe.wait_ge(exp_done, snap(pe, i + 1))
                    pe.wait_ge(logit_done, snap(pe, i + 1))
                    times(scored, xT_hi, xT_lo, fold.a_hi, fold.a_lo, s_ps)
                if has(i, 1):
                    turn1(i + 1)
                if has(i, -2):
                    turn3(i - 2)
                if has(i, -1):
                    pe.wait_ge(pT_l, snap(pe, i + 1))
                    if has(i, -2):
                        pe.wait_ge(x2_done, snap(pe, i - 1))
                    times(mixed, pT_hi, pT_lo, fold.b_hi, fold.b_lo, o_ps)
                if has(i, -2):
                    route(i - 2)
                if has(i, 0):
                    pe.wait_ge(prob_done, snap(pe, i + 1))
                    pe.wait_ge(pT_l, snap(pe, i + 1))
                    pe.wait_ge(h3T_done, snap(pe, i + 1))
                    turn(prob_ps, prob, p_ps)

            pe.sem_inc(p_ps, 1)
            pe.wait_ge(wr_ready, 1)
            turn1(0)
            steps(pe, step)
            pe.wait_ge(logit_done, TILES + 2)
            turn3(TILES - 1)
            route(TILES - 1)


class Routed:

    EXPERT, ACTIVE, SECOND, ORDER, ROW = range(5)

    def __init__(self, nc, ctx):
        sb = lambda n, s, d=F32: ctx.enter_context(nc.sbuf_tensor(n, s, d))
        self.tokens = sb("block_tokens", [P, LISTED], U32)
        self.rows = sb("token_rows", [P, 2, TILES], U32)
        self.gates = sb("gates", [P, 2, TILES])
        self.plan = sb("plan", [1, 5, SLOTS + 1], I32)
        self.totals = sb("totals", [1, 2], I32)


def routing(nc, keep, ins, routed):
    W = GROUPS + EXPERTS
    S1 = SLOTS + 1
    PAIRS = 2 * TILES
    FAR = 3.0e38
    with ExitStack() as ctx:
        sb = lambda n, s, d=F32: ctx.enter_context(nc.sbuf_tensor(n, s, d))
        sem = semaphores(nc, ctx)
        bank = ctx.enter_context(nc.psum_tensor("route_ps", [P, 8, 512], F32))
        bias = sb("router_bias", [P, W])
        logits = keep.logits
        grp = sb("grp", [P, TILES, 8])
        grp_top, grp_at = sb("grp_top", [P, TILES, 8]), sb("grp_at", [P, TILES, 8], U32)
        grp_exp, grp_sum = sb("grp_exp", [P, TILES, GROUPS]), sb("grp_sum", [P, TILES])
        grp_id = sb("grp_id", [P, TILES])
        mask, far = sb("mask", [P, TILES, GROUPS]), sb("far", [P, TILES, GROUPS])
        inside = sb("inside", [P, TILES, EXPERTS])
        exp_top, exp_at = sb("exp_top", [P, TILES, 8]), sb("exp_at", [P, TILES, 8], U32)
        ids = sb("ids", [P, 2, TILES])
        gap, ratio, den = sb("gap", [P, TILES]), sb("ratio", [P, TILES]), sb("den", [P, TILES])
        chosen = sb("chosen", [P, 2, TILES, EXPERTS])
        both = sb("both", [P, TILES, EXPERTS], BF16)
        so_far = sb("so_far", [P, 2, TILES + 1, EXPERTS], BF16)
        last = (TILES - 1).bit_length() % 2
        picked = sb("picked", [P, 2, TILES, EXPERTS])
        before, count = sb("before", [P, TILES, EXPERTS]), sb("count", [P, EXPERTS])
        count_i, slots_i = sb("count_i", [P, EXPERTS], I32), sb("slots_i", [P, EXPERTS], I32)
        slots_of = sb("slots_of", [P, EXPERTS])
        ends = sb("ends", [P, 2, EXPERTS])
        starts = sb("starts", [P, EXPERTS])
        sums = sb("count_sums", [P, 2, EXPERTS])
        row_starts, offset = sb("row_starts", [P, EXPERTS]), sb("offset", [1, EXPERTS])
        rank, base = sb("rank", [P, 2, TILES]), sb("base", [P, 2, TILES])
        rank_i, over_i = sb("rank_i", [P, 2, TILES], I32), sb("over_i", [P, 2, TILES], I32)
        over, dest = sb("over", [P, 2, TILES]), sb("dest", [P, 2, TILES])
        dest_i, part_i = sb("dest_i", [P, 2, TILES], I32), sb("part_i", [P, 2, 2, TILES], I32)
        part = sb("part", [P, 2, 2, TILES])
        place = sb("place", [P, PAIRS, P], BF16)
        blocks = sb("blocks", [P, 3, PAIRS, LISTED], BF16)
        iota_e = sb("iota_e", [P, EXPERTS])
        iota_p = sb("iota_p", [P, 1])
        iota_r = sb("iota_r", [P, P])
        iota_t = sb("iota_t", [P, PAIRS])
        earlier, ones_b = sb("earlier", [P, P], BF16), sb("ones_b", [P, P], BF16)
        list_f = sb("list_f", [P, LISTED])
        in_block = sb("in_block", [1, LISTED])
        ended = sb("ended", [1, S1, EXPERTS])
        expert_f, active_f, second_f, row_f = (sb(n, [1, S1]) for n in ("expert_f", "active_f", "second_f", "row_f"))
        order = sb("order", [1, 2, S1])
        totals_f = sb("totals_f", [1, 2])

        bias_in, made, chain = sem("bias_in"), sem("pool_made"), sem("route_chain")
        grp_ready, grp_exped, gap_ready, ratio_ready = [sem(n) for n in ("grp_ready", "grp_exped", "gap_ready", "ratio_ready")]
        both_ready, counted, blocks_ready, listed = [sem(n) for n in ("both_ready", "counted", "blocks_ready", "listed")]
        block = ctx.enter_context(nc.Block())

        @block.sync
        def _(sp):
            sp.dma_start(bias[:, 0:GROUPS], ins["b_grp"].broadcast_to((P, GROUPS))).then_inc(bias_in, 16)
            sp.dma_start(bias[:, GROUPS:], ins["b_rt"].broadcast_to((P, EXPERTS))).then_inc(bias_in, 16)

        @block.gpsimd
        def _(pool):
            pool.iota(iota_e[:], pattern=[[1, EXPERTS]], base=0, channel_multiplier=0,
                      allow_small_or_imprecise_dtypes=True).then_inc(made, 1)
            pool.iota(iota_p[:], pattern=[[0, 1]], base=0, channel_multiplier=1,
                      allow_small_or_imprecise_dtypes=True).then_inc(made, 1)
            pool.iota(iota_r[:], pattern=[[1, P]], base=0, channel_multiplier=0,
                      allow_small_or_imprecise_dtypes=True).then_inc(made, 1)
            pool.iota(iota_t[:], pattern=[[0, 2], [1, TILES]], base=0, channel_multiplier=0,
                      allow_small_or_imprecise_dtypes=True).then_inc(made, 1)
            pool.memset(ones_b[:], 1.0).then_inc(made, 1)
            pool.wait_ge(made, 5)
            pool.affine_select(out=earlier[:], in_=ones_b[:], compare_op=ALU.is_gt, fill=0.0, base=0,
                               pattern=[[1, P]], channel_multiplier=-1).then_inc(made, 1)

        @block.scalar
        def _(act):
            act.wait_ge(grp_ready, 1)
            act.activation(grp_exp[:], grp_exp[:], ACT.Exp).then_inc(grp_exped, 1)
            act.wait_ge(gap_ready, 1)
            act.activation(ratio[:], gap[:], ACT.Exp).then_inc(ratio_ready, 1)

        @block.tensor
        def _(pe):
            pe.wait_ge(made, 6)
            pe.wait_ge(both_ready, 1)
            flat = lambda tile: tile.rearrange("p t e -> p (t e)")
            pe.matmul(bank[:, 0], earlier[:], flat(both[:]), start=True, stop=False)
            pe.matmul(bank[:, 0], ones_b[:], flat(so_far[:, last, 0:TILES]), start=False, stop=True)
            pe.matmul(bank[:, 1, 0:EXPERTS], ones_b[:], so_far[:, last, TILES], start=True, stop=True).then_inc(counted, 1)
            pe.wait_ge(blocks_ready, 1)
            for k in range(2):
                for j in range(PAIRS):
                    pe.matmul(bank[:, 2 + k, 0:LISTED], place[:, j], blocks[:, 1 + k, j], start=(j == 0), stop=(j == PAIRS - 1))
            for j in range(PAIRS):
                mm = pe.matmul(bank[:, 4, 0:LISTED], ones_b[:], blocks[:, 0, j], start=(j == 0), stop=(j == PAIRS - 1))
            mm.then_inc(listed, 1)

        @block.vector
        def _(dve):
            steps = [0]

            def link(instruction):
                steps[0] += 1
                instruction.then_inc(chain, 1)
                dve.wait_ge(chain, steps[0])

            def copy(out, of):
                link(dve.tensor_copy(out, of))

            def running_sum(both_buffers, of, n):
                copy(both_buffers[:, 0], of)
                at, step = 0, 1
                while step < n:
                    link(dve.tensor_copy(both_buffers[:, 1 - at, 0:step], both_buffers[:, at, 0:step]))
                    link(dve.tensor_tensor(both_buffers[:, 1 - at, step:], both_buffers[:, at, step:],
                                           both_buffers[:, at, 0:n - step], ALU.add))
                    at, step = 1 - at, 2 * step
                return both_buffers[:, at]

            def bcast(ap, axis, shape):
                return ap.unsqueeze(axis).broadcast_to(shape)

            dve.wait_ge(bias_in, 32)
            link(dve.tensor_tensor(logits[:], logits[:], bcast(bias[:], 1, (P, TILES, W)), ALU.add))
            link(dve.memset(grp[:], -FAR))
            copy(grp[:, :, 0:GROUPS], logits[:, :, 0:GROUPS])
            for t in range(TILES):
                mm = dve.max(grp_top[:, t], grp[:, t])
            link(mm)
            for t in range(TILES):
                mm = dve.max_index(grp_at[:, t], grp_top[:, t], grp[:, t])
            link(mm)
            dve.tensor_tensor(grp_exp[:], logits[:, :, 0:GROUPS], grp_top[:, :, 0:1].broadcast_to((P, TILES, GROUPS)),
                              ALU.subtract).then_inc(grp_ready, 1)
            copy(grp_id[:], grp_at[:, :, 0])
            dve.wait_ge(made, 6)
            link(dve.tensor_tensor(mask[:], bcast(iota_e[:, 0:GROUPS], 1, (P, TILES, GROUPS)),
                                   bcast(grp_id[:], 2, (P, TILES, GROUPS)), ALU.is_equal))
            link(dve.tensor_scalar(far[:], mask[:], -1.0, FAR, ALU.add, ALU.mult))
            in_groups = inside[:].rearrange("p t (g e) -> p (t g) e", e=PER_GROUP)
            spread = lambda m: bcast(m[:].rearrange("p t g -> p (t g)"), 2, (P, TILES * GROUPS, PER_GROUP))
            copy(inside[:], logits[:, :, GROUPS:])
            link(dve.tensor_tensor(in_groups, in_groups, spread(mask), ALU.mult))
            link(dve.tensor_tensor(in_groups, in_groups, spread(far), ALU.add))
            for t in range(TILES):
                mm = dve.max(exp_top[:, t], inside[:, t])
            link(mm)
            for t in range(TILES):
                mm = dve.max_index(exp_at[:, t], exp_top[:, t], inside[:, t])
            link(mm)
            dve.tensor_tensor(gap[:], exp_top[:, :, 1], exp_top[:, :, 0], ALU.subtract).then_inc(gap_ready, 1)
            for c in range(2):
                copy(ids[:, c], exp_at[:, :, c])
            for c in range(2):
                link(dve.tensor_tensor(chosen[:, c], bcast(iota_e[:], 1, (P, TILES, EXPERTS)),
                                       bcast(ids[:, c], 2, (P, TILES, EXPERTS)), ALU.is_equal))
            link(dve.tensor_tensor(both[:], chosen[:, 0], chosen[:, 1], ALU.add))
            link(dve.memset(so_far[:, :, 0], 0.0))
            copy(so_far[:, 0, 1:], both[:])
            at, step = 0, 1
            while step < TILES:
                link(dve.tensor_copy(so_far[:, 1 - at, 1:step + 1], so_far[:, at, 1:step + 1]))
                added = dve.tensor_tensor(so_far[:, 1 - at, step + 1:], so_far[:, at, step + 1:],
                                          so_far[:, at, 1:TILES + 1 - step], ALU.add)
                at, step = 1 - at, 2 * step
                if step < TILES:
                    link(added)
            added.then_inc(both_ready, 1)
            dve.wait_ge(grp_exped, 1)
            link(dve.tensor_reduce(grp_sum[:], grp_exp[:], AX.X, ALU.add))
            dve.wait_ge(ratio_ready, 1)
            link(dve.tensor_scalar(den[:], ratio[:], 1.0, None, ALU.add))
            link(dve.tensor_tensor(den[:], den[:], grp_sum[:], ALU.mult))
            link(dve.reciprocal(routed.gates[:, 0], den[:]))
            link(dve.tensor_tensor(routed.gates[:, 1], routed.gates[:, 0], ratio[:], ALU.mult))

            dve.wait_ge(counted, 1)
            copy(before[:], bank[:, 0].rearrange("p (t e) -> p t e", e=EXPERTS))
            copy(count[:], bank[:, 1, 0:EXPERTS])
            link(dve.tensor_scalar(count_i[:], count[:], float(SLOT - 1), None, ALU.add))
            link(dve.tensor_scalar(slots_i[:], count_i[:], 8, None, ALU.arith_shift_right))
            copy(slots_of[:], slots_i[:])
            end = running_sum(ends, slots_of[:], EXPERTS)
            link(dve.tensor_tensor(starts[:], end, slots_of[:], ALU.subtract))
            row_end = running_sum(sums, count[:], EXPERTS)
            link(dve.tensor_tensor(row_starts[:], row_end, count[:], ALU.subtract))
            link(dve.scalar_tensor_tensor(offset[:], starts[0:1], -float(SLOT), row_starts[0:1], ALU.mult, ALU.add))
            flat2 = lambda tile: tile[:].rearrange("p c t e -> p (c t) e")
            flat_s = lambda tile: tile[:].rearrange("p c t -> p (c t)")
            for c in range(2):
                link(dve.tensor_tensor(picked[:, c], chosen[:, c], before[:], ALU.mult))
            link(dve.tensor_reduce(flat_s(rank), flat2(picked), AX.X, ALU.add))
            link(dve.tensor_tensor(flat2(picked), flat2(chosen), bcast(starts[:], 1, (P, PAIRS, EXPERTS)), ALU.mult))
            link(dve.tensor_reduce(flat_s(base), flat2(picked), AX.X, ALU.add))
            link(dve.scalar_tensor_tensor(flat_s(dest), flat_s(base), float(SLOT), flat_s(rank), ALU.mult, ALU.add))
            copy(dest_i[:], dest[:])
            link(dve.tensor_tensor(flat2(picked), flat2(chosen), bcast(row_starts[:], 1, (P, PAIRS, EXPERTS)), ALU.mult))
            link(dve.tensor_reduce(flat_s(base), flat2(picked), AX.X, ALU.add))
            link(dve.tensor_tensor(dest[:], base[:], rank[:], ALU.add))
            copy(routed.rows[:], dest[:])
            link(dve.tensor_scalar(part_i[:, 0], dest_i[:], P - 1, None, ALU.bitwise_and))
            link(dve.tensor_scalar(part_i[:, 1], dest_i[:], 7, None, ALU.arith_shift_right))
            copy(part[:], part_i[:])
            col = lambda k: part[:, k].rearrange("p c t -> p (c t)")
            link(dve.tensor_tensor(place[:], bcast(iota_r[:], 1, (P, PAIRS, P)), bcast(col(0), 2, (P, PAIRS, P)), ALU.is_equal))
            link(dve.tensor_tensor(blocks[:, 0], bcast(iota_r[:, 0:LISTED], 1, (P, PAIRS, LISTED)),
                                   bcast(col(1), 2, (P, PAIRS, LISTED)), ALU.is_equal))
            link(dve.tensor_scalar(blocks[:, 1], blocks[:, 0], iota_p[:], None, ALU.mult))
            dve.tensor_tensor(blocks[:, 2], blocks[:, 0], bcast(iota_t[:], 2, (P, PAIRS, LISTED)), ALU.mult).then_inc(blocks_ready, 1)

            slot_row = iota_r[0:1, 0:S1]
            link(dve.tensor_tensor(ended[:], bcast(end[0:1], 1, (1, S1, EXPERTS)),
                                   bcast(slot_row, 2, (1, S1, EXPERTS)), ALU.is_le))
            link(dve.tensor_reduce(expert_f[:], ended[:], AX.X, ALU.add))
            link(dve.tensor_scalar(expert_f[:], expert_f[:], float(EXPERTS - 1), None, ALU.min))
            copy(routed.plan[:, Routed.EXPERT], expert_f[:])
            link(dve.tensor_tensor(ended[:], bcast(expert_f[:], 2, (1, S1, EXPERTS)),
                                   bcast(iota_e[0:1], 1, (1, S1, EXPERTS)), ALU.is_equal))
            link(dve.tensor_tensor(ended[:], ended[:], bcast(offset[:], 1, (1, S1, EXPERTS)), ALU.mult))
            link(dve.tensor_reduce(row_f[:], ended[:], AX.X, ALU.add))
            link(dve.scalar_tensor_tensor(row_f[:], slot_row, float(SLOT), row_f[:], ALU.mult, ALU.add))
            copy(routed.plan[:, Routed.ROW], row_f[:])
            dve.wait_ge(listed, 1)
            copy(list_f[:], bank[:, 3, 0:LISTED])
            link(dve.scalar_tensor_tensor(list_f[:], list_f[:], float(P), bank[:, 2, 0:LISTED], ALU.mult, ALU.add))
            copy(routed.tokens[:], list_f[:])
            copy(in_block[:], bank[0:1, 4, 0:LISTED])
            halves = in_block[:].rearrange("p (s b) -> p b s", b=2)
            link(dve.tensor_scalar(active_f[:], halves[:, 0], 0.0, None, ALU.is_gt))
            link(dve.tensor_scalar(second_f[:], halves[:, 1], 0.0, None, ALU.is_gt))
            copy(routed.plan[:, Routed.ACTIVE], active_f[:])
            copy(routed.plan[:, Routed.SECOND], second_f[:])
            until = running_sum(order, second_f[:], S1)
            link(dve.tensor_tensor(second_f[:], until, second_f[:], ALU.subtract))
            link(dve.tensor_scalar(second_f[:], second_f[:], 1.0, None, ALU.add))
            copy(routed.plan[:, Routed.ORDER], second_f[:])
            copy(totals_f[:, 0:1], end[0:1, EXPERTS - 1:EXPERTS])
            copy(totals_f[:, 1:2], until[:, S1 - 1:S1])
            copy(routed.totals[:], totals_f[:])


def moe(nc, keep, ins, routed, h3, y):
    GU, DN = KD, DE // P
    UNITS = GU + DN
    RAW = 6
    EARLY = GU - 1
    ON_POOL = (GU + 1, GU + 3)
    LEAST = SEQ * 2 // SLOT
    w_gate, w_up, w_down = ins["w_gate"], ins["w_up"], ins["w_down"]
    with ExitStack() as ctx:
        sb = lambda n, s, d=F32: ctx.enter_context(nc.sbuf_tensor(n, s, d))
        sem = semaphores(nc, ctx)
        bank = ctx.enter_context(nc.psum_tensor("moe_ps", [P, 8, 512], F32))
        pair = lambda b: bank[:, b:b + 2].rearrange("p b n -> p (b n)")
        by_chunk = lambda ap: ap.rearrange("p (k n) -> p k n", n=P)
        raw = sb("moe_raw", [P, RAW, 1024])
        w_hi = sb("moe_w_hi", [P, UNITS, 1024], F32R)
        w_lo = sb("moe_w_lo", [P, UNITS, 1024], F32R)
        index = [sb(f"token_index_{b}", [P, 1], U32) for b in "AB"]
        tokens = [sb(f"moe_x_{b}", [P, D]) for b in "AB"]
        xT_hi = [sb(f"moe_xT_hi_{b}", [P, KD, P], F32R) for b in "AB"]
        xT_lo = [sb(f"moe_xT_lo_{b}", [P, KD, P], F32R) for b in "AB"]
        silu = [sb(f"silu_{b}", [P, DE]) for b in "AB"]
        hid = [sb(f"hidden_{b}", [P, DE]) for b in "AB"]
        hT_hi = [sb(f"hidT_hi_{b}", [P, DN, P], F32R) for b in "AB"]
        hT_lo = [sb(f"hidT_lo_{b}", [P, DN, P], F32R) for b in "AB"]
        y_sb = [sb(f"y_sb_{b}", [P, D]) for b in "AB"]

        raw_in = [sem(f"moe_raw_in{b}") for b in range(RAW)]
        hi_done, lo_dve, lo_pool = sem("moe_hi_done"), sem("moe_lo_dve"), sem("moe_lo_pool")
        gu_used, down_used = sem("gu_used"), sem("down_used")
        y_set, index_ready, pool_passed = sem("y_set"), sem("index_ready"), sem("moe_pool_passed")
        pe_passed, act_passed, dve_passed = sem("moe_pe_passed"), sem("moe_act_passed"), sem("moe_dve_passed")
        gathered = [sem(f"gathered_{b}") for b in "AB"]
        x_ps = [sem(f"x_ps_{b}") for b in "AB"]
        xT_h, xT_l = sem("moe_xT_h"), sem("moe_xT_l")
        gu_ps, down_ps = sem("gu_ps"), sem("down_ps")
        silu_done = [sem(f"silu_done_{b}") for b in "AB"]
        hid_done = [sem(f"hid_done_{b}") for b in "AB"]
        hid_ps = [sem(f"hid_ps_{b}") for b in "AB"]
        hT_h = [sem(f"hidT_h_{b}") for b in "AB"]
        hT_l = [sem(f"hidT_l_{b}") for b in "AB"]
        y_kept = [sem(f"y_kept_{b}") for b in "AB"]
        y_out = [sem(f"y_out_{b}") for b in "AB"]
        block = ctx.enter_context(nc.Block())
        gain = lambda k: keep.cols[:, COLS["g_ffn"] + k:COLS["g_ffn"] + k + 1]
        halves = lambda ap: ap.rearrange("p (h n) -> p h n", h=2)

        def planned(engine, row, slot, least, most):
            return engine.value_load(routed.plan[0:1, row, bass.ds(slot, 1)], min_val=least, max_val=most)

        def second(engine, slot):
            return planned(engine, Routed.SECOND, slot, 0, 1)

        def order(engine, slot):
            return planned(engine, Routed.ORDER, slot, 1, SLOTS + 1)

        def total(engine, k, least):
            return engine.value_load(routed.totals[0:1, k:k + 1], min_val=least, max_val=SLOTS)

        def steps(engine, step):
            step(0)
            with engine.Fori(1, SLOTS) as i:
                active = planned(engine, Routed.ACTIVE, i, 0, 1)
                with engine.If(active == 1):
                    step(i)

        def staging(u):
            return (GU + u) % RAW

        def arrived(i, u):
            return i * (UNITS // RAW * 32) + ((GU + u) // RAW + 1) * 32

        def lows_of_dve(u):
            return sum(1 for v in range(u + 1) if v not in ON_POOL)

        def split(i, u):
            if u in ON_POOL:
                return lo_pool, i * len(ON_POOL) + (ON_POOL.index(u) + 1)
            return lo_dve, i * (UNITS - len(ON_POOL)) + (GU + lows_of_dve(u))

        @block.sync
        def _(sp):
            def load_gu(expert, k, b):
                for half, w in enumerate((w_gate, w_up)):
                    sp.dma_start(raw[:, b, half * DE:(half + 1) * DE],
                                 w[0, bass.ds(expert, 1), k * P:(k + 1) * P, :].rearrange("e p n -> (e p) n")).then_inc(raw_in[b], 16)

            def step(i):
                following = planned(sp, Routed.EXPERT, i + 1, 0, EXPERTS - 1)
                own = planned(sp, Routed.EXPERT, i, 0, EXPERTS - 1)
                for u in range(UNITS):
                    if u >= RAW:
                        semaphore, count = split(i, u - RAW)
                    elif isinstance(i, int):
                        semaphore, count = lo_dve, GU - RAW + u + 1
                    else:
                        semaphore, count = split(i - 1, u - RAW + UNITS)
                    sp.wait_ge(semaphore, snap(sp, count))
                    if u < GU:
                        load_gu(following, u, staging(u))
                    else:
                        rows = slice((u - GU) * P, (u - GU + 1) * P)
                        for half in range(2):
                            cols = slice(half * 512, (half + 1) * 512)
                            sp.dma_start(raw[:, staging(u), cols],
                                         w_down[0, bass.ds(own, 1), rows, cols].rearrange("e p n -> (e p) n")).then_inc(raw_in[staging(u)], 16)

            first = planned(sp, Routed.EXPERT, 0, 0, EXPERTS - 1)
            for k in range(GU):
                if k >= RAW:
                    sp.wait_ge(lo_dve, k - RAW + 1)
                load_gu(first, k, k % RAW)
            steps(sp, step)

        @block.gpsimd
        def _(pool):
            def gather(slot, count):
                for b in range(2):
                    pool.tensor_copy(index[b][:], routed.tokens[:, bass.ds(slot * 2 + b, 1)]).then_inc(index_ready, 1)
                wait_apart(pool, pool_passed, (index_ready, count))
                for b in range(2):
                    pool.indirect_dma_start(out=tokens[b][:], out_offset=None, in_=h3[:, :],
                                            in_offset=bass.IndirectOffsetOnAxis(ap=index[b][:, :1], axis=0)).then_inc(gathered[b], 16)

            def step(i):
                count = snap(pool, i * 2 + 4)
                wait_apart(pool, pool_passed, (x_ps[0], i + 1), (x_ps[1], i + 1))
                gather(i + 1, count)
                for u in ON_POOL:
                    pool.wait_ge(hi_done, snap(pool, i * UNITS + (GU + u + 1)))
                    pool.tensor_tensor(w_lo[:, u], raw[:, staging(u)], f32(w_hi[:, u]), ALU.subtract).then_inc(lo_pool, 1)

            for b in range(2):
                pool.memset(y_sb[b][:], 0.0).then_inc(y_set, 1)
            gather(0, 2)
            steps(pool, step)

        @block.tensor
        def _(pe):
            def turn(of, out, done):
                for k in range(of.shape[-1] // P):
                    mm = pe.transpose(out[:, k * P:(k + 1) * P], of[:, k * P:(k + 1) * P], keep.ident[:])
                mm.then_inc(done, 1)

            def gate_up(i, b, last):
                for k in range(GU):
                    if b == 0:
                        semaphore, count = (lo_dve, k + 1) if isinstance(i, int) else split(i - 1, k)
                        pe.wait_ge(semaphore, snap(pe, count))
                    for half in range(2):
                        cols = slice(half * DE, (half + 1) * DE)
                        mm = product(pe, bank[:, 2 + 2 * b + half], xT_hi[b][:, k], xT_lo[b][:, k],
                                     w_hi[:, k, cols], w_lo[:, k, cols], k == 0, k == GU - 1)
                    if last:
                        mm.then_inc(gu_used, 1)
                if not last:
                    mm.then_inc(gu_ps, 1)

            def down(i, b, last, final):
                for k in range(DN):
                    if b == 0:
                        semaphore, count = split(i - 1, GU + k) if not final else (
                            (lo_dve, i * (UNITS - len(ON_POOL)) + GU) if k % 2 == 0 else (lo_pool, i * len(ON_POOL)))
                        pe.wait_ge(semaphore, snap(pe, count))
                    for half in range(2):
                        cols = slice(half * 512, (half + 1) * 512)
                        mm = product(pe, bank[:, (0, 6)[b] + half], hT_hi[b][:, k], hT_lo[b][:, k],
                                     w_hi[:, GU + k, cols], w_lo[:, GU + k, cols], k == 0, k == DN - 1)
                    if last:
                        mm.then_inc(down_used, 1)
                if not last:
                    mm.then_inc(down_ps, 1)

            def turn_hidden(i, had_b, b_before):
                pe.wait_ge(hid_done[0], snap(pe, i * 1))
                pe.wait_ge(y_kept[0], snap(pe, i * 1))
                turn(hid[0], bank[:, 0], hid_ps[0])
                with pe.If(had_b == 1):
                    pe.wait_ge(hid_done[1], snap(pe, b_before + 1))
                    turn(hid[1], bank[:, 1], hid_ps[1])

            def turn_tokens(slot, b_before, b_until):
                pe.wait_ge(gathered[0], snap(pe, slot * 16 + 16))
                pe.wait_ge(y_kept[1], snap(pe, b_before))
                turn(tokens[0], pair(6), x_ps[0])
                pe.wait_ge(gathered[1], snap(pe, slot * 16 + 16))
                pe.wait_ge(hid_done[1], snap(pe, b_until))
                turn(tokens[1], pair(4), x_ps[1])

            def finish(i, had_b, b_done, final=False):
                pe.wait_ge(hT_l[0], snap(pe, i * 1))
                pe.wait_ge(hT_l[1], snap(pe, b_done))
                with pe.If(had_b == 1):
                    down(i, 0, False, final)
                    down(i, 1, True, final)
                with pe.Else():
                    down(i, 0, True, final)

            def step(i):
                has_b = second(pe, i)
                b_here = order(pe, i)
                b_next = snap(pe, b_here + has_b)
                if isinstance(i, int):
                    had_b, b_before = None, 1
                else:
                    had_b = second(pe, i - 1)
                    b_before = order(pe, i - 1)
                pe.wait_ge(xT_l, snap(pe, i * 2 + 2))
                if not isinstance(i, int):
                    pe.wait_ge(hid_done[0], snap(pe, i * 1))
                with pe.If(has_b == 1):
                    gate_up(i, 0, False)
                    if had_b is not None:
                        turn_hidden(i, had_b, b_before)
                    gate_up(i, 1, True)
                with pe.Else():
                    gate_up(i, 0, True)
                    if had_b is not None:
                        turn_hidden(i, had_b, b_before)
                    pe.sem_inc(pe_passed, 1)
                turn_tokens(i + 1, b_before, b_next)
                if had_b is not None:
                    pe.wait_ge(xT_l, snap(pe, i * 2 + 3))
                    finish(i, had_b, b_here)

            turn_tokens(0, 1, 1)
            steps(pe, step)
            slots = total(pe, 0, LEAST)
            had_b = second(pe, slots - 1)
            turn_hidden(slots, had_b, order(pe, slots - 1))
            finish(slots, had_b, order(pe, slots), final=True)

        @block.scalar
        def _(act):
            def high(i, u):
                b = staging(u)
                act.wait_ge(raw_in[b], snap(act, arrived(i, u)))
                if u < GU:
                    act.wait_ge(gu_used, snap(act, i * GU + (u + 1)))
                elif not isinstance(i, int):
                    act.wait_ge(down_used, snap(act, i * DN - (DN - 1 - (u - GU))))
                act.activation(w_hi[:, u], raw[:, b], ACT.Copy, scale=gain(u) if u < GU else 1.0).then_inc(hi_done, 1)

            def gate(i, b, after, count):
                act.wait_ge(after, snap(act, count))
                act.activation(silu[b][:], bank[:, 2 + 2 * b], ACT.Silu).then_inc(silu_done[b], 1)

            def turned_hidden(i, had_b, b_before):
                act.wait_ge(hid_ps[0], snap(act, i * 1))
                act.activation(hT_hi[0][:], by_chunk(bank[:, 0]), ACT.Copy).then_inc(hT_h[0], 1)
                with act.If(had_b == 1):
                    act.wait_ge(hid_ps[1], snap(act, b_before))
                    act.activation(hT_hi[1][:], by_chunk(bank[:, 1]), ACT.Copy).then_inc(hT_h[1], 1)

            def turned_tokens(slot, b):
                act.wait_ge(x_ps[b], snap(act, slot + 1))
                act.activation(xT_hi[b][:], by_chunk(pair((6, 4)[b])), ACT.Copy).then_inc(xT_h, 1)

            def result(b, first_row, after, count, kept, stored):
                act.wait_ge(after, snap(act, count))
                act.wait_ge(y_out[b], snap(act, stored * 16))
                act.activation(y_sb[b][:], pair((0, 6)[b]), ACT.Copy).then_inc(y_kept[b], 1)
                act.wait_ge(y_kept[b], snap(act, kept))
                act.dma_start(y[bass.ds(snap(act, first_row + b * P), P), :], y_sb[b][:]).then_inc(y_out[b], 16)

            def results(i, had_b, b_before):
                first_row = planned(act, Routed.ROW, i - 1, 0, 2 * SEQ)
                wait_apart(act, act_passed, (y_out[1], b_before * 16))
                with act.If(had_b == 1):
                    result(0, first_row, down_ps, b_before, i + 1, i * 1)
                    result(1, first_row, down_used, i * DN, b_before + 1, b_before)
                with act.Else():
                    result(0, first_row, down_used, i * DN, i + 1, i * 1)

            def step(i):
                has_b = second(act, i)
                b_here = order(act, i)
                first = isinstance(i, int)
                if not first:
                    had_b = second(act, i - 1)
                    b_before = order(act, i - 1)
                with act.If(has_b == 1):
                    gate(i, 0, gu_ps, b_here)
                    if not first:
                        turned_hidden(i, had_b, b_before)
                    for u in range(EARLY):
                        high(i, u)
                    gate(i, 1, gu_used, i * GU + GU)
                with act.Else():
                    for u in range(EARLY):
                        high(i, u)
                    gate(i, 0, gu_used, i * GU + GU)
                    if not first:
                        turned_hidden(i, had_b, b_before)
                    act.sem_inc(act_passed, 1)
                turned_tokens(i + 1, 0)
                turned_tokens(i + 1, 1)
                for u in range(EARLY, UNITS):
                    high(i, u)
                if not first:
                    results(i, had_b, b_before)

            act.sem_inc(y_kept[0], 1)
            act.sem_inc(y_kept[1], 1)
            for b in range(2):
                act.wait_ge(y_set, 2)
                act.dma_start(y[2 * SEQ + b * P:2 * SEQ + (b + 1) * P, :], y_sb[b][:]).then_inc(y_out[b], 16)
            for b in range(2):
                turned_tokens(0, b)
            for k in range(GU):
                act.wait_ge(raw_in[k % RAW], (k // RAW + 1) * 32)
                act.activation(w_hi[:, k], raw[:, k % RAW], ACT.Copy, scale=gain(k)).then_inc(hi_done, 1)
            steps(act, step)
            slots, seconds = total(act, 0, LEAST), total(act, 1, 0)
            had_b = second(act, slots - 1)
            b_before = order(act, slots - 1)
            turned_hidden(slots, had_b, b_before)
            results(slots, had_b, b_before)
            act.wait_ge(y_out[0], snap(act, slots * 16 + 16))
            wait_apart(act, act_passed, (y_out[1], seconds * 16 + 16))

        @block.vector
        def _(dve):
            def low(i, u):
                b = staging(u)
                if u not in ON_POOL:
                    dve.wait_ge(hi_done, snap(dve, i * UNITS + (GU + u + 1)))
                    if u < GU:
                        dve.scalar_tensor_tensor(w_lo[:, u], raw[:, b], gain(u), f32(w_hi[:, u]),
                                                 ALU.mult, ALU.subtract).then_inc(lo_dve, 1)
                    else:
                        dve.tensor_tensor(w_lo[:, u], raw[:, b], f32(w_hi[:, u]), ALU.subtract).then_inc(lo_dve, 1)

            def gated(i, b, silu_count):
                dve.wait_ge(silu_done[b], snap(dve, silu_count))
                if b == 0:
                    if not isinstance(i, int):
                        dve.wait_ge(hid_ps[0], snap(dve, i * 1))
                dve.tensor_tensor(hid[b][:], silu[b][:], bank[:, 3 + 2 * b], ALU.mult).then_inc(hid_done[b], 1)

            def turned_hidden(i, had_b, b_before):
                dve.wait_ge(hT_h[0], snap(dve, i * 1))
                dve.tensor_tensor(hT_lo[0][:], by_chunk(bank[:, 0]), f32(hT_hi[0][:]), ALU.subtract).then_inc(hT_l[0], 1)
                with dve.If(had_b == 1):
                    dve.wait_ge(hT_h[1], snap(dve, b_before))
                    dve.tensor_tensor(hT_lo[1][:], by_chunk(bank[:, 1]), f32(hT_hi[1][:]), ALU.subtract).then_inc(hT_l[1], 1)

            def turned_tokens(slot, b):
                dve.wait_ge(xT_h, snap(dve, slot * 2 + (b + 1)))
                dve.tensor_tensor(xT_lo[b][:], by_chunk(pair((6, 4)[b])), f32(xT_hi[b][:]), ALU.subtract).then_inc(xT_l, 1)

            def step(i):
                has_b = second(dve, i)
                b_here = order(dve, i)
                first = isinstance(i, int)
                if not first:
                    had_b = second(dve, i - 1)
                    b_before = order(dve, i - 1)
                with dve.If(has_b == 1):
                    gated(i, 0, i + 1)
                    if not first:
                        turned_hidden(i, had_b, b_before)
                    for u in range(EARLY):
                        low(i, u)
                    gated(i, 1, b_here)
                with dve.Else():
                    for u in range(EARLY):
                        low(i, u)
                    gated(i, 0, i + 1)
                    if not first:
                        turned_hidden(i, had_b, b_before)
                    dve.sem_inc(dve_passed, 1)
                turned_tokens(i + 1, 0)
                turned_tokens(i + 1, 1)
                for u in range(EARLY, UNITS):
                    low(i, u)

            dve.sem_inc(hid_done[1], 1)
            dve.sem_inc(hT_l[1], 1)
            for b in range(2):
                turned_tokens(0, b)
            for k in range(GU):
                dve.wait_ge(hi_done, k + 1)
                dve.scalar_tensor_tensor(w_lo[:, k], raw[:, k % RAW], gain(k), f32(w_hi[:, k]),
                                         ALU.mult, ALU.subtract).then_inc(lo_dve, 1)
            steps(dve, step)
            slots = total(dve, 0, LEAST)
            turned_hidden(slots, second(dve, slots - 1), order(dve, slots - 1))


def combine(nc, keep, ins, routed, x2, y, out):
    with ExitStack() as ctx:
        sb = lambda n, s, d=F32: ctx.enter_context(nc.sbuf_tensor(n, s, d))
        sem = semaphores(nc, ctx)
        index = [[sb(f"row_index{b}{c}", [P, 1], U32) for c in range(2)] for b in range(2)]
        ys = [[sb(f"y_row{b}{c}", [P, D]) for c in range(2)] for b in range(2)]
        xs = [sb(f"x_tile{b}", [P, D]) for b in range(2)]
        outs = [sb(f"out_tile{b}", [P, D]) for b in range(2)]
        square = sb("final_square", [P, D], BF16)
        gain = sb("gain_final", [P, D])
        ss, r, half = sb("final_ss", [P, 2]), sb("final_r", [P, 2]), sb("final_half", [P, 1])
        gain_in, half_set, passed = sem("gain_in"), sem("final_half_set"), sem("final_pool_passed")
        x_in = [sem(f"final_x_in{b}") for b in range(2)]
        y_in = [sem(f"final_y_in{b}") for b in range(2)]
        stored = [sem(f"final_stored{b}") for b in range(2)]
        index_ready, added, summed, squared = [sem(n) for n in ("row_index_ready", "added", "summed", "squared")]
        mean_ready, root_ready, scaled = sem("mean_ready"), sem("root_ready"), sem("scaled")
        block = ctx.enter_context(nc.Block())

        def steps(engine, step):
            step(0)
            with engine.Fori(1, TILES // 2 - 1) as j:
                step(j)
            step(TILES // 2 - 1)

        def is_last(j):
            return isinstance(j, int) and j == TILES // 2 - 1

        def is_first(j):
            return isinstance(j, int) and j == 0

        @block.sync
        def _(sp):
            def load(j, b):
                row = snap(sp, j * 2 * P + b * P)
                sp.dma_start(xs[b][:], x2[bass.ds(row, P), :]).then_inc(x_in[b], 16)

            def step(j):
                for b in range(2):
                    row = snap(sp, j * 2 * P + b * P)
                    sp.wait_ge(scaled, snap(sp, j * 2 + (b + 1)))
                    sp.dma_start(out[0, bass.ds(row, P), :], outs[b][:]).then_inc(stored[b], 16)
                    if not is_last(j):
                        load(j + 1, b)

            for b in range(2):
                load(0, b)
            sp.dma_start(gain[:], ins["g_final"].unsqueeze(0).broadcast_to((P, D))).then_inc(gain_in, 16)
            steps(sp, step)
            for b in range(2):
                sp.wait_ge(stored[b], 16 * (TILES // 2))

        @block.gpsimd
        def _(pool):
            def gather(j, b):
                for c in range(2):
                    pool.tensor_copy(index[b][c][:], routed.rows[:, c, bass.ds(j * 2 + b, 1)]).then_inc(index_ready, 1)
                wait_apart(pool, passed, (index_ready, j * 4 + (2 * b + 2)))
                for c in range(2):
                    pool.indirect_dma_start(out=ys[b][c][:], out_offset=None, in_=y[:, :],
                                            in_offset=bass.IndirectOffsetOnAxis(ap=index[b][c][:, :1], axis=0)).then_inc(y_in[b], 16)

            def step(j):
                for b in range(2):
                    n = j * 2 + (b + 1)
                    if not is_last(j):
                        wait_apart(pool, passed, (summed, n))
                        gather(j + 1, b)
                    wait_apart(pool, passed, (squared, n))
                    if not is_first(j):
                        wait_apart(pool, passed, (scaled, n - 2))
                    pool.tensor_scalar(r[:, b:b + 1], ss[:, b:b + 1], 1.0 / D, EPS, ALU.mult, ALU.add).then_inc(mean_ready, 1)
                    pool.wait_ge(mean_ready, snap(pool, n))
                    pool.tensor_tensor(r[:, b:b + 1], r[:, b:b + 1], half[:], ALU.pow).then_inc(root_ready, 1)

            pool.memset(half[:], -0.5).then_inc(half_set, 1)
            pool.wait_ge(half_set, 1)
            for b in range(2):
                gather(0, b)
            steps(pool, step)

        @block.scalar
        def _(act):
            def step(j):
                for b in range(2):
                    n = j * 2 + (b + 1)
                    act.wait_ge(summed, snap(act, n))
                    if not (is_first(j) and b == 0):
                        act.wait_ge(squared, snap(act, n - 1))
                    if not is_first(j):
                        act.wait_ge(mean_ready, snap(act, n - 2))
                    act.activation(square[:], xs[b][:], ACT.Square, accum_out=ss[:, b:b + 1]).then_inc(squared, 1)

            steps(act, step)

        @block.vector
        def _(dve):
            def step(j):
                for b in range(2):
                    n = j * 2 + (b + 1)
                    gate = lambda c: routed.gates[:, c, bass.ds(j * 2 + b, 1)]
                    dve.wait_ge(x_in[b], snap(dve, j * 16 + 16))
                    dve.wait_ge(y_in[b], snap(dve, j * 32 + 32))
                    dve.scalar_tensor_tensor(xs[b][:], ys[b][0][:], gate(0), xs[b][:], ALU.mult, ALU.add).then_inc(added, 1)
                    dve.wait_ge(added, snap(dve, n))
                    dve.scalar_tensor_tensor(xs[b][:], ys[b][1][:], gate(1), xs[b][:], ALU.mult, ALU.add).then_inc(summed, 1)
                for b in range(2):
                    n = j * 2 + (b + 1)
                    dve.wait_ge(summed, snap(dve, n))
                    dve.wait_ge(root_ready, snap(dve, n))
                    if not is_first(j):
                        dve.wait_ge(stored[b], snap(dve, j * 16))
                    dve.scalar_tensor_tensor(outs[b][:], xs[b][:], r[:, b:b + 1], gain[:], ALU.mult, ALU.mult).then_inc(scaled, 1)

            dve.wait_ge(gain_in, 16)
            steps(dve, step)


def hybrid_layer_kernel(nc, out, **ins):
    dram = lambda name, rows: nc.dram_tensor(name, (rows, D), F32, kind="Internal").ap()
    x1, x2, h3 = dram("x1", SEQ), dram("x2", SEQ), dram("h3", SEQ)
    y = dram("y_rows", 2 * SEQ + SLOT)
    with ExitStack() as ctx:
        keep = Kept(nc, ctx)
        setup(nc, keep, ins)
        mixer(nc, keep, ins, x1)
        with Fold(nc) as fold:
            folding(nc, keep, ins, fold)
            xattn(nc, keep, ins, fold, x1, x2, h3)
        routed = Routed(nc, ctx)
        routing(nc, keep, ins, routed)
        moe(nc, keep, ins, routed, h3, y)
        combine(nc, keep, ins, routed, x2, y, out)


_INS = ["x", "mem", "g_mix", "w_in", "conv_w", "g_v", "w_s", "b_s", "g_out_conv", "g_out_gmlp", "w_out",
        "g_xattn", "g_mem", "w_q", "w_k", "w_v", "w_o", "g_ffn", "w_grp", "b_grp", "w_rt", "b_rt",
        "w_gate", "w_up", "w_down", "g_final"]


def kernel(**inputs):
    import numpy as _np
    import concourse.bacc as _bacc
    from concourse import mybir as _mybir
    from concourse.bass_utils import run_bass_kernel_spmd as _run

    nc = _bacc.Bacc("TRN2", target_bir_lowering=False, num_devices=1)
    arrays, args = {}, {}
    for name in _INS:
        a = _np.ascontiguousarray(inputs[name])
        arrays[f"in_{name}_dram"] = a
        args[name] = nc.dram_tensor(f"in_{name}_dram", a.shape, _mybir.dt.from_np(a.dtype), kind="ExternalInput").ap()
    out = nc.dram_tensor("out_0_dram", (1, SEQ, D), F32, kind="ExternalOutput").ap()
    hybrid_layer_kernel(nc, out, **args)
    r = _run(nc, [arrays], core_ids=[0])
    return r.results[0]["out_0_dram"]
```

```python
from contextlib import ExitStack

import concourse.bass as bass
import concourse.mybir as mybir
import numpy as np

F32 = mybir.dt.float32
F32R = mybir.dt.float32r
BF16 = mybir.dt.bfloat16
I32 = mybir.dt.int32
U32 = mybir.dt.uint32
ALU = mybir.AluOpType
ACT = mybir.ActivationFunctionType
AX = mybir.AxisListType

P = 128
D = 1024
KD = D // P
SEQ = 2048
TILES = SEQ // P
CONV = 512
GMLP = 512
HEADS = 8
HEAD = GMLP // HEADS
CHUNK = 128
CONV_K = 3
MEM = 256
XHEADS = 4
XDIM = D // XHEADS
GROUPS = 4
PER_GROUP = 8
EXPERTS = GROUPS * PER_GROUP
DE = 512
EPS = 1e-6

SUPER = 512
SUPERS = SEQ // SUPER
ST = SUPER // P

SLOT = 2 * P
SLOTS = SEQ * 2 // SLOT + EXPERTS - 1
LISTED = 2 * (SLOTS + 1)

COLS = {}
at = 0
for name, n in (("g_mix", 8), ("g_out_conv", 4), ("g_out_gmlp", 4), ("g_xattn", 8), ("g_ffn", 8),
                ("g_v", 4), ("conv_w", 12)):
    COLS[name] = at
    at += n
GAIN_ROWS = at


def f32(ap):
    return ap.bitcast(F32)


def snap(engine, value):
    return value if isinstance(value, int) else engine.snap(value)


def semaphores(nc, ctx):
    made = []
    ctx.callback(nc.all_engine_barrier)
    ctx.callback(lambda: nc.clear_and_free_semaphores(made))

    def make(name):
        made.append(nc.alloc_semaphore(name))
        return made[-1]
    return make


def wait_apart(engine, passed, *waits):
    waits = [(semaphore, snap(engine, value)) for semaphore, value in waits]
    for semaphore, value in waits:
        engine.wait_ge(semaphore, value)
    engine.sem_inc(passed, 1)


def product(pe, out, ahi, alo, bhi, blo, first, last):
    pe.matmul(out, ahi, bhi, start=first, stop=False)
    pe.matmul(out, ahi, blo, start=False, stop=False)
    return pe.matmul(out, alo, bhi, start=False, stop=last)


class Kept:

    def __init__(self, nc, ctx):
        sb = lambda n, s, d=F32: ctx.enter_context(nc.sbuf_tensor(n, s, d))
        self.ident = sb("ident", [P, P])
        self.ones = sb("ones", [P, 2])
        self.cols = sb("gain_cols", [P, GAIN_ROWS])
        self.logits = sb("logits", [P, TILES, GROUPS + EXPERTS])


class Fold:

    def __init__(self, nc):
        self.nc, self.ctx = nc, ExitStack()

    def __enter__(self):
        sb = lambda n: self.ctx.enter_context(self.nc.sbuf_tensor(n, [P, KD, XHEADS * MEM], F32R))
        self.a_hi, self.a_lo, self.b_hi, self.b_lo = (sb(n) for n in ("A_hi", "A_lo", "B_hi", "B_lo"))
        return self

    def __exit__(self, *exc):
        self.ctx.close()


def setup(nc, keep, ins):
    with ExitStack() as ctx:
        rows = ctx.enter_context(nc.sbuf_tensor("gain_rows", [GAIN_ROWS, P], F32))
        ps = ctx.enter_context(nc.psum_tensor("setup_ps", [P, 512], F32))
        sem = semaphores(nc, ctx)
        loaded = sem("gains_loaded")
        zeroed = sem("ident_zeroed")
        ident_ready = sem("ident_ready")
        turned = sem("gains_turned")
        kept = sem("gains_kept")
        block = ctx.enter_context(nc.Block())

        @block.sync
        def _(sp):
            for name in COLS:
                n = ins[name].shape[1] // P if name != "conv_w" else CONV_K * CONV // P
                src = ins[name].rearrange("a (k p) -> (a k) p", p=P) if name != "conv_w" else \
                    ins[name].rearrange("a j (k p) -> (a j k) p", p=P)
                sp.dma_start(rows[COLS[name]:COLS[name] + n, :], src).then_inc(loaded, 16)

        @block.gpsimd
        def _(pool):
            pool.memset(keep.ident[:], 0.0).then_inc(zeroed, 1)
            pool.memset(keep.ones[:], 1.0).then_inc(zeroed, 1)
            pool.wait_ge(zeroed, 1)
            pool.affine_select(out=keep.ident[:], in_=keep.ident[:], compare_op=ALU.not_equal, fill=1.0,
                               base=0, pattern=[[-1, P]], channel_multiplier=1).then_inc(ident_ready, 1)

        @block.tensor
        def _(pe):
            pe.wait_ge(loaded, 16 * len(COLS))
            pe.wait_ge(ident_ready, 1)
            pe.transpose(ps[:, 0:GAIN_ROWS], rows[:], keep.ident[0:GAIN_ROWS, 0:GAIN_ROWS]).then_inc(turned, 1)

        @block.vector
        def _(dve):
            dve.wait_ge(turned, 1)
            dve.tensor_copy(keep.cols[:], ps[:, 0:GAIN_ROWS]).then_inc(kept, 1)


def mixer(nc, keep, ins, x1):
    UNITS = 4 + 4 * 4
    FIRST_WO = 4
    PAIR = (4, 6, 0)
    w_in, w_out, x = ins["w_in"], ins["w_out"], ins["x"]
    col = lambda name, k: keep.cols[:, COLS[name] + k:COLS[name] + k + 1]
    with ExitStack() as ctx:
        sb = lambda n, s, d=F32: ctx.enter_context(nc.sbuf_tensor(n, s, d))
        sem = semaphores(nc, ctx)
        bank = ctx.enter_context(nc.psum_tensor("mix_ps", [P, 8, 512], F32))

        wo_hi = sb("wo_hi", [P, KD, D], F32R)
        wo_lo = sb("wo_lo", [P, KD, D], F32R)
        w_raw = sb("w_raw", [P, 2, 1024])
        w_hi = sb("w_hi", [P, 2, 1024], F32R)
        w_lo = sb("w_lo", [P, 2, 1024], F32R)
        xin = sb("xin", [P, 2, D])
        gain = sb("gain_mix", [P, D])
        square = sb("square_out", [P, D], BF16)
        hT_hi = sb("hT_hi", [P, KD, SUPER], F32R)
        hT_lo = sb("hT_lo", [P, KD, SUPER], F32R)
        yT_hi = sb("yT_hi", [P, KD, SUPER], F32R)
        yT_lo = sb("yT_lo", [P, KD, SUPER], F32R)
        v = sb("v", [P, ST, GMLP])
        wsT = sb("wsT", [P, HEADS, CHUNK])
        bias = sb("b_s_rows", [P, HEADS // 2, CHUNK])
        c_sb = sb("c_sb", [P, SUPER])
        z = sb("z", [P, SUPER + CONV_K - 1])
        halo = sb("halo", [P, 4, CONV_K - 1])
        ya = sb("ya", [P, SUPER])
        u_sb = sb("u_sb", [P, SUPER])
        yb = sb("yb", [P, SUPER])
        sq = sb("sq", [P, SUPER])
        sum_a = sb("sum_a", [P, SUPER])
        sum_b = sb("sum_b", [P, SUPER])
        xres = sb("xres", [P, D])
        ssx = sb("ssx", [P, 2])
        rx = sb("rx", [P, 2])
        ssv = sb("ssv", [P, ST, HEADS])
        rv = sb("rv", [P, ST, HEADS])
        ssy = sb("ssy", [P, 2 * ST])
        ry = sb("ry", [P, 2 * ST])
        half = sb("neg_half", [P, HEADS])

        wo_in, wo_hi_done, wo_lo_done = sem("wo_in"), sem("wo_hi_done"), sem("wo_lo_done")
        raw_in = [sem(f"w_raw_in{b}") for b in range(2)]
        hi_done, lo_done, unit_used = sem("w_hi_done"), sem("w_lo_done"), sem("w_unit_used")
        ws_in, ws_turned, ws_copied, ws_masked = sem("ws_in"), sem("ws_turned"), sem("ws_copied"), sem("ws_masked")
        pool_passed, sp_passed = sem("pool_passed"), sem("sp_passed")
        const_in, pool_const, halo_zero = sem("const_in"), sem("pool_const"), sem("halo_zero")
        x_in = [sem(f"x_in{b}") for b in range(2)]
        x_sq, x_ms, x_r, x_scaled = sem("x_sq"), sem("x_ms"), sem("x_r"), sem("x_scaled")
        xT_ps, hT_hi_done, hT_lo_done = sem("xT_ps"), sem("hT_hi_done"), sem("hT_lo_done")
        v_gelu, v_sq, v_ss, v_ms, v_r, v_done = [sem(n) for n in (
            "v_gelu", "v_sq", "v_ss", "v_ms", "v_r", "v_done")]
        c_done, z_halo, z_done, conv0, conv1, conv2, ya_done = [sem(n) for n in (
            "c_done", "z_halo", "z_done", "conv0", "conv1", "conv2", "ya_done")]
        u_done, s_ps, t_done, yb_done, halo_kept = [sem(n) for n in (
            "u_done", "s_ps", "t_done", "yb_done", "halo_kept")]
        y_hi, y_lo, y_sq, y_sum = [sem(n) for n in ("y_hi", "y_lo", "y_sq", "y_sum")]
        ssy_ps, ssy_done, ry_ms, ry_done = [sem(n) for n in ("ssy_ps", "ssy_done", "ry_ms", "ry_done")]
        o_ps, o_done, res_in, x1_out = [sem(n) for n in ("o_ps", "o_done", "res_in", "x1_out")]
        block = ctx.enter_context(nc.Block())

        def unit_source(u):
            if u < 4:
                return w_in[0, 2 * u * P:(2 * u + 2) * P, 3 * CONV + GMLP:].rearrange("(k p) n -> p k n", p=P)
            g, which = divmod(u - 4, 4)
            start = {0: CONV, 1: 2 * CONV, 2: 0, 3: 3 * CONV}[which] + g * P
            return w_in[0, :, start:start + P].rearrange("(k p) n -> p k n", p=P)

        def as_unit(tile, u):
            return tile[:, u % 2].rearrange("p (k n) -> p k n", k=2 if u < 4 else KD)

        def steps(engine, step):
            step(0, False)
            with engine.Fori(1, SUPERS - 1) as i:
                step(i, False)
            step(SUPERS - 1, True)

        def is_first(i):
            return isinstance(i, int) and i == 0

        @block.sync
        def _(sp):
            def load_x(tiles, t):
                row = snap(sp, (tiles + t) * P)
                sp.wait_ge(xT_ps, tiles + t + 1)
                sp.dma_start(xin[:, t % 2], x[0, bass.ds(row, P), :]).then_inc(x_in[t % 2], 16)

            def load_unit(units, u):
                sp.wait_ge(hi_done, units + (u + 1))
                sp.wait_ge(lo_done, units + (u + 1))
                sp.dma_start(as_unit(w_raw, u), unit_source(u)).then_inc(raw_in[u % 2], 16)

            def step(i, last):
                units = snap(sp, i * UNITS)
                units_next = snap(sp, i * UNITS + UNITS)
                tiles = snap(sp, i * ST)
                tiles_next = snap(sp, i * ST + ST)
                for u in range(2, UNITS):
                    load_unit(units, u)
                    if u == 10 and not last:
                        load_x(tiles_next, 0)
                        load_x(tiles_next, 1)
                    k = u - FIRST_WO - 2
                    if is_first(i) and 0 <= k < KD:
                        if k:
                            sp.wait_ge(wo_lo_done, k)
                        sp.dma_start(xres[:], w_out[0, k * P:(k + 1) * P, :]).then_inc(wo_in, 16)
                if is_first(i):
                    sp.wait_ge(wo_lo_done, KD)
                for t in range(ST):
                    row = snap(sp, (tiles + t) * P)
                    sp.dma_start(xres[:], x[0, bass.ds(row, P), :]).then_inc(res_in, 16)
                    if t < 2 and not last:
                        load_x(tiles_next, t + 2)
                    if t == 2 and not last:
                        load_unit(units_next, 0)
                        load_unit(units_next, 1)
                    done = snap(sp, (tiles + t) * 16 + 16)
                    both = snap(sp, (tiles + t) * 2 + 5)
                    sp.wait_ge(o_done, both)
                    sp.dma_start(x1[bass.ds(row, P), :], xres[:]).then_inc(x1_out, 16)
                    wait_apart(sp, sp_passed, (x1_out, done))

            sp.dma_start(gain[:], ins["g_mix"].broadcast_to((P, D))).then_inc(const_in, 16)
            for h in range(HEADS):
                sp.dma_start(bias[(h % 2) * HEAD:(h % 2 + 1) * HEAD, h // 2, :],
                             ins["b_s"][0, h:h + 1, :].broadcast_to((HEAD, CHUNK))).then_inc(const_in, 16)
            load_x(0, 0)
            load_x(0, 1)
            sp.dma_start(v[:, 0:2, :].rearrange("p a (h s) -> p (a h) s", s=CHUNK),
                         ins["w_s"][0].rearrange("h t s -> t h s")).then_inc(ws_in, 16)
            load_x(0, 2)
            load_x(0, 3)
            load_unit(0, 0)
            load_unit(0, 1)
            steps(sp, step)

        @block.gpsimd
        def _(pool):
            def inverse_root(ss, out, n, ready, ms, done, k, ahead=0):
                wait_apart(pool, pool_passed, (ready, k + ahead))
                pool.tensor_scalar(out, ss, 1.0 / n, EPS, ALU.mult, ALU.add).then_inc(ms, 1)
                pool.wait_ge(ms, k)
                pool.tensor_tensor(out, out, half[:, 0:out.shape[-1]], ALU.pow).then_inc(done, 1)

            def norm_x(tiles, t):
                pool.wait_ge(x_scaled, tiles + (t + 1))
                inverse_root(ssx[:, t % 2:t % 2 + 1], rx[:, t % 2:t % 2 + 1], D, x_sq, x_ms, x_r, tiles + (t + 1), 1)

            def add_square(target, k, first):
                wait_apart(pool, pool_passed, (y_sum, k), (y_sq, k + 2))
                if first:
                    pool.tensor_copy(target, sq[:]).then_inc(y_sum, 1)
                else:
                    pool.tensor_tensor(target, target, sq[:], ALU.add).then_inc(y_sum, 1)

            def step(i, last):
                groups = snap(pool, i * 4)
                ys = snap(pool, i * 8)
                tiles = snap(pool, i * ST)
                tiles_next = snap(pool, i * ST + ST)
                for t in range(ST):
                    inverse_root(ssv[:, t], rv[:, t], HEAD, v_ss, v_ms, v_r, tiles + (t + 1), 1)
                pool.wait_ge(ssy_ps, snap(pool, i + 1))
                for g in range(4):
                    if g == 3 and not last:
                        norm_x(tiles_next, 0)
                        norm_x(tiles_next, 1)
                    add_square(sum_a[:], ys + (2 * g + 1), g == 0)
                    pool.wait_ge(u_done, groups + (g + 2))
                    pool.wait_ge(t_done, groups + (g + 3))
                    pool.tensor_tensor(yb[:], yb[:], u_sb[:], ALU.mult).then_inc(yb_done, 1)
                    add_square(sum_b[:], ys + (2 * g + 2), g == 0)
                n = snap(pool, i + 1)
                inverse_root(ssy[:], ry[:], CONV, ssy_done, ry_ms, ry_done, n)
                if not last:
                    norm_x(tiles_next, 2)
                    norm_x(tiles_next, 3)

            pool.memset(half[:], -0.5).then_inc(pool_const, 1)
            pool.wait_ge(pool_const, 1)
            pool.sem_inc(y_sum, 1)
            pool.sem_inc(yb_done, 1)
            pool.sem_inc(x_r, 2)
            for t in range(ST):
                norm_x(0, t)
            pool.wait_ge(ws_copied, 1)
            pool.affine_select(out=wsT[:], in_=wsT[:], compare_op=ALU.is_ge, fill=0.0, base=0,
                               pattern=[[0, HEADS], [1, CHUNK]], channel_multiplier=-1).then_inc(ws_masked, 1)
            steps(pool, step)

        @block.scalar
        def _(act):
            def split_raw(out, uses16, u, k):
                act.wait_ge(raw_in[u % 2], uses16)
                act.activation(out, w_raw[:, u % 2], ACT.Copy).then_inc(hi_done, 1)

            def split_unit(units, uses16, u):
                act.wait_ge(unit_used, units + (u + 1))
                split_raw(w_hi[:, u % 2], uses16 + 16 * (u // 2 + 1), u, None)

            def square_x(tiles, halves16, t):
                act.wait_ge(x_in[t % 2], halves16 + 16 * (t // 2 + 1))
                act.wait_ge(x_r, tiles + (t + 1))
                act.wait_ge(x_sq, tiles + (t + 1))
                act.activation(square[:], xin[:, t % 2], ACT.Square,
                               accum_out=ssx[:, t % 2:t % 2 + 1]).then_inc(x_sq, 1)

            def turn_x(tiles, t):
                act.wait_ge(xT_ps, tiles + (t + 3))
                act.activation(hT_hi[:, :, t * P:(t + 1) * P],
                               bank[:, 2:4, :].rearrange("p b (k n) -> p (b k) n", n=P), ACT.Copy).then_inc(hT_hi_done, 1)

            def keep_y(chunk, tile, ready, k_ready, y_index):
                act.wait_ge(ready, k_ready)
                act.activation(yT_hi[:, chunk], tile[:], ACT.Copy).then_inc(y_hi, 1)
                act.wait_ge(y_sum, y_index + 1)
                act.activation(sq[:], tile[:], ACT.Square).then_inc(y_sq, 1)

            def step(i, last):
                units = snap(act, i * UNITS)
                units_next = snap(act, i * UNITS + UNITS)
                uses = snap(act, i * (UNITS * 8))
                uses_next = snap(act, i * (UNITS * 8) + UNITS * 8)
                groups = snap(act, i * 4)
                ys = snap(act, i * 8)
                tiles = snap(act, i * ST)
                tiles_next = snap(act, i * ST + ST)
                halves_next = snap(act, (i + 1) * (ST * 8))
                used = snap(act, i * UNITS + 2)
                for u in range(UNITS):
                    g, which = divmod(u - 4, 4)
                    if u + 2 < UNITS:
                        split_unit(units, uses, u + 2)
                    k = u - FIRST_WO
                    if is_first(i) and 0 <= k < KD:
                        gain_col = col("g_out_conv", k) if k < 4 else col("g_out_gmlp", k - 4)
                        act.wait_ge(wo_in, 16 * (k + 1))
                        act.activation(wo_hi[:, k], xres[:], ACT.Copy, scale=gain_col).then_inc(wo_hi_done, 1)
                    if u == 14 and not last:
                        square_x(tiles_next, halves_next, 0)
                        square_x(tiles_next, halves_next, 1)
                    if u == 3:
                        act.wait_ge(s_ps, groups + 1)
                        for t in range(ST):
                            act.wait_ge(unit_used, used + (u + 1))
                            act.activation(v[:, t], bank[:, t], ACT.Gelu_apprx_tanh).then_inc(v_gelu, 1)
                    if u >= 4 and which == 0:
                        act.wait_ge(unit_used, used + (u + 1))
                        act.wait_ge(z_done, groups + (g + 1))
                        act.activation(c_sb[:], bank[:, 4], ACT.Copy).then_inc(c_done, 1)
                        if g:
                            keep_y(4 + g - 1, yb, yb_done, groups + (g + 1), ys + (2 * g - 1))
                    if u >= 4 and which == 3:
                        act.wait_ge(unit_used, used + (u + 1))
                        act.wait_ge(yb_done, groups + (g + 1))
                        act.activation(u_sb[:], bank[:, 7], ACT.Gelu_apprx_tanh).then_inc(u_done, 1)
                        if g == 0:
                            act.wait_ge(o_ps, ys + 1)
                        keep_y(g, ya, ya_done, groups + (g + 2), ys + 2 * g)
                keep_y(7, yb, yb_done, groups + 5, ys + 7)
                if not last:
                    for t in range(ST):
                        turn_x(tiles_next, t)
                        if t < 2:
                            square_x(tiles_next, halves_next, t + 2)
                        if t == 2:
                            split_unit(units_next, uses_next, 0)
                            split_unit(units_next, uses_next, 1)

            act.sem_inc(x_sq, 1)
            act.sem_inc(y_sq, 2)
            act.sem_inc(hi_done, 2)
            act.sem_inc(c_done, 1)
            act.sem_inc(u_done, 1)
            act.sem_inc(hT_hi_done, 1)
            for t in range(ST):
                square_x(0, 0, t)
                if t >= 1:
                    turn_x(0, t - 1)
            turn_x(0, 3)
            split_unit(0, 0, 0)
            split_unit(0, 0, 1)
            steps(act, step)

        @block.vector
        def _(dve):
            def split_unit(units, u):
                dve.wait_ge(hi_done, units + (u + 3))
                dve.wait_ge(unit_used, units + (u + 1))
                dve.tensor_tensor(w_lo[:, u % 2], w_raw[:, u % 2], f32(w_hi[:, u % 2]), ALU.subtract).then_inc(lo_done, 1)

            def scale_x(tiles, t):
                dve.wait_ge(x_r, tiles + (t + 3))
                if t == 0:
                    dve.wait_ge(const_in, 16 * (1 + HEADS))
                dve.scalar_tensor_tensor(xin[:, t % 2], xin[:, t % 2], rx[:, t % 2:t % 2 + 1], gain[:],
                                         ALU.mult, ALU.mult).then_inc(x_scaled, 1)

            def turn_x(tiles, t):
                dve.wait_ge(hT_hi_done, tiles + (t + 2))
                cols = slice(t * P, (t + 1) * P)
                dve.tensor_tensor(hT_lo[:, :, cols], bank[:, 2:4, :].rearrange("p b (k n) -> p (b k) n", n=P),
                                  f32(hT_hi[:, :, cols]), ALU.subtract).then_inc(hT_lo_done, 1)

            def lower_y(chunk, tile, k):
                dve.wait_ge(y_hi, k)
                dve.tensor_tensor(yT_lo[:, chunk], tile[:], f32(yT_hi[:, chunk]), ALU.subtract).then_inc(y_lo, 1)

            def step(i, last):
                units = snap(dve, i * UNITS)
                units_next = snap(dve, i * UNITS + UNITS)
                used = snap(dve, i * UNITS + 2)
                groups = snap(dve, i * 4)
                ys = snap(dve, i * 8)
                tiles = snap(dve, i * ST)
                tiles_next = snap(dve, i * ST + ST)
                for u in range(UNITS):
                    g, which = divmod(u - 4, 4)
                    if u + 2 < UNITS:
                        split_unit(units, u + 2)
                    k = u - FIRST_WO
                    if is_first(i) and 0 <= k < KD:
                        gain_col = col("g_out_conv", k) if k < 4 else col("g_out_gmlp", k - 4)
                        dve.wait_ge(wo_hi_done, k + 1)
                        dve.scalar_tensor_tensor(wo_lo[:, k], xres[:], gain_col, f32(wo_hi[:, k]),
                                                 ALU.mult, ALU.subtract).then_inc(wo_lo_done, 1)
                    if u == 16 and not last:
                        scale_x(tiles_next, 0)
                        scale_x(tiles_next, 1)
                    if u == 3:
                        for t in range(ST):
                            dve.wait_ge(v_gelu, tiles + (t + 1))
                            dve.wait_ge(v_ss, tiles + (t + 1))
                            dve.tensor_tensor(z[:, 0:GMLP], v[:, t], v[:, t], ALU.mult).then_inc(v_sq, 1)
                            dve.wait_ge(v_sq, tiles + (t + 1))
                            dve.tensor_reduce(ssv[:, t], z[:, 0:GMLP].rearrange("p (h d) -> p h d", d=HEAD),
                                              AX.X, ALU.add).then_inc(v_ss, 1)
                    if u == 4:
                        for t in range(ST):
                            dve.wait_ge(v_r, tiles + (t + 1))
                            heads = v[:, t].rearrange("p (h d) -> p h d", d=HEAD)
                            dve.tensor_tensor(heads, heads, rv[:, t].unsqueeze(2).broadcast_to((P, HEADS, HEAD)),
                                              ALU.mult).then_inc(v_done, 1)
                        dve.wait_ge(v_ss, tiles + (ST + 1))
                    if u >= 8 and which == 0:
                        lower_y(4 + g - 1, yb, ys + 2 * g)
                    if u >= 4 and which == 1:
                        dve.wait_ge(unit_used, used + (u + 1))
                        dve.wait_ge(c_done, groups + (g + 2))
                        dve.wait_ge(halo_kept, groups + (g + 1))
                        dve.tensor_copy(z[:, 0:2], halo[:, g]).then_inc(z_halo, 1)
                        dve.tensor_tensor(z[:, 2:], bank[:, 5], c_sb[:], ALU.mult).then_inc(z_done, 1)
                        dve.wait_ge(z_halo, groups + (g + 1))
                        dve.wait_ge(z_done, groups + (g + 2))
                        dve.wait_ge(y_sq, ys + (2 * g + 1))
                        dve.tensor_scalar(ya[:], z[:, 2:], col("conv_w", 8 + g), None, ALU.mult).then_inc(conv0, 1)
                        dve.wait_ge(conv0, groups + (g + 1))
                        dve.scalar_tensor_tensor(ya[:], z[:, 1:SUPER + 1], col("conv_w", 4 + g), ya[:],
                                                 ALU.mult, ALU.add).then_inc(conv1, 1)
                        dve.wait_ge(conv1, groups + (g + 1))
                        dve.scalar_tensor_tensor(ya[:], z[:, 0:SUPER], col("conv_w", g), ya[:],
                                                 ALU.mult, ALU.add).then_inc(conv2, 1)
                        dve.tensor_copy(halo[:, g], z[:, SUPER:]).then_inc(halo_kept, 1)
                    if u >= 4 and which == 2:
                        dve.wait_ge(unit_used, used + (u + 1))
                        dve.wait_ge(conv2, groups + (g + 1))
                        dve.tensor_tensor(ya[:], bank[:, 6], ya[:], ALU.mult).then_inc(ya_done, 1)
                    if u >= 4 and which == 3:
                        lower_y(g, ya, ys + (2 * g + 1))
                        dve.wait_ge(s_ps, groups + (g + 2))
                        dve.wait_ge(y_sq, ys + (2 * g + 2))
                        dve.scalar_tensor_tensor(
                            yb[:].rearrange("p (t n) -> p t n", n=P), bank[:, g % 2].rearrange("p (t n) -> p t n", n=P),
                            col("g_v", g), bias[:, g].unsqueeze(1).broadcast_to((P, ST, CHUNK)),
                            ALU.mult, ALU.add).then_inc(t_done, 1)
                if not last:
                    turn_x(tiles_next, 0)
                lower_y(7, yb, ys + 8)
                n = snap(dve, i + 1)
                dve.wait_ge(ssy_ps, n + 1)
                dve.tensor_copy(ssy[:], bank[:, 0, 0:2 * ST]).then_inc(ssy_done, 1)
                dve.wait_ge(ry_done, n)
                for t in range(ST):
                    if not last:
                        if t:
                            turn_x(tiles_next, t)
                        if t < 2:
                            scale_x(tiles_next, t + 2)
                    res16 = snap(dve, (tiles + t) * 16 + 16)
                    for part in range(2):
                        k = 2 * t + part
                        dve.wait_ge(o_ps, ys + (k + 2))
                        if part == 0:
                            dve.wait_ge(res_in, res16)
                        else:
                            dve.wait_ge(o_done, ys + (k + 3))
                        pair = PAIR[k % 3]
                        dve.scalar_tensor_tensor(
                            xres[:], bank[:, pair:pair + 2].rearrange("p b n -> p (b n)"),
                            ry[:, part * ST + t:part * ST + t + 1], xres[:], ALU.mult, ALU.add).then_inc(o_done, 1)
                    if t == 2 and not last:
                        split_unit(units_next, 0)
                        split_unit(units_next, 1)

            dve.memset(halo[:], 0.0).then_inc(halo_zero, 1)
            dve.wait_ge(halo_zero, 1)
            dve.sem_inc(lo_done, 2)
            dve.sem_inc(z_done, 1)
            dve.sem_inc(ya_done, 1)
            dve.sem_inc(t_done, 2)
            dve.sem_inc(v_ss, 1)
            dve.sem_inc(halo_kept, 1)
            dve.sem_inc(hT_lo_done, 1)
            dve.sem_inc(o_done, 3)
            dve.sem_inc(x_scaled, 2)
            for t in range(ST):
                scale_x(0, t)
                if t >= 1:
                    turn_x(0, t - 1)
            turn_x(0, 3)
            dve.wait_ge(ws_turned, 1)
            dve.tensor_copy(wsT[:], bank[:, 0:2].rearrange("p b (h n) -> p (b h) n", n=CHUNK)).then_inc(ws_copied, 1)
            split_unit(0, 0)
            split_unit(0, 1)
            steps(dve, step)

        @block.tensor
        def _(pe):
            def turn_x(tiles, t):
                pe.wait_ge(x_scaled, tiles + (t + 3))
                pe.wait_ge(hT_hi_done, tiles + (t + 1))
                pe.wait_ge(hT_lo_done, tiles + (t + 1))
                for k in range(KD):
                    mm = pe.transpose(bank[:, 2 + k // 4, (k % 4) * P:(k % 4 + 1) * P],
                                      xin[:, t % 2, k * P:(k + 1) * P], keep.ident[:])
                mm.then_inc(xT_ps, 1)

            def step(i, last):
                units = snap(pe, i * UNITS)
                groups = snap(pe, i * 4)
                ys = snap(pe, i * 8)
                tiles = snap(pe, i * ST)
                tiles_next = snap(pe, i * ST + ST)
                pe.wait_ge(o_done, ys + 1)
                pe.wait_ge(hT_hi_done, tiles + (ST + 1))
                pe.wait_ge(hT_lo_done, tiles + (ST + 1))
                for u in range(UNITS):
                    pe.wait_ge(hi_done, units + (u + 3))
                    pe.wait_ge(lo_done, units + (u + 3))
                    g, which = divmod(u - 4, 4)
                    hi, lo = as_unit(w_hi, u), as_unit(w_lo, u)
                    if u < 4:
                        for kk in range(2):
                            for t in range(ST):
                                k, cols = 2 * u + kk, slice(t * P, (t + 1) * P)
                                mm = product(pe, bank[:, t], hT_hi[:, k, cols], hT_lo[:, k, cols],
                                             hi[:, kk], lo[:, kk], k == 0, k == KD - 1)
                        mm.then_inc(unit_used, 1)
                        continue
                    if u == 4:
                        pe.wait_ge(o_done, ys + 3)
                    pe.wait_ge((c_done, z_done, ya_done, u_done)[which], groups + (g + 1))
                    for k in range(KD):
                        mm = product(pe, bank[:, 4 + which], hi[:, k], lo[:, k], hT_hi[:, k], hT_lo[:, k],
                                     k == 0, k == KD - 1)
                    mm.then_inc(unit_used, 1)
                    if which == 3:
                        pe.wait_ge(v_done, tiles + ST)
                        pe.wait_ge(t_done, groups + (g + 1))
                        for t in range(ST):
                            for hh in range(2):
                                h = 2 * g + hh
                                mm = pe.matmul(bank[hh * HEAD:(hh + 1) * HEAD, g % 2, t * P:(t + 1) * P],
                                               v[:, t, h * HEAD:(h + 1) * HEAD], wsT[:, h], start=True, stop=True)
                        mm.then_inc(s_ps, 1)
                if not last:
                    turn_x(tiles_next, 0)

                def out_part(t, part):
                    cols = slice(t * P, (t + 1) * P)
                    k = 2 * t + part
                    pair = PAIR[k % 3]
                    pe.wait_ge(o_done, ys + (k + 1))
                    for c in range(4 * part, 4 * part + 4):
                        for n_half in range(2):
                            w = slice(n_half * 512, (n_half + 1) * 512)
                            mm = product(pe, bank[:, pair + n_half], yT_hi[:, c, cols], yT_lo[:, c, cols],
                                         wo_hi[:, c, w], wo_lo[:, c, w], c % 4 == 0, c % 4 == 3)
                    mm.then_inc(o_ps, 1)

                if is_first(i):
                    pe.wait_ge(wo_lo_done, KD)
                pe.wait_ge(y_hi, ys + 7)
                pe.wait_ge(y_lo, ys + 7)
                out_part(0, 0)
                pe.wait_ge(y_sum, ys + 9)
                for part, total in enumerate((sum_a, sum_b)):
                    for t in range(ST):
                        mm = pe.matmul(bank[:, 0, part * ST + t:part * ST + t + 1], total[:, t * P:(t + 1) * P],
                                       keep.ones[:, 0:1], start=True, stop=True)
                mm.then_inc(ssy_ps, 1)
                n = snap(pe, i + 1)
                pe.wait_ge(y_hi, ys + 8)
                pe.wait_ge(y_lo, ys + 8)
                out_part(0, 1)
                for t in range(1, ST):
                    if not last:
                        turn_x(tiles_next, t)
                    if t == 1:
                        pe.wait_ge(ssy_done, n)
                    for part in range(2):
                        out_part(t, part)

            pe.sem_inc(unit_used, 2)
            pe.sem_inc(xT_ps, 2)
            pe.sem_inc(s_ps, 1)
            pe.sem_inc(ssy_ps, 1)
            pe.sem_inc(o_ps, 1)
            pe.wait_ge(ws_in, 16)
            for h in range(HEADS):
                mm = pe.transpose(bank[:, h // 4, (h % 4) * P:(h % 4 + 1) * P], v[:, h // 4, (h % 4) * P:(h % 4 + 1) * P],
                                  keep.ident[:])
            mm.then_inc(ws_turned, 1)
            for t in range(ST):
                turn_x(0, t)
            pe.wait_ge(ws_copied, 1)
            pe.wait_ge(ws_masked, 1)
            steps(pe, step)


def folding(nc, keep, ins, fold):
    MT = MEM // P
    DC = XDIM // P
    with ExitStack() as ctx:
        sb = lambda n, s, d=F32: ctx.enter_context(nc.sbuf_tensor(n, s, d))
        sem = semaphores(nc, ctx)
        bank = ctx.enter_context(nc.psum_tensor("fold_ps", [P, 8, 512], F32))
        raw = sb("fold_raw", [P, 2, 2048])
        w_hi = sb("fold_w_hi", [P, 2, 2048], F32R)
        w_lo = sb("fold_w_lo", [P, 2, 2048], F32R)
        memT_hi = sb("memT_hi", [P, KD, MEM], F32R)
        memT_lo = sb("memT_lo", [P, KD, MEM], F32R)
        kT_hi, kT_lo = sb("kT_hi", [P, DC, MEM], F32R), sb("kT_lo", [P, DC, MEM], F32R)
        vT_hi, vT_lo = sb("vT_hi", [P, DC, MEM], F32R), sb("vT_lo", [P, DC, MEM], F32R)
        gain = sb("gain_mem", [P, D])
        ssm, rm, half = sb("ssm", [P, MT]), sb("rm", [P, MT]), sb("fold_half", [P, MT])

        mem_in, mem_sq, mem_ms, mem_r, mem_scaled = [sem(n) for n in (
            "mem_in", "mem_sq", "mem_ms", "mem_r", "mem_scaled")]
        mem_ps, mem_hi, mem_lo, half_set = [sem(n) for n in ("mem_ps", "mem_hi", "mem_lo", "half_set")]
        k_in, v_in, q_in, o_in = [sem(n) for n in ("k_in", "v_in", "q_in", "o_in")]
        k_hi, k_lo, v_hi, v_lo, o_hi, o_lo = [sem(n) for n in ("k_hi", "k_lo", "v_hi", "v_lo", "wo_hi_d", "wo_lo_d")]
        k_ps, q_ps, v_ps, a_ps, b_ps = [sem(n) for n in ("k_ps", "q_ps", "v_ps_f", "a_ps", "b_ps")]
        qT_h, qT_l, kT_h, kT_l, vT_h, vT_l = [sem(n) for n in ("qT_h", "qT_l", "kT_h", "kT_l", "vT_h", "vT_l")]
        a_hi, a_lo, b_hi, b_lo = [sem(n) for n in ("a_hi", "a_lo", "b_hi", "b_lo")]
        block = ctx.enter_context(nc.Block())
        col = lambda i: keep.cols[:, COLS["g_xattn"] + i:COLS["g_xattn"] + i + 1]
        mem_raw = raw[:, 1].rearrange("p (t n) -> p t n", t=MT)
        CHUNKS = (0, 1, 4, 5, 6, 7, 2, 3)

        def heads(engine, step):
            with engine.Fori(0, XHEADS - 1) as h:
                step(h, False)
            step(XHEADS - 1, True)

        @block.sync
        def _(sp):
            sp.dma_start(mem_raw, ins["mem"][0].rearrange("(t p) n -> p t n", p=P)).then_inc(mem_in, 16)
            sp.dma_start(gain[:], ins["g_mem"].broadcast_to((P, D))).then_inc(mem_in, 16)
            by_k = lambda w, h: ins[w][0, :, bass.ds(h * XDIM, XDIM)].rearrange("(k p) n -> p k n", p=P)

            def load_k(h):
                sp.dma_start(raw[:, 0].rearrange("p (k n) -> p k n", k=KD), by_k("w_k", h)).then_inc(k_in, 16)

            def load_v(h):
                sp.dma_start(raw[:, 1].rearrange("p (k n) -> p k n", k=KD), by_k("w_v", h)).then_inc(v_in, 16)

            load_k(0)
            sp.wait_ge(mem_ps, 1)
            load_v(0)

            def step(h, last):
                n = snap(sp, h + 1)
                sp.wait_ge(k_lo, n)
                sp.dma_start(raw[:, 0].rearrange("p (k n) -> p k n", k=KD), by_k("w_q", h)).then_inc(q_in, 16)
                sp.wait_ge(v_lo, n)
                sp.dma_start(raw[:, 1].rearrange("p (c n) -> p c n", c=DC),
                             ins["w_o"][0, bass.ds(h * XDIM, XDIM), :].rearrange("(c p) n -> p c n", p=P)).then_inc(o_in, 16)
                if not last:
                    sp.wait_ge(q_ps, n)
                    load_k(h + 1)
                    sp.wait_ge(o_lo, n)
                    load_v(h + 1)

            heads(sp, step)

        @block.gpsimd
        def _(pool):
            pool.memset(half[:], -0.5).then_inc(half_set, 1)
            pool.wait_ge(mem_sq, MT)
            pool.tensor_scalar(rm[:], ssm[:], 1.0 / D, EPS, ALU.mult, ALU.add).then_inc(mem_ms, 1)
            pool.wait_ge(mem_ms, 1)
            pool.wait_ge(half_set, 1)
            pool.tensor_tensor(rm[:], rm[:], half[:], ALU.pow).then_inc(mem_r, 1)

        @block.scalar
        def _(act):
            act.wait_ge(mem_in, 32)
            for t in range(MT):
                act.activation(memT_lo[:, 4 * t:4 * t + 4, :].rearrange("p k n -> p (k n)"), mem_raw[:, t], ACT.Square,
                               accum_out=ssm[:, t:t + 1]).then_inc(mem_sq, 1)
            act.wait_ge(k_in, 16)
            act.activation(w_hi[:, 0], raw[:, 0], ACT.Copy).then_inc(k_hi, 1)
            act.wait_ge(mem_ps, 1)
            act.activation(memT_hi[:], bank[:, 0:4].rearrange("p b (k n) -> p (b k) n", n=MEM), ACT.Copy).then_inc(mem_hi, 1)

            def split_k(h):
                act.wait_ge(k_in, snap(act, h * 16 + 16))
                act.wait_ge(a_ps, snap(act, h + 1))
                act.activation(w_hi[:, 0], raw[:, 0], ACT.Copy).then_inc(k_hi, 1)

            def split_v(h):
                act.wait_ge(v_in, snap(act, h * 16 + 16))
                act.wait_ge(b_ps, snap(act, h + 1))
                act.activation(w_hi[:, 1], raw[:, 1], ACT.Copy).then_inc(v_hi, 1)

            def step(h, last):
                n = snap(act, h + 1)
                n1 = snap(act, h + 2)
                n16 = snap(act, h * 16 + 16)
                act.wait_ge(k_ps, n)
                act.activation(kT_hi[:], bank[:, 4].rearrange("p (c n) -> p c n", n=MEM), ACT.Copy).then_inc(kT_h, 1)
                act.wait_ge(q_ps, n)
                act.activation(w_hi[:, 0], bank[:, 0:4].rearrange("p b n -> p (b n)"), ACT.Copy).then_inc(qT_h, 1)
                act.wait_ge(v_ps, n)
                act.activation(vT_hi[:], bank[:, 5].rearrange("p (c n) -> p c n", n=MEM), ACT.Copy).then_inc(vT_h, 1)
                act.wait_ge(o_in, n16)
                act.activation(w_hi[:, 1], raw[:, 1], ACT.Copy).then_inc(o_hi, 1)
                act.wait_ge(a_ps, n1)
                if not last:
                    split_k(h + 1)
                for i in CHUNKS:
                    mm = act.activation(fold.a_hi[:, i, bass.ds(h * MEM, MEM)], bank[:, 4 + i // 2, (i % 2) * MEM:(i % 2 + 1) * MEM],
                                        ACT.Copy, scale=col(i))
                    if i % 2:
                        mm.then_inc(a_hi, 1)
                act.wait_ge(b_ps, n1)
                act.activation(fold.b_hi[:, bass.ds(h * MT, MT), :].rearrange("p m n -> p (m n)"),
                               bank[:, 0:4].rearrange("p b n -> p (b n)"), ACT.Copy).then_inc(b_hi, 1)
                if not last:
                    split_v(h + 1)

            split_v(0)
            heads(act, step)

        @block.vector
        def _(dve):
            dve.sem_inc(a_lo, 4)
            dve.sem_inc(b_lo, 1)
            dve.wait_ge(mem_r, 1)
            dve.wait_ge(mem_in, 32)
            for t in range(MT):
                dve.scalar_tensor_tensor(mem_raw[:, t], mem_raw[:, t], rm[:, t:t + 1], gain[:],
                                         ALU.mult, ALU.mult).then_inc(mem_scaled, 1)
            dve.wait_ge(k_hi, 1)
            dve.tensor_tensor(w_lo[:, 0], raw[:, 0], f32(w_hi[:, 0]), ALU.subtract).then_inc(k_lo, 1)
            dve.wait_ge(mem_hi, 1)
            dve.tensor_tensor(memT_lo[:], bank[:, 0:4].rearrange("p b (k n) -> p (b k) n", n=MEM), f32(memT_hi[:]),
                              ALU.subtract).then_inc(mem_lo, 1)

            def low(out, of, high, after, n, done):
                dve.wait_ge(after, n)
                return dve.tensor_tensor(out, of, f32(high), ALU.subtract).then_inc(done, 1)

            def step(h, last):
                n = snap(dve, h + 1)
                low(kT_lo[:], bank[:, 4].rearrange("p (c n) -> p c n", n=MEM), kT_hi[:], kT_h, n, kT_l)
                low(w_lo[:, 0], bank[:, 0:4].rearrange("p b n -> p (b n)"), w_hi[:, 0], qT_h, n, qT_l)
                low(vT_lo[:], bank[:, 5].rearrange("p (c n) -> p c n", n=MEM), vT_hi[:], vT_h, n, vT_l)
                low(w_lo[:, 1], raw[:, 1], w_hi[:, 1], o_hi, n, o_lo)
                if not last:
                    low(w_lo[:, 0], raw[:, 0], w_hi[:, 0], k_hi, snap(dve, h + 2), k_lo)
                for at, i in enumerate(CHUNKS):
                    here = bass.ds(h * MEM, MEM)
                    if i % 2 == 0:
                        dve.wait_ge(a_hi, snap(dve, h * 4 + at // 2 + 1))
                    mm = dve.scalar_tensor_tensor(fold.a_lo[:, i, here], bank[:, 4 + i // 2, (i % 2) * MEM:(i % 2 + 1) * MEM],
                                                  col(i), f32(fold.a_hi[:, i, here]), ALU.mult, ALU.subtract)
                    if i % 2:
                        mm.then_inc(a_lo, 1)
                here = bass.ds(h * MT, MT)
                low(fold.b_lo[:, here, :].rearrange("p m n -> p (m n)"), bank[:, 0:4].rearrange("p b n -> p (b n)"),
                    fold.b_hi[:, here, :].rearrange("p m n -> p (m n)"), b_hi, n, b_lo)
                if not last:
                    low(w_lo[:, 1], raw[:, 1], w_hi[:, 1], v_hi, snap(dve, h + 2), v_lo)

            low(w_lo[:, 1], raw[:, 1], w_hi[:, 1], v_hi, 1, v_lo)
            heads(dve, step)

        @block.tensor
        def _(pe):
            pe.sem_inc(a_ps, 1)
            pe.sem_inc(b_ps, 1)
            pe.wait_ge(mem_scaled, MT)
            for k in range(KD):
                for t in range(MT):
                    c = k * MEM + t * P
                    mm = pe.transpose(bank[:, c // 512, c % 512:c % 512 + P], mem_raw[:, t, k * P:(k + 1) * P], keep.ident[:])
            mm.then_inc(mem_ps, 1)
            pe.wait_ge(mem_lo, 1)
            wide = lambda tile, b: tile[:, b].rearrange("p (k n) -> p k n", k=KD)

            def step(h, last):
                n = snap(pe, h + 1)
                n16 = snap(pe, h * 16 + 16)

                def project(b, out, ready, done):
                    pe.wait_ge(ready, n)
                    for c in range(DC):
                        for k in range(KD):
                            cols = slice(c * P, (c + 1) * P)
                            mm = product(pe, bank[:, out, c * MEM:(c + 1) * MEM], wide(w_hi, b)[:, k, cols],
                                         wide(w_lo, b)[:, k, cols], memT_hi[:, k], memT_lo[:, k], k == 0, k == KD - 1)
                    mm.then_inc(done, 1)

                pe.wait_ge(a_lo, snap(pe, h * 4 + 1))
                project(0, 4, k_lo, k_ps)
                pe.wait_ge(q_in, n16)
                pe.wait_ge(b_lo, n)
                for c in range(DC):
                    for k in range(KD):
                        mm = pe.transpose(bank[:, 2 * c + k // 4, (k % 4) * P:(k % 4 + 1) * P],
                                          wide(raw, 0)[:, k, c * P:(c + 1) * P], keep.ident[:])
                mm.then_inc(q_ps, 1)
                pe.wait_ge(a_lo, snap(pe, h * 4 + 4))
                project(1, 5, v_lo, v_ps)
                pe.wait_ge(kT_l, n)
                pe.wait_ge(qT_l, n)
                for k in CHUNKS:
                    if k == 2:
                        pe.wait_ge(vT_l, n)
                    for c in range(DC):
                        cols = slice(c * D + k * P, c * D + (k + 1) * P)
                        mm = product(pe, bank[:, 4 + k // 2, (k % 2) * MEM:(k % 2 + 1) * MEM], w_hi[:, 0, cols], w_lo[:, 0, cols],
                                     kT_hi[:, c], kT_lo[:, c], c == 0, c == DC - 1)
                mm.then_inc(a_ps, 1)
                pe.wait_ge(o_lo, n)
                for t in range(MT):
                    for nh in range(2):
                        for c in range(DC):
                            cols = slice(c * D + nh * 512, c * D + (nh + 1) * 512)
                            mm = product(pe, bank[:, 2 * t + nh], vT_hi[:, c, t * P:(t + 1) * P], vT_lo[:, c, t * P:(t + 1) * P],
                                         w_hi[:, 1, cols], w_lo[:, 1, cols], c == 0, c == DC - 1)
                mm.then_inc(b_ps, 1)

            heads(pe, step)


def xattn(nc, keep, ins, fold, x1, x2, h3):
    with ExitStack() as ctx:
        sb = lambda n, s, d=F32: ctx.enter_context(nc.sbuf_tensor(n, s, d))
        sem = semaphores(nc, ctx)
        bank = ctx.enter_context(nc.psum_tensor("att_ps", [P, 8, 512], F32))
        turned, scored, mixed, prob_ps = (bank[:, b:b + 2].rearrange("p b n -> p (b n)") for b in (0, 2, 4, 6))
        by_k = lambda ap: ap.rearrange("p (k n) -> p k n", n=P)
        xa, xb = sb("xa", [P, D]), sb("xb", [P, D])
        square = sb("att_square", [P, 2, D], BF16)
        xT_hi, xT_lo = sb("xT_hi", [P, KD, P], F32R), sb("xT_lo", [P, KD, P], F32R)
        pT_hi, pT_lo = sb("pT_hi", [P, KD, P], F32R), sb("pT_lo", [P, KD, P], F32R)
        prob = sb("prob", [P, XHEADS * MEM])
        h3_sb = sb("h3_sb", [P, D])
        h3T = sb("h3T", [P, KD, P])
        wr = sb("w_router", [P, KD, GROUPS + EXPERTS])
        ss1, rs1, ss3, r3, half = [sb(n, [P, 1]) for n in ("ss1", "rs1", "ss3", "r3", "att_half")]
        top, shift, total, inv = [sb(n, [P, XHEADS]) for n in ("top", "shift", "total", "inv")]

        wr_in, wr_ready, half_set = sem("wr_in"), sem("wr_ready"), sem("att_half_set")
        xa_in, xb_in, x2_out, h3_out = [sem(n) for n in ("xa_in", "xb_in", "x2_out", "h3_out")]
        sq1, ms1, ms1b, r1_done, sq3, ms3, r3_done = [sem(n) for n in (
            "sq1", "ms1", "ms1b", "r1_done", "sq3", "ms3", "r3_done")]
        t1_ps, xT_h, xT_l, s_ps, max_done, shift_done, exp_done, inv_done, prob_done = [sem(n) for n in (
            "t1_ps", "xT_h", "xT_l", "att_s_ps", "max_done", "shift_done", "exp_done", "inv_done", "prob_done")]
        p_ps, pT_h, pT_l, o_ps, x2_done, h3_done, t3_ps, h3T_done, l_ps, logit_done = [sem(n) for n in (
            "p_ps", "pT_h", "pT_l", "att_o_ps", "x2_done", "h3_done", "t3_ps", "h3T_done", "l_ps", "logit_done")]
        passed, sp_passed = sem("att_pool_passed"), sem("att_sp_passed")
        block = ctx.enter_context(nc.Block())
        W = GROUPS + EXPERTS

        def steps(engine, step):
            step(0)
            step(1)
            with engine.Fori(2, TILES - 1) as i:
                step(i)
            step(TILES - 1)
            step(TILES)

        def has(i, offset):
            return not isinstance(i, int) or 0 <= i + offset < TILES

        @block.sync
        def _(sp):
            sp.dma_start(wr[:, :, 0:GROUPS], ins["w_grp"][0].rearrange("(k p) n -> p k n", p=P)).then_inc(wr_in, 16)
            sp.dma_start(wr[:, :, GROUPS:], ins["w_rt"][0].rearrange("(k p) n -> p k n", p=P)).then_inc(wr_in, 16)
            sp.dma_start(xa[:], x1[0:P, :]).then_inc(xa_in, 16)

            def step(i):
                if has(i, 1):
                    row, n1, n2 = snap(sp, (i + 1) * P), snap(sp, i + 1), snap(sp, i + 2)
                    wait_apart(sp, sp_passed, (t1_ps, n1))
                    wait_apart(sp, sp_passed, (sq1, n2))
                    sp.dma_start(xa[:], x1[bass.ds(row, P), :]).then_inc(xa_in, 16)
                if has(i, -1):
                    row = snap(sp, (i - 1) * P)
                    stored = snap(sp, i * 16)
                    sp.dma_start(xb[:], x1[bass.ds(row, P), :]).then_inc(xb_in, 16)
                    sp.wait_ge(x2_done, snap(sp, i * 1))
                    sp.dma_start(x2[bass.ds(row, P), :], xb[:]).then_inc(x2_out, 16)
                    sp.wait_ge(h3_done, snap(sp, i + 1))
                    sp.dma_start(h3[bass.ds(row, P), :], h3_sb[:]).then_inc(h3_out, 16)
                    wait_apart(sp, sp_passed, (x2_out, stored))

            steps(sp, step)
            sp.wait_ge(h3_out, 16 * TILES)

        @block.gpsimd
        def _(pool):
            pool.memset(half[:], -0.5).then_inc(half_set, 1)
            pool.wait_ge(half_set, 1)

            def root1(j):
                n1, n2 = snap(pool, j + 1), snap(pool, j + 2)
                wait_apart(pool, passed, (sq1, n2), (exp_done, n1))
                pool.tensor_scalar(rs1[:], ss1[:], 1.0 / D, EPS, ALU.mult, ALU.add).then_inc(ms1, 1)
                pool.wait_ge(ms1, n2)
                pool.tensor_tensor(rs1[:], rs1[:], half[:], ALU.pow).then_inc(ms1b, 1)
                wait_apart(pool, passed, (ms1b, n1))
                pool.tensor_scalar(rs1[:], rs1[:], float(XDIM) ** -0.5, None, ALU.mult).then_inc(r1_done, 1)

            def root3(j):
                n1, n2 = snap(pool, j + 1), snap(pool, j + 2)
                wait_apart(pool, passed, (sq3, n2), (h3_done, n1))
                pool.tensor_scalar(r3[:], ss3[:], 1.0 / D, EPS, ALU.mult, ALU.add).then_inc(ms3, 1)
                pool.wait_ge(ms3, n2)
                pool.tensor_tensor(r3[:], r3[:], half[:], ALU.pow).then_inc(r3_done, 1)

            def step(i):
                if has(i, 1):
                    root1(i + 1)
                if has(i, -1):
                    root3(i - 1)

            pool.sem_inc(ms1, 1)
            pool.sem_inc(ms3, 1)
            root1(0)
            steps(pool, step)

        @block.scalar
        def _(act):
            def square1(j):
                act.wait_ge(xa_in, snap(act, j * 16 + 16))
                act.wait_ge(ms1, snap(act, j + 1))
                act.wait_ge(sq1, snap(act, j + 1))
                act.activation(square[:, 0], xa[:], ACT.Square, accum_out=ss1[:]).then_inc(sq1, 1)

            def exps(j):
                n1 = snap(act, j + 1)
                act.wait_ge(shift_done, n1)
                act.wait_ge(p_ps, n1)
                act.wait_ge(inv_done, n1)
                for h in range(XHEADS):
                    cols = slice(h * MEM, (h + 1) * MEM)
                    e = act.activation(prob[:, cols], scored[:, cols], ACT.Exp, bias=shift[:, h:h + 1], scale=rs1[:],
                                       accum_out=total[:, h:h + 1])
                e.then_inc(exp_done, 1)

            def turn1(j):
                act.wait_ge(t1_ps, snap(act, j + 1))
                act.activation(xT_hi[:], by_k(turned), ACT.Copy).then_inc(xT_h, 1)

            def step(i):
                if has(i, 1):
                    square1(i + 1)
                if has(i, 0):
                    exps(i)
                if has(i, 1):
                    turn1(i + 1)
                if has(i, -2):
                    act.wait_ge(t3_ps, snap(act, i - 1))
                    act.activation(h3T[:], by_k(prob_ps), ACT.Copy).then_inc(h3T_done, 1)
                if has(i, -1):
                    act.wait_ge(x2_done, snap(act, i * 1))
                    act.wait_ge(ms3, snap(act, i * 1))
                    act.wait_ge(sq3, snap(act, i * 1))
                    act.activation(square[:, 1], xb[:], ACT.Square, accum_out=ss3[:]).then_inc(sq3, 1)
                if has(i, 0):
                    act.wait_ge(p_ps, snap(act, i + 2))
                    act.activation(pT_hi[:], by_k(prob_ps), ACT.Copy).then_inc(pT_h, 1)

            act.sem_inc(sq1, 1)
            act.sem_inc(sq3, 1)
            act.sem_inc(exp_done, 1)
            act.sem_inc(h3T_done, 2)
            square1(0)
            turn1(0)
            steps(act, step)
            act.wait_ge(t3_ps, TILES)
            act.activation(h3T[:], by_k(prob_ps), ACT.Copy).then_inc(h3T_done, 1)

        @block.vector
        def _(dve):
            def turn1(j):
                dve.wait_ge(xT_h, snap(dve, j + 1))
                dve.tensor_tensor(xT_lo[:], by_k(turned), f32(xT_hi[:]), ALU.subtract).then_inc(xT_l, 1)

            def keep_logits(j):
                dve.wait_ge(l_ps, snap(dve, j + 1))
                dve.tensor_copy(keep.logits[:, bass.ds(j, 1), :], scored[:, 0:W].unsqueeze(1)).then_inc(logit_done, 1)

            def step(i):
                n1, n2 = snap(dve, i + 1), snap(dve, i + 2)
                if has(i, 0):
                    dve.wait_ge(s_ps, n1)
                    dve.tensor_reduce(top[:], scored.rearrange("p (h m) -> p h m", m=MEM), AX.X, ALU.max).then_inc(max_done, 1)
                    dve.wait_ge(max_done, n1)
                    dve.wait_ge(r1_done, n1)
                    dve.tensor_scalar(shift[:], top[:], rs1[:], -1.0, ALU.mult, ALU.mult).then_inc(shift_done, 1)
                if has(i, 1):
                    turn1(i + 1)
                if has(i, 0):
                    dve.wait_ge(exp_done, n2)
                    dve.reciprocal(inv[:], total[:]).then_inc(inv_done, 1)
                    dve.wait_ge(inv_done, n2)
                    heads = prob[:].rearrange("p (h m) -> p h m", m=MEM)
                    dve.tensor_tensor(heads, heads, inv[:].unsqueeze(2).broadcast_to((P, XHEADS, MEM)),
                                      ALU.mult).then_inc(prob_done, 1)
                if has(i, -1):
                    dve.wait_ge(o_ps, snap(dve, i * 1))
                    dve.wait_ge(xb_in, snap(dve, i * 16))
                    dve.tensor_tensor(xb[:], mixed, xb[:], ALU.add).then_inc(x2_done, 1)
                if has(i, -2):
                    keep_logits(i - 2)
                if has(i, 0):
                    dve.wait_ge(pT_h, n1)
                    dve.tensor_tensor(pT_lo[:], by_k(prob_ps), f32(pT_hi[:]), ALU.subtract).then_inc(pT_l, 1)
                if has(i, -1):
                    dve.wait_ge(r3_done, snap(dve, i * 1))
                    dve.wait_ge(x2_done, snap(dve, i * 1))
                    if has(i, -2):
                        dve.wait_ge(h3_out, snap(dve, i * 16 - 16))
                        dve.wait_ge(t3_ps, snap(dve, i - 1))
                    dve.tensor_scalar(h3_sb[:], xb[:], r3[:], None, ALU.mult).then_inc(h3_done, 1)

            dve.sem_inc(xT_l, 1)
            dve.sem_inc(inv_done, 1)
            dve.sem_inc(pT_l, 1)
            dve.sem_inc(h3_done, 1)
            dve.sem_inc(logit_done, 3)
            dve.wait_ge(wr_in, 32)
            gain = keep.cols[:, COLS["g_ffn"]:COLS["g_ffn"] + KD]
            dve.tensor_tensor(wr[:], wr[:], gain.unsqueeze(2).broadcast_to((P, KD, W)), ALU.mult).then_inc(wr_ready, 1)
            turn1(0)
            steps(dve, step)
            keep_logits(TILES - 1)

        @block.tensor
        def _(pe):
            def turn(out, of, done):
                for k in range(KD):
                    mm = pe.transpose(out[:, k * P:(k + 1) * P], of[:, k * P:(k + 1) * P], keep.ident[:])
                mm.then_inc(done, 1)

            def turn1(j):
                pe.wait_ge(xa_in, snap(pe, j * 16 + 16))
                pe.wait_ge(xT_l, snap(pe, j + 1))
                turn(turned, xa, t1_ps)

            def times(out, a_hi, a_lo, b_hi, b_lo, done):
                for k in range(KD):
                    for nh in range(2):
                        cols = slice(nh * 512, (nh + 1) * 512)
                        mm = product(pe, out[:, cols], a_hi[:, k], a_lo[:, k], b_hi[:, k, cols], b_lo[:, k, cols],
                                     k == 0, k == KD - 1)
                mm.then_inc(done, 1)

            def turn3(j):
                pe.wait_ge(h3_done, snap(pe, j + 2))
                pe.wait_ge(pT_l, snap(pe, j + 3) if has(j, 1) else TILES + 1)
                turn(prob_ps, h3_sb, t3_ps)

            def route(j):
                pe.wait_ge(h3T_done, snap(pe, j + 3))
                pe.wait_ge(exp_done, snap(pe, j + 4) if has(j, 2) else TILES + 1)
                for k in range(KD):
                    mm = pe.matmul(scored[:, 0:W], h3T[:, k], wr[:, k], start=(k == 0), stop=(k == KD - 1))
                mm.then_inc(l_ps, 1)

            def step(i):
                if has(i, 0):
                    pe.wait_ge(xT_l, snap(pe, i + 2))
                    pe.wait_ge(exp_done, snap(pe, i + 1))
                    pe.wait_ge(logit_done, snap(pe, i + 1))
                    times(scored, xT_hi, xT_lo, fold.a_hi, fold.a_lo, s_ps)
                if has(i, 1):
                    turn1(i + 1)
                if has(i, -2):
                    turn3(i - 2)
                if has(i, -1):
                    pe.wait_ge(pT_l, snap(pe, i + 1))
                    if has(i, -2):
                        pe.wait_ge(x2_done, snap(pe, i - 1))
                    times(mixed, pT_hi, pT_lo, fold.b_hi, fold.b_lo, o_ps)
                if has(i, -2):
                    route(i - 2)
                if has(i, 0):
                    pe.wait_ge(prob_done, snap(pe, i + 1))
                    pe.wait_ge(pT_l, snap(pe, i + 1))
                    pe.wait_ge(h3T_done, snap(pe, i + 1))
                    turn(prob_ps, prob, p_ps)

            pe.sem_inc(p_ps, 1)
            pe.wait_ge(wr_ready, 1)
            turn1(0)
            steps(pe, step)
            pe.wait_ge(logit_done, TILES + 2)
            turn3(TILES - 1)
            route(TILES - 1)


class Routed:

    ACTIVE, SECOND, NEXT, PREVIOUS, ORDER, ROW = 0, 1, 2, 3, 4, 10
    EXPERT, FOLLOWING = 0, 5

    def __init__(self, nc, ctx):
        sb = lambda n, s, d=F32: ctx.enter_context(nc.sbuf_tensor(n, s, d))
        self.tokens = sb("block_tokens", [P, LISTED], U32)
        self.rows = sb("token_rows", [P, 2, TILES], U32)
        self.gates = sb("gates", [P, 2, TILES])
        self.plan = sb("plan", [1, 2, SLOTS + 1], I32)
        self.slots = sb("active_slots", [1, 1], I32)


def routing(nc, keep, ins, routed):
    W = GROUPS + EXPERTS
    S1 = SLOTS + 1
    PAIRS = 2 * TILES
    FAR = 3.0e38
    with ExitStack() as ctx:
        sb = lambda n, s, d=F32: ctx.enter_context(nc.sbuf_tensor(n, s, d))
        sem = semaphores(nc, ctx)
        bank = ctx.enter_context(nc.psum_tensor("route_ps", [P, 8, 512], F32))
        bias = sb("router_bias", [P, W])
        logits = keep.logits
        grp = sb("grp", [P, TILES, 8])
        grp_top, grp_at = sb("grp_top", [P, TILES, 8]), sb("grp_at", [P, TILES, 8], U32)
        grp_exp, grp_sum = sb("grp_exp", [P, TILES, GROUPS]), sb("grp_sum", [P, TILES])
        grp_id = sb("grp_id", [P, TILES])
        mask, far = sb("mask", [P, TILES, GROUPS]), sb("far", [P, TILES, GROUPS])
        inside = sb("inside", [P, TILES, EXPERTS])
        exp_top, exp_at = sb("exp_top", [P, TILES, 8]), sb("exp_at", [P, TILES, 8], U32)
        ids = sb("ids", [P, 2, TILES])
        gap, ratio, den = sb("gap", [P, TILES]), sb("ratio", [P, TILES]), sb("den", [P, TILES])
        chosen = sb("chosen", [P, 2, TILES, EXPERTS])
        both = sb("both", [P, TILES, EXPERTS], BF16)
        so_far = sb("so_far", [P, 2, TILES + 1, EXPERTS], BF16)
        last = (TILES - 1).bit_length() % 2
        picked = sb("picked", [P, 2, TILES, EXPERTS])
        before, count = sb("before", [P, TILES, EXPERTS]), sb("count", [P, EXPERTS])
        count_i, slots_i = sb("count_i", [P, EXPERTS], I32), sb("slots_i", [P, EXPERTS], I32)
        slots_of = sb("slots_of", [P, EXPERTS])
        ends = sb("ends", [P, 2, EXPERTS])
        starts = sb("starts", [P, EXPERTS])
        sums = sb("count_sums", [P, 2, EXPERTS])
        row_starts, offset = sb("row_starts", [P, EXPERTS]), sb("offset", [1, EXPERTS])
        rank, base = sb("rank", [P, 2, TILES]), sb("base", [P, 2, TILES])
        rank_i, over_i = sb("rank_i", [P, 2, TILES], I32), sb("over_i", [P, 2, TILES], I32)
        over, dest = sb("over", [P, 2, TILES]), sb("dest", [P, 2, TILES])
        dest_i, part_i = sb("dest_i", [P, 2, TILES], I32), sb("part_i", [P, 2, 2, TILES], I32)
        part = sb("part", [P, 2, 2, TILES])
        place = sb("place", [P, PAIRS, P], BF16)
        blocks = sb("blocks", [P, 3, PAIRS, LISTED], BF16)
        iota_e = sb("iota_e", [P, EXPERTS])
        iota_p = sb("iota_p", [P, 1])
        iota_r = sb("iota_r", [P, P])
        iota_t = sb("iota_t", [P, PAIRS])
        earlier, ones_b = sb("earlier", [P, P], BF16), sb("ones_b", [P, P], BF16)
        list_f = sb("list_f", [P, LISTED])
        in_block = sb("in_block", [1, LISTED])
        ended = sb("ended", [1, S1, EXPERTS])
        expert_f, active_f, second_f, row_f = (sb(n, [1, S1]) for n in ("expert_f", "active_f", "second_f", "row_f"))
        order_f = sb("order_f", [1, S1])
        order = sb("order", [1, 2, S1])
        plan_f = sb("plan_f", [1, 2, S1])

        bias_in, made, chain = sem("bias_in"), sem("pool_made"), sem("route_chain")
        grp_ready, grp_exped, gap_ready, ratio_ready = [sem(n) for n in ("grp_ready", "grp_exped", "gap_ready", "ratio_ready")]
        both_ready, counted, blocks_ready, listed = [sem(n) for n in ("both_ready", "counted", "blocks_ready", "listed")]
        block = ctx.enter_context(nc.Block())

        @block.sync
        def _(sp):
            sp.dma_start(bias[:, 0:GROUPS], ins["b_grp"].broadcast_to((P, GROUPS))).then_inc(bias_in, 16)
            sp.dma_start(bias[:, GROUPS:], ins["b_rt"].broadcast_to((P, EXPERTS))).then_inc(bias_in, 16)

        @block.gpsimd
        def _(pool):
            pool.iota(iota_e[:], pattern=[[1, EXPERTS]], base=0, channel_multiplier=0,
                      allow_small_or_imprecise_dtypes=True).then_inc(made, 1)
            pool.iota(iota_p[:], pattern=[[0, 1]], base=0, channel_multiplier=1,
                      allow_small_or_imprecise_dtypes=True).then_inc(made, 1)
            pool.iota(iota_r[:], pattern=[[1, P]], base=0, channel_multiplier=0,
                      allow_small_or_imprecise_dtypes=True).then_inc(made, 1)
            pool.iota(iota_t[:], pattern=[[0, 2], [1, TILES]], base=0, channel_multiplier=0,
                      allow_small_or_imprecise_dtypes=True).then_inc(made, 1)
            pool.memset(ones_b[:], 1.0).then_inc(made, 1)
            pool.wait_ge(made, 5)
            pool.affine_select(out=earlier[:], in_=ones_b[:], compare_op=ALU.is_gt, fill=0.0, base=0,
                               pattern=[[1, P]], channel_multiplier=-1).then_inc(made, 1)

        @block.scalar
        def _(act):
            act.wait_ge(grp_ready, 1)
            act.activation(grp_exp[:], grp_exp[:], ACT.Exp).then_inc(grp_exped, 1)
            act.wait_ge(gap_ready, 1)
            act.activation(ratio[:], gap[:], ACT.Exp).then_inc(ratio_ready, 1)

        @block.tensor
        def _(pe):
            pe.wait_ge(made, 6)
            pe.wait_ge(both_ready, 1)
            flat = lambda tile: tile.rearrange("p t e -> p (t e)")
            pe.matmul(bank[:, 0], earlier[:], flat(both[:]), start=True, stop=False)
            pe.matmul(bank[:, 0], ones_b[:], flat(so_far[:, last, 0:TILES]), start=False, stop=True)
            pe.matmul(bank[:, 1, 0:EXPERTS], ones_b[:], so_far[:, last, TILES], start=True, stop=True).then_inc(counted, 1)
            pe.wait_ge(blocks_ready, 1)
            for k in range(2):
                for j in range(PAIRS):
                    pe.matmul(bank[:, 2 + k, 0:LISTED], place[:, j], blocks[:, 1 + k, j], start=(j == 0), stop=(j == PAIRS - 1))
            for j in range(PAIRS):
                mm = pe.matmul(bank[:, 4, 0:LISTED], ones_b[:], blocks[:, 0, j], start=(j == 0), stop=(j == PAIRS - 1))
            mm.then_inc(listed, 1)

        @block.vector
        def _(dve):
            steps = [0]

            def link(instruction):
                steps[0] += 1
                instruction.then_inc(chain, 1)
                dve.wait_ge(chain, steps[0])

            def copy(out, of):
                link(dve.tensor_copy(out, of))

            def running_sum(both_buffers, of, n):
                copy(both_buffers[:, 0], of)
                at, step = 0, 1
                while step < n:
                    link(dve.tensor_copy(both_buffers[:, 1 - at, 0:step], both_buffers[:, at, 0:step]))
                    link(dve.tensor_tensor(both_buffers[:, 1 - at, step:], both_buffers[:, at, step:],
                                           both_buffers[:, at, 0:n - step], ALU.add))
                    at, step = 1 - at, 2 * step
                return both_buffers[:, at]

            def bcast(ap, axis, shape):
                return ap.unsqueeze(axis).broadcast_to(shape)

            dve.wait_ge(bias_in, 32)
            link(dve.tensor_tensor(logits[:], logits[:], bcast(bias[:], 1, (P, TILES, W)), ALU.add))
            link(dve.memset(grp[:], -FAR))
            copy(grp[:, :, 0:GROUPS], logits[:, :, 0:GROUPS])
            for t in range(TILES):
                mm = dve.max(grp_top[:, t], grp[:, t])
            link(mm)
            for t in range(TILES):
                mm = dve.max_index(grp_at[:, t], grp_top[:, t], grp[:, t])
            link(mm)
            dve.tensor_tensor(grp_exp[:], logits[:, :, 0:GROUPS], grp_top[:, :, 0:1].broadcast_to((P, TILES, GROUPS)),
                              ALU.subtract).then_inc(grp_ready, 1)
            copy(grp_id[:], grp_at[:, :, 0])
            dve.wait_ge(made, 6)
            link(dve.tensor_tensor(mask[:], bcast(iota_e[:, 0:GROUPS], 1, (P, TILES, GROUPS)),
                                   bcast(grp_id[:], 2, (P, TILES, GROUPS)), ALU.is_equal))
            link(dve.tensor_scalar(far[:], mask[:], -1.0, FAR, ALU.add, ALU.mult))
            in_groups = inside[:].rearrange("p t (g e) -> p (t g) e", e=PER_GROUP)
            spread = lambda m: bcast(m[:].rearrange("p t g -> p (t g)"), 2, (P, TILES * GROUPS, PER_GROUP))
            copy(inside[:], logits[:, :, GROUPS:])
            link(dve.tensor_tensor(in_groups, in_groups, spread(mask), ALU.mult))
            link(dve.tensor_tensor(in_groups, in_groups, spread(far), ALU.add))
            for t in range(TILES):
                mm = dve.max(exp_top[:, t], inside[:, t])
            link(mm)
            for t in range(TILES):
                mm = dve.max_index(exp_at[:, t], exp_top[:, t], inside[:, t])
            link(mm)
            dve.tensor_tensor(gap[:], exp_top[:, :, 1], exp_top[:, :, 0], ALU.subtract).then_inc(gap_ready, 1)
            for c in range(2):
                copy(ids[:, c], exp_at[:, :, c])
            for c in range(2):
                link(dve.tensor_tensor(chosen[:, c], bcast(iota_e[:], 1, (P, TILES, EXPERTS)),
                                       bcast(ids[:, c], 2, (P, TILES, EXPERTS)), ALU.is_equal))
            link(dve.tensor_tensor(both[:], chosen[:, 0], chosen[:, 1], ALU.add))
            link(dve.memset(so_far[:, :, 0], 0.0))
            copy(so_far[:, 0, 1:], both[:])
            at, step = 0, 1
            while step < TILES:
                link(dve.tensor_copy(so_far[:, 1 - at, 1:step + 1], so_far[:, at, 1:step + 1]))
                added = dve.tensor_tensor(so_far[:, 1 - at, step + 1:], so_far[:, at, step + 1:],
                                          so_far[:, at, 1:TILES + 1 - step], ALU.add)
                at, step = 1 - at, 2 * step
                if step < TILES:
                    link(added)
            added.then_inc(both_ready, 1)
            dve.wait_ge(grp_exped, 1)
            link(dve.tensor_reduce(grp_sum[:], grp_exp[:], AX.X, ALU.add))
            dve.wait_ge(ratio_ready, 1)
            link(dve.tensor_scalar(den[:], ratio[:], 1.0, None, ALU.add))
            link(dve.tensor_tensor(den[:], den[:], grp_sum[:], ALU.mult))
            link(dve.reciprocal(routed.gates[:, 0], den[:]))
            link(dve.tensor_tensor(routed.gates[:, 1], routed.gates[:, 0], ratio[:], ALU.mult))

            dve.wait_ge(counted, 1)
            copy(before[:], bank[:, 0].rearrange("p (t e) -> p t e", e=EXPERTS))
            copy(count[:], bank[:, 1, 0:EXPERTS])
            link(dve.tensor_scalar(count_i[:], count[:], float(SLOT - 1), None, ALU.add))
            link(dve.tensor_scalar(slots_i[:], count_i[:], 8, None, ALU.arith_shift_right))
            copy(slots_of[:], slots_i[:])
            end = running_sum(ends, slots_of[:], EXPERTS)
            link(dve.tensor_tensor(starts[:], end, slots_of[:], ALU.subtract))
            row_end = running_sum(sums, count[:], EXPERTS)
            link(dve.tensor_tensor(row_starts[:], row_end, count[:], ALU.subtract))
            link(dve.scalar_tensor_tensor(offset[:], starts[0:1], -float(SLOT), row_starts[0:1], ALU.mult, ALU.add))
            flat2 = lambda tile: tile[:].rearrange("p c t e -> p (c t) e")
            flat_s = lambda tile: tile[:].rearrange("p c t -> p (c t)")
            for c in range(2):
                link(dve.tensor_tensor(picked[:, c], chosen[:, c], before[:], ALU.mult))
            link(dve.tensor_reduce(flat_s(rank), flat2(picked), AX.X, ALU.add))
            link(dve.tensor_tensor(flat2(picked), flat2(chosen), bcast(starts[:], 1, (P, PAIRS, EXPERTS)), ALU.mult))
            link(dve.tensor_reduce(flat_s(base), flat2(picked), AX.X, ALU.add))
            link(dve.scalar_tensor_tensor(flat_s(dest), flat_s(base), float(SLOT), flat_s(rank), ALU.mult, ALU.add))
            copy(dest_i[:], dest[:])
            link(dve.tensor_tensor(flat2(picked), flat2(chosen), bcast(row_starts[:], 1, (P, PAIRS, EXPERTS)), ALU.mult))
            link(dve.tensor_reduce(flat_s(base), flat2(picked), AX.X, ALU.add))
            link(dve.tensor_tensor(dest[:], base[:], rank[:], ALU.add))
            copy(routed.rows[:], dest[:])
            link(dve.tensor_scalar(part_i[:, 0], dest_i[:], P - 1, None, ALU.bitwise_and))
            link(dve.tensor_scalar(part_i[:, 1], dest_i[:], 7, None, ALU.arith_shift_right))
            copy(part[:], part_i[:])
            col = lambda k: part[:, k].rearrange("p c t -> p (c t)")
            link(dve.tensor_tensor(place[:], bcast(iota_r[:], 1, (P, PAIRS, P)), bcast(col(0), 2, (P, PAIRS, P)), ALU.is_equal))
            link(dve.tensor_tensor(blocks[:, 0], bcast(iota_r[:, 0:LISTED], 1, (P, PAIRS, LISTED)),
                                   bcast(col(1), 2, (P, PAIRS, LISTED)), ALU.is_equal))
            link(dve.tensor_scalar(blocks[:, 1], blocks[:, 0], iota_p[:], None, ALU.mult))
            dve.tensor_tensor(blocks[:, 2], blocks[:, 0], bcast(iota_t[:], 2, (P, PAIRS, LISTED)), ALU.mult).then_inc(blocks_ready, 1)

            slot_row = iota_r[0:1, 0:S1]
            link(dve.tensor_tensor(ended[:], bcast(end[0:1], 1, (1, S1, EXPERTS)),
                                   bcast(slot_row, 2, (1, S1, EXPERTS)), ALU.is_le))
            link(dve.tensor_reduce(expert_f[:], ended[:], AX.X, ALU.add))
            link(dve.tensor_scalar(expert_f[:], expert_f[:], float(EXPERTS - 1), None, ALU.min))
            link(dve.tensor_tensor(ended[:], bcast(expert_f[:], 2, (1, S1, EXPERTS)),
                                   bcast(iota_e[0:1], 1, (1, S1, EXPERTS)), ALU.is_equal))
            link(dve.tensor_tensor(ended[:], ended[:], bcast(offset[:], 1, (1, S1, EXPERTS)), ALU.mult))
            link(dve.tensor_reduce(row_f[:], ended[:], AX.X, ALU.add))
            link(dve.scalar_tensor_tensor(row_f[:], slot_row, float(SLOT), row_f[:], ALU.mult, ALU.add))
            dve.wait_ge(listed, 1)
            copy(list_f[:], bank[:, 3, 0:LISTED])
            link(dve.scalar_tensor_tensor(list_f[:], list_f[:], float(P), bank[:, 2, 0:LISTED], ALU.mult, ALU.add))
            copy(routed.tokens[:], list_f[:])
            copy(in_block[:], bank[0:1, 4, 0:LISTED])
            halves = in_block[:].rearrange("p (s b) -> p b s", b=2)
            link(dve.tensor_scalar(active_f[:], halves[:, 0], 0.0, None, ALU.is_gt))
            link(dve.tensor_scalar(second_f[:], halves[:, 1], 0.0, None, ALU.is_gt))
            until = running_sum(order, second_f[:], S1)
            link(dve.scalar_tensor_tensor(order_f[:], until, 1.0, second_f[:], ALU.add, ALU.subtract))
            link(dve.tensor_tensor(order_f[:, 1:], order_f[:, 1:], second_f[:, 0:S1 - 1], ALU.subtract))

            def field(word, bit, of, shift=0):
                to = plan_f[:, word, max(0, -shift):S1 - max(0, shift)]
                link(dve.scalar_tensor_tensor(to, of[:, max(0, shift):S1 - max(0, -shift)], float(1 << bit), to, ALU.mult, ALU.add))

            link(dve.memset(plan_f[:], 0.0))
            field(0, Routed.ACTIVE, active_f)
            field(0, Routed.SECOND, second_f)
            field(0, Routed.NEXT, second_f, 1)
            field(0, Routed.PREVIOUS, second_f, -1)
            field(0, Routed.ORDER, order_f)
            field(0, Routed.ROW, row_f, -1)
            field(1, Routed.EXPERT, expert_f)
            field(1, Routed.FOLLOWING, expert_f, 1)
            copy(routed.plan[:], plan_f[:])
            copy(routed.slots[:], end[0:1, EXPERTS - 1:EXPERTS])


def moe(nc, keep, ins, routed, h3, y):
    GU, DN = KD, DE // P
    UNITS = GU + DN
    RAW = UNITS
    EARLY = GU - 1
    ON_POOL = (GU + 1, GU + 3)
    LEAST = SEQ * 2 // SLOT
    w_gate, w_up, w_down = ins["w_gate"], ins["w_up"], ins["w_down"]
    with ExitStack() as ctx:
        sb = lambda n, s, d=F32: ctx.enter_context(nc.sbuf_tensor(n, s, d))
        sem = semaphores(nc, ctx)
        bank = ctx.enter_context(nc.psum_tensor("moe_ps", [P, 8, 512], F32))
        pair = lambda b: bank[:, b:b + 2].rearrange("p b n -> p (b n)")
        by_chunk = lambda ap: ap.rearrange("p (k n) -> p k n", n=P)
        raw = sb("moe_raw", [P, RAW, 1024])
        w_hi = sb("moe_w_hi", [P, UNITS, 1024], F32R)
        w_lo = sb("moe_w_lo", [P, UNITS, 1024], F32R)
        index = [sb(f"token_index_{b}", [P, 1], U32) for b in "AB"]
        tokens = [sb(f"moe_x_{b}", [P, D]) for b in "AB"]
        xT_hi = [sb(f"moe_xT_hi_{b}", [P, KD, P], F32R) for b in "AB"]
        xT_lo = [sb(f"moe_xT_lo_{b}", [P, KD, P], F32R) for b in "AB"]
        silu = [sb(f"silu_{b}", [P, DE]) for b in "AB"]
        hid = [sb(f"hidden_{b}", [P, DE]) for b in "AB"]
        hT_hi = [sb(f"hidT_hi_{b}", [P, DN, P], F32R) for b in "AB"]
        hT_lo = [sb(f"hidT_lo_{b}", [P, DN, P], F32R) for b in "AB"]
        y_sb = [sb(f"y_sb_{b}", [P, D]) for b in "AB"]

        raw_in = [sem(f"moe_raw_in{b}") for b in range(RAW)]
        hi_done, lo_dve, lo_pool = sem("moe_hi_done"), sem("moe_lo_dve"), sem("moe_lo_pool")
        gu_used, down_used = sem("gu_used"), sem("down_used")
        y_set, index_ready, pool_passed = sem("y_set"), [sem(f"index_ready_{b}") for b in "AB"], sem("moe_pool_passed")
        sp_passed = sem("moe_sp_passed")
        gathered = [sem(f"gathered_{b}") for b in "AB"]
        x_ps = [sem(f"x_ps_{b}") for b in "AB"]
        xT_h = [sem(f"moe_xT_h_{b}") for b in "AB"]
        xT_l = [sem(f"moe_xT_l_{b}") for b in "AB"]
        gu_ps, down_ps = sem("gu_ps"), sem("down_ps")
        silu_done = [sem(f"silu_done_{b}") for b in "AB"]
        hid_done = [sem(f"hid_done_{b}") for b in "AB"]
        hid_ps = [sem(f"hid_ps_{b}") for b in "AB"]
        hT_h = [sem(f"hidT_h_{b}") for b in "AB"]
        hT_l = [sem(f"hidT_l_{b}") for b in "AB"]
        y_kept = [sem(f"y_kept_{b}") for b in "AB"]
        y_out = [sem(f"y_out_{b}") for b in "AB"]
        block = ctx.enter_context(nc.Block())
        gain = lambda k: keep.cols[:, COLS["g_ffn"] + k:COLS["g_ffn"] + k + 1]
        halves = lambda ap: ap.rearrange("p (h n) -> p h n", h=2)

        def word(engine, slot, k=0):
            return engine.value_load(routed.plan[0:1, k, bass.ds(slot, 1)], min_val=0, max_val=(1 << 24) - 1)

        def field(engine, of, first, width=1):
            return snap(engine, (of >> first) & ((1 << width) - 1))

        class Blocks:

            def __init__(self, engine, plan):
                self.has_b, self.next_b, self.had_b = (
                    field(engine, plan, f) for f in (Routed.SECOND, Routed.NEXT, Routed.PREVIOUS))
                self.before = field(engine, plan, Routed.ORDER, 6)
                self.here = snap(engine, self.before + self.had_b)
                self.next = snap(engine, self.here + self.has_b)

        def steps(engine, step):
            step(0, word(engine, 0))
            with engine.Fori(1, SLOTS) as i:
                plan = word(engine, i)
                with engine.If(field(engine, plan, Routed.ACTIVE) == 1):
                    step(i, plan)

        def behind(engine):
            slots = engine.value_load(routed.slots[0:1, 0:1], min_val=LEAST, max_val=SLOTS)
            return slots, word(engine, slots)

        def staging(u):
            return (GU + u) % RAW

        def arrived(i, u):
            return i * 32 + ((GU + u) // RAW + 1) * 32

        def lows_of_dve(u):
            return sum(1 for v in range(u + 1) if v not in ON_POOL)

        def split(i, u):
            if u in ON_POOL:
                return lo_pool, i * len(ON_POOL) + (ON_POOL.index(u) + 1)
            return lo_dve, i * (UNITS - len(ON_POOL)) + (GU + lows_of_dve(u))

        @block.sync
        def _(sp):
            def load_gu(expert, k, b):
                for half, w in enumerate((w_gate, w_up)):
                    sp.dma_start(raw[:, b, half * DE:(half + 1) * DE],
                                 w[0, bass.ds(expert, 1), k * P:(k + 1) * P, :].rearrange("e p n -> (e p) n")).then_inc(raw_in[b], 16)

            def step(i, plan):
                experts = word(sp, i, 1)
                own, following = (field(sp, experts, f, 5) for f in (Routed.EXPERT, Routed.FOLLOWING))
                for u in range(UNITS):
                    if not isinstance(i, int):
                        wait_apart(sp, sp_passed, split(i - 1, u))
                    elif u >= RAW - GU:
                        sp.wait_ge(lo_dve, u - (RAW - GU) + 1)
                    if u < GU:
                        load_gu(following, u, staging(u))
                    else:
                        rows = slice((u - GU) * P, (u - GU + 1) * P)
                        for half in range(2):
                            cols = slice(half * 512, (half + 1) * 512)
                            sp.dma_start(raw[:, staging(u), cols],
                                         w_down[0, bass.ds(own, 1), rows, cols].rearrange("e p n -> (e p) n")).then_inc(raw_in[staging(u)], 16)

            first = field(sp, word(sp, 0, 1), Routed.EXPERT, 5)
            for k in range(GU):
                load_gu(first, k, k)
            steps(sp, step)

        @block.gpsimd
        def _(pool):
            def gather(slot, b, count):
                pool.tensor_copy(index[b][:], routed.tokens[:, bass.ds(slot * 2 + b, 1)]).then_inc(index_ready[b], 1)
                wait_apart(pool, pool_passed, (index_ready[b], count))
                pool.indirect_dma_start(out=tokens[b][:], out_offset=None, in_=h3[:, :],
                                        in_offset=bass.IndirectOffsetOnAxis(ap=index[b][:, :1], axis=0)).then_inc(gathered[b], 16)

            def step(i, plan):
                blocks = Blocks(pool, plan)
                next_b, b_next = blocks.next_b, blocks.next
                wait_apart(pool, pool_passed, (x_ps[0], i + 1))
                gather(i + 1, 0, i + 2)
                with pool.If(next_b == 1):
                    wait_apart(pool, pool_passed, (x_ps[1], b_next))
                    gather(i + 1, 1, b_next)
                for u in ON_POOL:
                    pool.wait_ge(hi_done, snap(pool, i * UNITS + (GU + u + 1)))
                    pool.tensor_tensor(w_lo[:, u], raw[:, staging(u)], f32(w_hi[:, u]), ALU.subtract).then_inc(lo_pool, 1)
                if not isinstance(i, int):
                    store(i, blocks, plan)

            def store(i, blocks, plan):
                row = field(pool, plan, Routed.ROW, 13).with_bounds(min_val=0, max_val=2 * SEQ)
                wait_apart(pool, pool_passed, (y_out[0], i * 16))
                wait_apart(pool, pool_passed, (y_out[1], blocks.before * 16))
                wait_apart(pool, pool_passed, (y_kept[0], i + 1))
                pool.dma_start(y[bass.ds(row, P), :], y_sb[0][:]).then_inc(y_out[0], 16)
                with pool.If(blocks.had_b == 1):
                    wait_apart(pool, pool_passed, (y_kept[1], blocks.before + 1))
                    pool.dma_start(y[bass.ds(row + P, P), :], y_sb[1][:]).then_inc(y_out[1], 16)

            for b in range(2):
                pool.memset(y_sb[b][:], 0.0).then_inc(y_set, 1)
            pool.wait_ge(y_set, 2)
            for b in range(2):
                pool.dma_start(y[2 * SEQ + b * P:2 * SEQ + (b + 1) * P, :], y_sb[b][:]).then_inc(y_out[b], 16)
            gather(0, 0, 1)
            with pool.If(field(pool, word(pool, 0), Routed.SECOND) == 1):
                gather(0, 1, 1)
            steps(pool, step)
            slots, plan = behind(pool)
            blocks = Blocks(pool, plan)
            store(slots, blocks, plan)
            wait_apart(pool, pool_passed, (y_out[0], slots * 16 + 16))
            wait_apart(pool, pool_passed, (y_out[1], blocks.here * 16))

        @block.tensor
        def _(pe):
            def turn(of, out, done):
                for k in range(of.shape[-1] // P):
                    mm = pe.transpose(out[:, k * P:(k + 1) * P], of[:, k * P:(k + 1) * P], keep.ident[:])
                mm.then_inc(done, 1)

            def gate_up(i, b, last):
                for k in range(GU):
                    if b == 0:
                        semaphore, count = (lo_dve, k + 1) if isinstance(i, int) else split(i - 1, k)
                        pe.wait_ge(semaphore, snap(pe, count))
                    for half in range(2):
                        cols = slice(half * DE, (half + 1) * DE)
                        mm = product(pe, bank[:, 2 + 2 * b + half], xT_hi[b][:, k], xT_lo[b][:, k],
                                     w_hi[:, k, cols], w_lo[:, k, cols], k == 0, k == GU - 1)
                    if last:
                        mm.then_inc(gu_used, 1)
                if not last:
                    mm.then_inc(gu_ps, 1)

            def down(i, b, last, final):
                for k in range(DN):
                    if b == 0:
                        semaphore, count = split(i - 1, GU + k) if not final else (
                            (lo_dve, i * (UNITS - len(ON_POOL)) + GU) if k % 2 == 0 else (lo_pool, i * len(ON_POOL)))
                        pe.wait_ge(semaphore, snap(pe, count))
                    for half in range(2):
                        cols = slice(half * 512, (half + 1) * 512)
                        mm = product(pe, bank[:, (0, 6)[b] + half], hT_hi[b][:, k], hT_lo[b][:, k],
                                     w_hi[:, GU + k, cols], w_lo[:, GU + k, cols], k == 0, k == DN - 1)
                    if last:
                        mm.then_inc(down_used, 1)
                if not last:
                    mm.then_inc(down_ps, 1)

            def turn_hidden(i, had_b, b_here):
                pe.wait_ge(hid_done[0], snap(pe, i * 1))
                pe.wait_ge(hid_done[1], b_here)
                turn(hid[0], bank[:, 4], hid_ps[0])
                with pe.If(had_b == 1):
                    turn(hid[1], bank[:, 5], hid_ps[1])

            def turn_tokens(slot, b_before, has_b, b_until):
                pe.wait_ge(gathered[0], snap(pe, slot * 16 + 16))
                pe.wait_ge(y_kept[1], snap(pe, b_before))
                turn(tokens[0], pair(6), x_ps[0])
                with pe.If(has_b == 1):
                    pe.wait_ge(gathered[1], snap(pe, b_until * 16))
                    pe.wait_ge(hid_done[1], snap(pe, b_until))
                    turn(tokens[1], pair(4), x_ps[1])

            def finish(i, had_b, b_done, final=False):
                pe.wait_ge(hT_l[0], snap(pe, i * 1))
                pe.wait_ge(hT_l[1], snap(pe, b_done))
                pe.wait_ge(y_kept[0], snap(pe, i * 1))
                with pe.If(had_b == 1):
                    down(i, 0, False, final)
                    if not final:
                        pe.wait_ge(xT_l[0], snap(pe, i + 2))
                    down(i, 1, True, final)
                with pe.Else():
                    down(i, 0, True, final)

            def step(i, plan):
                blocks = Blocks(pe, plan)
                has_b, b_here, b_next, b_before = blocks.has_b, blocks.here, blocks.next, blocks.before
                had_b = None if isinstance(i, int) else blocks.had_b
                pe.wait_ge(xT_l[1], b_next)
                if had_b is not None:
                    turn_hidden(i, had_b, b_here)
                    pe.wait_ge(hid_done[0], snap(pe, i * 1))
                pe.wait_ge(xT_l[0], snap(pe, i + 1))
                with pe.If(has_b == 1):
                    gate_up(i, 0, False)
                    if had_b is not None:
                        pe.wait_ge(hT_l[0], snap(pe, i * 1))
                        pe.wait_ge(hT_l[1], b_here)
                    gate_up(i, 1, True)
                with pe.Else():
                    gate_up(i, 0, True)
                if had_b is not None:
                    pe.wait_ge(hT_l[0], snap(pe, i * 1))
                    pe.wait_ge(hT_l[1], b_here)
                turn_tokens(i + 1, b_before, blocks.next_b, b_next)
                if had_b is not None:
                    finish(i, had_b, b_here)

            pe.sem_inc(x_ps[1], 1)
            turn_tokens(0, 1, field(pe, word(pe, 0), Routed.SECOND), 1)
            steps(pe, step)
            slots, plan = behind(pe)
            blocks = Blocks(pe, plan)
            turn_hidden(slots, blocks.had_b, blocks.here)
            finish(slots, blocks.had_b, blocks.here, final=True)

        @block.scalar
        def _(act):
            def high(i, u):
                b = staging(u)
                act.wait_ge(raw_in[b], snap(act, arrived(i, u)))
                if u < GU:
                    act.wait_ge(gu_used, snap(act, i * GU + (u + 1)))
                elif not isinstance(i, int):
                    act.wait_ge(down_used, snap(act, i * DN - (DN - 1 - (u - GU))))
                act.activation(w_hi[:, u], raw[:, b], ACT.Copy, scale=gain(u) if u < GU else 1.0).then_inc(hi_done, 1)

            def gate(i, b, after, count):
                act.wait_ge(after, snap(act, count))
                act.activation(silu[b][:], bank[:, 2 + 2 * b], ACT.Silu).then_inc(silu_done[b], 1)

            def turned_hidden(i, had_b, b_before):
                act.wait_ge(hid_ps[0], snap(act, i * 1))
                act.activation(hT_hi[0][:], by_chunk(bank[:, 4]), ACT.Copy).then_inc(hT_h[0], 1)
                with act.If(had_b == 1):
                    act.wait_ge(hid_ps[1], snap(act, b_before))
                    act.activation(hT_hi[1][:], by_chunk(bank[:, 5]), ACT.Copy).then_inc(hT_h[1], 1)

            def turned_tokens(slot, b, count):
                act.wait_ge(x_ps[b], snap(act, count))
                act.activation(xT_hi[b][:], by_chunk(pair((6, 4)[b])), ACT.Copy).then_inc(xT_h[b], 1)

            def turn_next(slot, next_b, b_next):
                turned_tokens(slot, 0, slot + 1)
                with act.If(next_b == 1):
                    turned_tokens(slot, 1, b_next + 1)

            def result(b, after, count, stored):
                act.wait_ge(after, snap(act, count))
                act.wait_ge(y_out[b], snap(act, stored * 16))
                act.activation(y_sb[b][:], pair((0, 6)[b]), ACT.Copy).then_inc(y_kept[b], 1)

            def results(i, blocks):
                with act.If(blocks.had_b == 1):
                    result(0, down_ps, blocks.before, i * 1)
                    result(1, down_used, i * DN, blocks.before)
                with act.Else():
                    result(0, down_used, i * DN, i * 1)

            def step(i, plan):
                blocks = Blocks(act, plan)
                has_b, b_here, had_b, b_before = blocks.has_b, blocks.here, blocks.had_b, blocks.before
                first = isinstance(i, int)
                if not first:
                    turned_hidden(i, had_b, b_before)
                with act.If(has_b == 1):
                    gate(i, 0, gu_ps, b_here)
                    for u in range(EARLY):
                        high(i, u)
                    gate(i, 1, gu_used, i * GU + GU)
                with act.Else():
                    for u in range(EARLY):
                        high(i, u)
                    gate(i, 0, gu_used, i * GU + GU)
                turn_next(i + 1, blocks.next_b, blocks.next)
                for u in range(EARLY, UNITS):
                    high(i, u)
                if not first:
                    results(i, blocks)

            act.sem_inc(y_kept[0], 1)
            act.sem_inc(y_kept[1], 1)
            turn_next(0, field(act, word(act, 0), Routed.SECOND), 1)
            for k in range(GU):
                act.wait_ge(raw_in[k], 32)
                act.activation(w_hi[:, k], raw[:, k], ACT.Copy, scale=gain(k)).then_inc(hi_done, 1)
            steps(act, step)
            slots, plan = behind(act)
            blocks = Blocks(act, plan)
            turned_hidden(slots, blocks.had_b, blocks.before)
            results(slots, blocks)

        @block.vector
        def _(dve):
            def low(i, u):
                b = staging(u)
                if u not in ON_POOL:
                    dve.wait_ge(hi_done, snap(dve, i * UNITS + (GU + u + 1)))
                    if u < GU:
                        dve.scalar_tensor_tensor(w_lo[:, u], raw[:, b], gain(u), f32(w_hi[:, u]),
                                                 ALU.mult, ALU.subtract).then_inc(lo_dve, 1)
                    else:
                        dve.tensor_tensor(w_lo[:, u], raw[:, b], f32(w_hi[:, u]), ALU.subtract).then_inc(lo_dve, 1)

            def gated(i, b, silu_count):
                dve.wait_ge(silu_done[b], snap(dve, silu_count))
                if b == 0:
                    if not isinstance(i, int):
                        dve.wait_ge(hid_ps[0], snap(dve, i * 1))
                dve.tensor_tensor(hid[b][:], silu[b][:], bank[:, 3 + 2 * b], ALU.mult).then_inc(hid_done[b], 1)

            def turned_hidden(i, had_b, b_before):
                dve.wait_ge(hT_h[0], snap(dve, i * 1))
                dve.tensor_tensor(hT_lo[0][:], by_chunk(bank[:, 4]), f32(hT_hi[0][:]), ALU.subtract).then_inc(hT_l[0], 1)
                with dve.If(had_b == 1):
                    dve.wait_ge(hT_h[1], snap(dve, b_before))
                    dve.tensor_tensor(hT_lo[1][:], by_chunk(bank[:, 5]), f32(hT_hi[1][:]), ALU.subtract).then_inc(hT_l[1], 1)

            def turned_tokens(slot, b, count):
                dve.wait_ge(xT_h[b], snap(dve, count))
                dve.tensor_tensor(xT_lo[b][:], by_chunk(pair((6, 4)[b])), f32(xT_hi[b][:]), ALU.subtract).then_inc(xT_l[b], 1)

            def turn_next(slot, next_b, b_next):
                turned_tokens(slot, 0, slot + 1)
                with dve.If(next_b == 1):
                    turned_tokens(slot, 1, b_next)

            def step(i, plan):
                blocks = Blocks(dve, plan)
                has_b, b_here, had_b, b_before = blocks.has_b, blocks.here, blocks.had_b, blocks.before
                first = isinstance(i, int)
                if not first:
                    turned_hidden(i, had_b, b_before)
                with dve.If(has_b == 1):
                    gated(i, 0, i + 1)
                    for u in range(EARLY):
                        low(i, u)
                    gated(i, 1, b_here)
                with dve.Else():
                    for u in range(EARLY):
                        low(i, u)
                    gated(i, 0, i + 1)
                turn_next(i + 1, blocks.next_b, blocks.next)
                for u in range(EARLY, UNITS):
                    low(i, u)

            dve.sem_inc(hid_done[1], 1)
            dve.sem_inc(hT_l[1], 1)
            dve.sem_inc(xT_l[1], 1)
            turn_next(0, field(dve, word(dve, 0), Routed.SECOND), 1)
            for k in range(GU):
                dve.wait_ge(hi_done, k + 1)
                dve.scalar_tensor_tensor(w_lo[:, k], raw[:, k], gain(k), f32(w_hi[:, k]),
                                         ALU.mult, ALU.subtract).then_inc(lo_dve, 1)
            steps(dve, step)
            slots, plan = behind(dve)
            blocks = Blocks(dve, plan)
            turned_hidden(slots, blocks.had_b, blocks.before)


def combine(nc, keep, ins, routed, x2, y, out):
    with ExitStack() as ctx:
        sb = lambda n, s, d=F32: ctx.enter_context(nc.sbuf_tensor(n, s, d))
        sem = semaphores(nc, ctx)
        index = [[sb(f"row_index{b}{c}", [P, 1], U32) for c in range(2)] for b in range(2)]
        ys = [[sb(f"y_row{b}{c}", [P, D]) for c in range(2)] for b in range(2)]
        xs = [sb(f"x_tile{b}", [P, D]) for b in range(2)]
        outs = [sb(f"out_tile{b}", [P, D]) for b in range(2)]
        square = sb("final_square", [P, D], BF16)
        gain = sb("gain_final", [P, D])
        ss, r, half = sb("final_ss", [P, 2]), sb("final_r", [P, 2]), sb("final_half", [P, 1])
        gain_in, half_set, passed = sem("gain_in"), sem("final_half_set"), sem("final_pool_passed")
        x_in = [sem(f"final_x_in{b}") for b in range(2)]
        y_in = [sem(f"final_y_in{b}") for b in range(2)]
        stored = [sem(f"final_stored{b}") for b in range(2)]
        index_ready, added, summed, squared = [sem(n) for n in ("row_index_ready", "added", "summed", "squared")]
        mean_ready, root_ready, scaled = sem("mean_ready"), sem("root_ready"), sem("scaled")
        block = ctx.enter_context(nc.Block())

        def steps(engine, step):
            step(0)
            with engine.Fori(1, TILES // 2 - 1) as j:
                step(j)
            step(TILES // 2 - 1)

        def is_last(j):
            return isinstance(j, int) and j == TILES // 2 - 1

        def is_first(j):
            return isinstance(j, int) and j == 0

        @block.sync
        def _(sp):
            def load(j, b):
                row = snap(sp, j * 2 * P + b * P)
                sp.dma_start(xs[b][:], x2[bass.ds(row, P), :]).then_inc(x_in[b], 16)

            def step(j):
                for b in range(2):
                    row = snap(sp, j * 2 * P + b * P)
                    sp.wait_ge(scaled, snap(sp, j * 2 + (b + 1)))
                    sp.dma_start(out[0, bass.ds(row, P), :], outs[b][:]).then_inc(stored[b], 16)
                    if not is_last(j):
                        load(j + 1, b)

            for b in range(2):
                load(0, b)
            sp.dma_start(gain[:], ins["g_final"].unsqueeze(0).broadcast_to((P, D))).then_inc(gain_in, 16)
            steps(sp, step)
            for b in range(2):
                sp.wait_ge(stored[b], 16 * (TILES // 2))

        @block.gpsimd
        def _(pool):
            def gather(j, b):
                for c in range(2):
                    pool.tensor_copy(index[b][c][:], routed.rows[:, c, bass.ds(j * 2 + b, 1)]).then_inc(index_ready, 1)
                wait_apart(pool, passed, (index_ready, j * 4 + (2 * b + 2)))
                for c in range(2):
                    pool.indirect_dma_start(out=ys[b][c][:], out_offset=None, in_=y[:, :],
                                            in_offset=bass.IndirectOffsetOnAxis(ap=index[b][c][:, :1], axis=0)).then_inc(y_in[b], 16)

            def step(j):
                for b in range(2):
                    n = j * 2 + (b + 1)
                    if not is_last(j):
                        wait_apart(pool, passed, (summed, n))
                        gather(j + 1, b)
                    wait_apart(pool, passed, (squared, n))
                    if not is_first(j):
                        wait_apart(pool, passed, (scaled, n - 2))
                    pool.tensor_scalar(r[:, b:b + 1], ss[:, b:b + 1], 1.0 / D, EPS, ALU.mult, ALU.add).then_inc(mean_ready, 1)
                    pool.wait_ge(mean_ready, snap(pool, n))
                    pool.tensor_tensor(r[:, b:b + 1], r[:, b:b + 1], half[:], ALU.pow).then_inc(root_ready, 1)

            pool.memset(half[:], -0.5).then_inc(half_set, 1)
            pool.wait_ge(half_set, 1)
            for b in range(2):
                gather(0, b)
            steps(pool, step)

        @block.scalar
        def _(act):
            def step(j):
                for b in range(2):
                    n = j * 2 + (b + 1)
                    act.wait_ge(summed, snap(act, n))
                    if not (is_first(j) and b == 0):
                        act.wait_ge(squared, snap(act, n - 1))
                    if not is_first(j):
                        act.wait_ge(mean_ready, snap(act, n - 2))
                    act.activation(square[:], xs[b][:], ACT.Square, accum_out=ss[:, b:b + 1]).then_inc(squared, 1)

            steps(act, step)

        @block.vector
        def _(dve):
            def step(j):
                for b in range(2):
                    n = j * 2 + (b + 1)
                    gate = lambda c: routed.gates[:, c, bass.ds(j * 2 + b, 1)]
                    dve.wait_ge(x_in[b], snap(dve, j * 16 + 16))
                    dve.wait_ge(y_in[b], snap(dve, j * 32 + 32))
                    dve.scalar_tensor_tensor(xs[b][:], ys[b][0][:], gate(0), xs[b][:], ALU.mult, ALU.add).then_inc(added, 1)
                    dve.wait_ge(added, snap(dve, n))
                    dve.scalar_tensor_tensor(xs[b][:], ys[b][1][:], gate(1), xs[b][:], ALU.mult, ALU.add).then_inc(summed, 1)
                for b in range(2):
                    n = j * 2 + (b + 1)
                    dve.wait_ge(summed, snap(dve, n))
                    dve.wait_ge(root_ready, snap(dve, n))
                    if not is_first(j):
                        dve.wait_ge(stored[b], snap(dve, j * 16))
                    dve.scalar_tensor_tensor(outs[b][:], xs[b][:], r[:, b:b + 1], gain[:], ALU.mult, ALU.mult).then_inc(scaled, 1)

            dve.wait_ge(gain_in, 16)
            steps(dve, step)


def hybrid_layer_kernel(nc, out, **ins):
    dram = lambda name, rows: nc.dram_tensor(name, (rows, D), F32, kind="Internal").ap()
    x1, x2, h3 = dram("x1", SEQ), dram("x2", SEQ), dram("h3", SEQ)
    y = dram("y_rows", 2 * SEQ + SLOT)
    with ExitStack() as ctx:
        keep = Kept(nc, ctx)
        setup(nc, keep, ins)
        mixer(nc, keep, ins, x1)
        with Fold(nc) as fold:
            folding(nc, keep, ins, fold)
            xattn(nc, keep, ins, fold, x1, x2, h3)
        routed = Routed(nc, ctx)
        routing(nc, keep, ins, routed)
        moe(nc, keep, ins, routed, h3, y)
        combine(nc, keep, ins, routed, x2, y, out)


_INS = ["x", "mem", "g_mix", "w_in", "conv_w", "g_v", "w_s", "b_s", "g_out_conv", "g_out_gmlp", "w_out",
        "g_xattn", "g_mem", "w_q", "w_k", "w_v", "w_o", "g_ffn", "w_grp", "b_grp", "w_rt", "b_rt",
        "w_gate", "w_up", "w_down", "g_final"]


def kernel(**inputs):
    import numpy as _np
    import concourse.bacc as _bacc
    from concourse import mybir as _mybir
    from concourse.bass_utils import run_bass_kernel_spmd as _run

    nc = _bacc.Bacc("TRN2", target_bir_lowering=False, num_devices=1)
    arrays, args = {}, {}
    for name in _INS:
        a = _np.ascontiguousarray(inputs[name])
        arrays[f"in_{name}_dram"] = a
        args[name] = nc.dram_tensor(f"in_{name}_dram", a.shape, _mybir.dt.from_np(a.dtype), kind="ExternalInput").ap()
    out = nc.dram_tensor("out_0_dram", (1, SEQ, D), F32, kind="ExternalOutput").ap()
    hybrid_layer_kernel(nc, out, **args)
    r = _run(nc, [arrays], core_ids=[0])
    return r.results[0]["out_0_dram"]
```

```python
from contextlib import ExitStack

import concourse.bass as bass
import concourse.mybir as mybir

F32 = mybir.dt.float32
F32R = mybir.dt.float32r
BF16 = mybir.dt.bfloat16
I32 = mybir.dt.int32
U32 = mybir.dt.uint32
ALU = mybir.AluOpType
ACT = mybir.ActivationFunctionType
AX = mybir.AxisListType

P = 128
D = 1024
KD = D // P
SEQ = 2048
TILES = SEQ // P
CONV = 512
GMLP = 512
HEADS = 8
HEAD = GMLP // HEADS
CHUNK = 128
CONV_K = 3
MEM = 256
XHEADS = 4
XDIM = D // XHEADS
GROUPS = 4
PER_GROUP = 8
EXPERTS = GROUPS * PER_GROUP
DE = 512
EPS = 1e-6

SUPER = 512
SUPERS = SEQ // SUPER
ST = SUPER // P

SLOT = 2 * P
SLOTS = SEQ * 2 // SLOT + EXPERTS - 1
LISTED = 2 * (SLOTS + 1)

COLS = {}
at = 0
for name, n in (("g_mix", 8), ("g_out_conv", 4), ("g_out_gmlp", 4), ("g_xattn", 8), ("g_ffn", 8),
                ("g_v", 4), ("conv_w", 12)):
    COLS[name] = at
    at += n
GAIN_ROWS = at


def f32(ap):
    return ap.bitcast(F32)


def snap(engine, value):
    return value if isinstance(value, int) else engine.snap(value)


def semaphores(nc, ctx):
    made = []
    ctx.callback(nc.all_engine_barrier)
    ctx.callback(lambda: nc.clear_and_free_semaphores(made))

    def make(name):
        made.append(nc.alloc_semaphore(name))
        return made[-1]
    return make


def wait_apart(engine, passed, *waits):
    waits = [(semaphore, snap(engine, value)) for semaphore, value in waits]
    for semaphore, value in waits:
        engine.wait_ge(semaphore, value)
    engine.sem_inc(passed, 1)


def product(pe, out, ahi, alo, bhi, blo, first, last):
    pe.matmul(out, ahi, bhi, start=first, stop=False)
    pe.matmul(out, ahi, blo, start=False, stop=False)
    return pe.matmul(out, alo, bhi, start=False, stop=last)


class Kept:

    def __init__(self, nc, ctx):
        sb = lambda n, s, d=F32: ctx.enter_context(nc.sbuf_tensor(n, s, d))
        self.ident = sb("ident", [P, P])
        self.ones = sb("ones", [P, 2])
        self.cols = sb("gain_cols", [P, GAIN_ROWS])
        self.logits = sb("logits", [P, TILES, GROUPS + EXPERTS])
        self.bias = sb("router_bias", [P, GROUPS + EXPERTS])


class Fold:

    def __init__(self, nc):
        self.nc, self.ctx = nc, ExitStack()

    def __enter__(self):
        sb = lambda n: self.ctx.enter_context(self.nc.sbuf_tensor(n, [P, KD, XHEADS * MEM], F32R))
        self.a_hi, self.a_lo, self.b_hi, self.b_lo = (sb(n) for n in ("A_hi", "A_lo", "B_hi", "B_lo"))
        return self

    def __exit__(self, *exc):
        self.ctx.close()


def mixer(nc, keep, ins, x1):
    UNITS = 4 + 4 * 4
    FIRST_WO = 4
    PAIR = (4, 6, 0)
    w_in, w_out, x = ins["w_in"], ins["w_out"], ins["x"]
    col = lambda name, k: keep.cols[:, COLS[name] + k:COLS[name] + k + 1]
    with ExitStack() as ctx:
        sb = lambda n, s, d=F32: ctx.enter_context(nc.sbuf_tensor(n, s, d))
        sem = semaphores(nc, ctx)
        bank = ctx.enter_context(nc.psum_tensor("mix_ps", [P, 8, 512], F32))

        wo_hi = sb("wo_hi", [P, KD, D], F32R)
        wo_lo = sb("wo_lo", [P, KD, D], F32R)
        w_raw = sb("w_raw", [P, 2, 1024])
        w_hi = sb("w_hi", [P, 2, 1024], F32R)
        w_lo = sb("w_lo", [P, 2, 1024], F32R)
        xin = sb("xin", [P, 2, D])
        gain = sb("gain_mix", [P, D])
        square = sb("square_out", [P, D], BF16)
        hT_hi = sb("hT_hi", [P, KD, SUPER], F32R)
        hT_lo = sb("hT_lo", [P, KD, SUPER], F32R)
        yT_hi = sb("yT_hi", [P, KD, SUPER], F32R)
        yT_lo = sb("yT_lo", [P, KD, SUPER], F32R)
        v = sb("v", [P, ST, GMLP])
        wsT = sb("wsT", [P, HEADS, CHUNK])
        bias = sb("b_s_rows", [P, HEADS // 2, CHUNK])
        c_sb = sb("c_sb", [P, SUPER])
        z = sb("z", [P, SUPER + CONV_K - 1])
        halo = sb("halo", [P, 4, CONV_K - 1])
        ya = sb("ya", [P, SUPER])
        u_sb = sb("u_sb", [P, SUPER])
        yb = sb("yb", [P, SUPER])
        sq = sb("sq", [P, SUPER])
        sum_a = sb("sum_a", [P, SUPER])
        sum_b = sb("sum_b", [P, SUPER])
        xres = sb("xres", [P, D])
        ssx = sb("ssx", [P, 2])
        rx = sb("rx", [P, 2])
        ssv = sb("ssv", [P, ST, HEADS])
        rv = sb("rv", [P, ST, HEADS])
        ssy = sb("ssy", [P, 2 * ST])
        ry = sb("ry", [P, 2 * ST])
        half = sb("neg_half", [P, HEADS])
        rows = sb("gain_rows", [GAIN_ROWS, P])

        rows_in, bias_in, gain_in = sem("gain_rows_in"), sem("router_bias_in"), sem("g_mix_in")
        zeroed, ident_ready = sem("ident_zeroed"), sem("ident_ready")
        gains_turned, gains_kept = sem("gains_turned"), sem("gains_kept")
        wo_in, wo_hi_done, wo_lo_done = sem("wo_in"), sem("wo_hi_done"), sem("wo_lo_done")
        raw_in = [sem(f"w_raw_in{b}") for b in range(2)]
        hi_done, lo_done, unit_used = sem("w_hi_done"), sem("w_lo_done"), sem("w_unit_used")
        ws_in, ws_turned, ws_copied, ws_masked = sem("ws_in"), sem("ws_turned"), sem("ws_copied"), sem("ws_masked")
        pool_passed, sp_passed = sem("pool_passed"), sem("sp_passed")
        const_in, pool_const, halo_zero = sem("const_in"), sem("pool_const"), sem("halo_zero")
        x_in = [sem(f"x_in{b}") for b in range(2)]
        x_sq, x_ms, x_r, x_scaled = sem("x_sq"), sem("x_ms"), sem("x_r"), sem("x_scaled")
        xT_ps, hT_hi_done, hT_lo_done = sem("xT_ps"), sem("hT_hi_done"), sem("hT_lo_done")
        v_gelu, v_sq, v_ss, v_ms, v_r, v_done = [sem(n) for n in (
            "v_gelu", "v_sq", "v_ss", "v_ms", "v_r", "v_done")]
        c_done, z_halo, z_done, conv0, conv1, conv2, ya_done = [sem(n) for n in (
            "c_done", "z_halo", "z_done", "conv0", "conv1", "conv2", "ya_done")]
        u_done, s_ps, t_done, yb_done, halo_kept = [sem(n) for n in (
            "u_done", "s_ps", "t_done", "yb_done", "halo_kept")]
        y_hi, y_lo, y_sq, y_sum = [sem(n) for n in ("y_hi", "y_lo", "y_sq", "y_sum")]
        ssy_ps, ssy_done, ry_ms, ry_done = [sem(n) for n in ("ssy_ps", "ssy_done", "ry_ms", "ry_done")]
        o_ps, o_done, res_in, x1_out = [sem(n) for n in ("o_ps", "o_done", "res_in", "x1_out")]
        block = ctx.enter_context(nc.Block())

        def unit_source(u):
            if u < 4:
                return w_in[0, 2 * u * P:(2 * u + 2) * P, 3 * CONV + GMLP:].rearrange("(k p) n -> p k n", p=P)
            g, which = divmod(u - 4, 4)
            start = {0: CONV, 1: 2 * CONV, 2: 0, 3: 3 * CONV}[which] + g * P
            return w_in[0, :, start:start + P].rearrange("(k p) n -> p k n", p=P)

        def as_unit(tile, u):
            return tile[:, u % 2].rearrange("p (k n) -> p k n", k=2 if u < 4 else KD)

        def steps(engine, step):
            step(0, False)
            with engine.Fori(1, SUPERS - 1) as i:
                step(i, False)
            step(SUPERS - 1, True)

        def is_first(i):
            return isinstance(i, int) and i == 0

        @block.sync
        def _(sp):
            def load_x(tiles, t):
                row = snap(sp, (tiles + t) * P)
                sp.wait_ge(xT_ps, tiles + t + 1)
                sp.dma_start(xin[:, t % 2], x[0, bass.ds(row, P), :]).then_inc(x_in[t % 2], 16)

            def load_unit(units, u):
                sp.wait_ge(hi_done, units + (u + 1))
                sp.wait_ge(lo_done, units + (u + 1))
                sp.dma_start(as_unit(w_raw, u), unit_source(u)).then_inc(raw_in[u % 2], 16)

            def step(i, last):
                units = snap(sp, i * UNITS)
                units_next = snap(sp, i * UNITS + UNITS)
                tiles = snap(sp, i * ST)
                tiles_next = snap(sp, i * ST + ST)
                for u in range(2, UNITS):
                    load_unit(units, u)
                    if u == 10 and not last:
                        load_x(tiles_next, 0)
                        load_x(tiles_next, 1)
                    k = u - FIRST_WO - 2
                    if is_first(i) and 0 <= k < KD:
                        if k:
                            sp.wait_ge(wo_lo_done, k)
                        sp.dma_start(xres[:], w_out[0, k * P:(k + 1) * P, :]).then_inc(wo_in, 16)
                if is_first(i):
                    sp.wait_ge(wo_lo_done, KD)
                for t in range(ST):
                    row = snap(sp, (tiles + t) * P)
                    sp.dma_start(xres[:], x[0, bass.ds(row, P), :]).then_inc(res_in, 16)
                    if t < 2 and not last:
                        load_x(tiles_next, t + 2)
                    if t == 2 and not last:
                        load_unit(units_next, 0)
                        load_unit(units_next, 1)
                    done = snap(sp, (tiles + t) * 16 + 16)
                    both = snap(sp, (tiles + t) * 2 + 5)
                    sp.wait_ge(o_done, both)
                    sp.dma_start(x1[bass.ds(row, P), :], xres[:]).then_inc(x1_out, 16)
                    wait_apart(sp, sp_passed, (x1_out, done))

            load_x(0, 0)
            load_x(0, 1)
            sp.dma_start(gain[:], ins["g_mix"].broadcast_to((P, D))).then_inc(gain_in, 16)
            load_x(0, 2)
            load_x(0, 3)
            sp.dma_start(v[:, 0:2, :].rearrange("p a (h s) -> p (a h) s", s=CHUNK),
                         ins["w_s"][0].rearrange("h t s -> t h s")).then_inc(ws_in, 16)
            load_unit(0, 0)
            load_unit(0, 1)
            for name in COLS:
                n = ins[name].shape[1] // P if name != "conv_w" else CONV_K * CONV // P
                src = ins[name].rearrange("a (k p) -> (a k) p", p=P) if name != "conv_w" else \
                    ins[name].rearrange("a j (k p) -> (a j k) p", p=P)
                sp.dma_start(rows[COLS[name]:COLS[name] + n, :], src).then_inc(rows_in, 16)
            for h in range(HEADS):
                sp.dma_start(bias[(h % 2) * HEAD:(h % 2 + 1) * HEAD, h // 2, :],
                             ins["b_s"][0, h:h + 1, :].broadcast_to((HEAD, CHUNK))).then_inc(const_in, 16)
            sp.dma_start(keep.bias[:, 0:GROUPS], ins["b_grp"].broadcast_to((P, GROUPS))).then_inc(bias_in, 16)
            sp.dma_start(keep.bias[:, GROUPS:], ins["b_rt"].broadcast_to((P, EXPERTS))).then_inc(bias_in, 16)
            sp.wait_ge(bias_in, 32)
            steps(sp, step)

        @block.gpsimd
        def _(pool):
            def inverse_root(ss, out, n, ready, ms, done, k, ahead=0):
                wait_apart(pool, pool_passed, (ready, k + ahead))
                pool.tensor_scalar(out, ss, 1.0 / n, EPS, ALU.mult, ALU.add).then_inc(ms, 1)
                pool.wait_ge(ms, k)
                pool.tensor_tensor(out, out, half[:, 0:out.shape[-1]], ALU.pow).then_inc(done, 1)

            def norm_x(tiles, t):
                pool.wait_ge(x_scaled, tiles + (t + 1))
                inverse_root(ssx[:, t % 2:t % 2 + 1], rx[:, t % 2:t % 2 + 1], D, x_sq, x_ms, x_r, tiles + (t + 1), 1)

            def add_square(target, k, first):
                wait_apart(pool, pool_passed, (y_sum, k), (y_sq, k + 2))
                if first:
                    pool.tensor_copy(target, sq[:]).then_inc(y_sum, 1)
                else:
                    pool.tensor_tensor(target, target, sq[:], ALU.add).then_inc(y_sum, 1)

            def step(i, last):
                groups = snap(pool, i * 4)
                ys = snap(pool, i * 8)
                tiles = snap(pool, i * ST)
                tiles_next = snap(pool, i * ST + ST)
                for t in range(ST):
                    inverse_root(ssv[:, t], rv[:, t], HEAD, v_ss, v_ms, v_r, tiles + (t + 1), 1)
                pool.wait_ge(ssy_ps, snap(pool, i + 1))
                for g in range(4):
                    if g == 3 and not last:
                        norm_x(tiles_next, 0)
                        norm_x(tiles_next, 1)
                    add_square(sum_a[:], ys + (2 * g + 1), g == 0)
                    pool.wait_ge(u_done, groups + (g + 2))
                    pool.wait_ge(t_done, groups + (g + 3))
                    pool.tensor_tensor(yb[:], yb[:], u_sb[:], ALU.mult).then_inc(yb_done, 1)
                    add_square(sum_b[:], ys + (2 * g + 2), g == 0)
                n = snap(pool, i + 1)
                inverse_root(ssy[:], ry[:], CONV, ssy_done, ry_ms, ry_done, n)
                if not last:
                    norm_x(tiles_next, 2)
                    norm_x(tiles_next, 3)

            pool.memset(half[:], -0.5).then_inc(pool_const, 1)
            pool.memset(keep.ident[:], 0.0).then_inc(zeroed, 1)
            pool.memset(keep.ones[:], 1.0).then_inc(zeroed, 1)
            pool.wait_ge(zeroed, 1)
            pool.affine_select(out=keep.ident[:], in_=keep.ident[:], compare_op=ALU.not_equal, fill=1.0,
                               base=0, pattern=[[-1, P]], channel_multiplier=1).then_inc(ident_ready, 1)
            pool.wait_ge(pool_const, 1)
            pool.sem_inc(y_sum, 1)
            pool.sem_inc(yb_done, 1)
            pool.sem_inc(x_r, 2)
            for t in range(ST):
                norm_x(0, t)
            pool.wait_ge(ws_copied, 1)
            pool.affine_select(out=wsT[:], in_=wsT[:], compare_op=ALU.is_ge, fill=0.0, base=0,
                               pattern=[[0, HEADS], [1, CHUNK]], channel_multiplier=-1).then_inc(ws_masked, 1)
            steps(pool, step)

        @block.scalar
        def _(act):
            def split_raw(out, uses16, u, k):
                act.wait_ge(raw_in[u % 2], uses16)
                act.activation(out, w_raw[:, u % 2], ACT.Copy).then_inc(hi_done, 1)

            def split_unit(units, uses16, u):
                act.wait_ge(unit_used, units + (u + 1))
                split_raw(w_hi[:, u % 2], uses16 + 16 * (u // 2 + 1), u, None)

            def square_x(tiles, halves16, t):
                act.wait_ge(x_in[t % 2], halves16 + 16 * (t // 2 + 1))
                act.wait_ge(x_r, tiles + (t + 1))
                act.wait_ge(x_sq, tiles + (t + 1))
                act.activation(square[:], xin[:, t % 2], ACT.Square,
                               accum_out=ssx[:, t % 2:t % 2 + 1]).then_inc(x_sq, 1)

            def turn_x(tiles, t):
                act.wait_ge(xT_ps, tiles + (t + 3))
                act.activation(hT_hi[:, :, t * P:(t + 1) * P],
                               bank[:, 2:4, :].rearrange("p b (k n) -> p (b k) n", n=P), ACT.Copy).then_inc(hT_hi_done, 1)

            def keep_y(chunk, tile, ready, k_ready, y_index):
                act.wait_ge(ready, k_ready)
                act.activation(yT_hi[:, chunk], tile[:], ACT.Copy).then_inc(y_hi, 1)
                act.wait_ge(y_sum, y_index + 1)
                act.activation(sq[:], tile[:], ACT.Square).then_inc(y_sq, 1)

            def step(i, last):
                units = snap(act, i * UNITS)
                units_next = snap(act, i * UNITS + UNITS)
                uses = snap(act, i * (UNITS * 8))
                uses_next = snap(act, i * (UNITS * 8) + UNITS * 8)
                groups = snap(act, i * 4)
                ys = snap(act, i * 8)
                tiles = snap(act, i * ST)
                tiles_next = snap(act, i * ST + ST)
                halves_next = snap(act, (i + 1) * (ST * 8))
                used = snap(act, i * UNITS + 2)
                for u in range(UNITS):
                    g, which = divmod(u - 4, 4)
                    if u + 2 < UNITS:
                        split_unit(units, uses, u + 2)
                    k = u - FIRST_WO
                    if is_first(i) and 0 <= k < KD:
                        gain_col = col("g_out_conv", k) if k < 4 else col("g_out_gmlp", k - 4)
                        if k == 0:
                            act.wait_ge(gains_kept, 1)
                        act.wait_ge(wo_in, 16 * (k + 1))
                        act.activation(wo_hi[:, k], xres[:], ACT.Copy, scale=gain_col).then_inc(wo_hi_done, 1)
                    if u == 14 and not last:
                        square_x(tiles_next, halves_next, 0)
                        square_x(tiles_next, halves_next, 1)
                    if u == 3:
                        act.wait_ge(s_ps, groups + 1)
                        for t in range(ST):
                            act.wait_ge(unit_used, used + (u + 1))
                            act.activation(v[:, t], bank[:, t], ACT.Gelu_apprx_tanh).then_inc(v_gelu, 1)
                    if u >= 4 and which == 0:
                        act.wait_ge(unit_used, used + (u + 1))
                        act.wait_ge(z_done, groups + (g + 1))
                        act.activation(c_sb[:], bank[:, 4], ACT.Copy).then_inc(c_done, 1)
                        if g:
                            keep_y(4 + g - 1, yb, yb_done, groups + (g + 1), ys + (2 * g - 1))
                    if u >= 4 and which == 3:
                        act.wait_ge(unit_used, used + (u + 1))
                        act.wait_ge(yb_done, groups + (g + 1))
                        act.activation(u_sb[:], bank[:, 7], ACT.Gelu_apprx_tanh).then_inc(u_done, 1)
                        if g == 0:
                            act.wait_ge(o_ps, ys + 1)
                        keep_y(g, ya, ya_done, groups + (g + 2), ys + 2 * g)
                keep_y(7, yb, yb_done, groups + 5, ys + 7)
                if not last:
                    for t in range(ST):
                        turn_x(tiles_next, t)
                        if t < 2:
                            square_x(tiles_next, halves_next, t + 2)
                        if t == 2:
                            split_unit(units_next, uses_next, 0)
                            split_unit(units_next, uses_next, 1)

            act.sem_inc(x_sq, 1)
            act.sem_inc(y_sq, 2)
            act.sem_inc(hi_done, 2)
            act.sem_inc(c_done, 1)
            act.sem_inc(u_done, 1)
            act.sem_inc(hT_hi_done, 1)
            for t in range(ST):
                square_x(0, 0, t)
                if t >= 1:
                    turn_x(0, t - 1)
            turn_x(0, 3)
            split_unit(0, 0, 0)
            split_unit(0, 0, 1)
            steps(act, step)

        @block.vector
        def _(dve):
            def split_unit(units, u):
                dve.wait_ge(hi_done, units + (u + 3))
                dve.wait_ge(unit_used, units + (u + 1))
                dve.tensor_tensor(w_lo[:, u % 2], w_raw[:, u % 2], f32(w_hi[:, u % 2]), ALU.subtract).then_inc(lo_done, 1)

            def scale_x(tiles, t):
                dve.wait_ge(x_r, tiles + (t + 3))
                if t == 0:
                    dve.wait_ge(gain_in, 16)
                dve.scalar_tensor_tensor(xin[:, t % 2], xin[:, t % 2], rx[:, t % 2:t % 2 + 1], gain[:],
                                         ALU.mult, ALU.mult).then_inc(x_scaled, 1)

            def turn_x(tiles, t):
                dve.wait_ge(hT_hi_done, tiles + (t + 2))
                cols = slice(t * P, (t + 1) * P)
                dve.tensor_tensor(hT_lo[:, :, cols], bank[:, 2:4, :].rearrange("p b (k n) -> p (b k) n", n=P),
                                  f32(hT_hi[:, :, cols]), ALU.subtract).then_inc(hT_lo_done, 1)

            def lower_y(chunk, tile, k):
                dve.wait_ge(y_hi, k)
                dve.tensor_tensor(yT_lo[:, chunk], tile[:], f32(yT_hi[:, chunk]), ALU.subtract).then_inc(y_lo, 1)

            def step(i, last):
                units = snap(dve, i * UNITS)
                units_next = snap(dve, i * UNITS + UNITS)
                used = snap(dve, i * UNITS + 2)
                groups = snap(dve, i * 4)
                ys = snap(dve, i * 8)
                tiles = snap(dve, i * ST)
                tiles_next = snap(dve, i * ST + ST)
                for u in range(UNITS):
                    g, which = divmod(u - 4, 4)
                    if u + 2 < UNITS:
                        split_unit(units, u + 2)
                    k = u - FIRST_WO
                    if is_first(i) and 0 <= k < KD:
                        gain_col = col("g_out_conv", k) if k < 4 else col("g_out_gmlp", k - 4)
                        if k == 0:
                            dve.wait_ge(gains_kept, 1)
                        dve.wait_ge(wo_hi_done, k + 1)
                        dve.scalar_tensor_tensor(wo_lo[:, k], xres[:], gain_col, f32(wo_hi[:, k]),
                                                 ALU.mult, ALU.subtract).then_inc(wo_lo_done, 1)
                    if u == 16 and not last:
                        scale_x(tiles_next, 0)
                        scale_x(tiles_next, 1)
                    if u == 3:
                        for t in range(ST):
                            dve.wait_ge(v_gelu, tiles + (t + 1))
                            dve.wait_ge(v_ss, tiles + (t + 1))
                            dve.tensor_tensor(z[:, 0:GMLP], v[:, t], v[:, t], ALU.mult).then_inc(v_sq, 1)
                            dve.wait_ge(v_sq, tiles + (t + 1))
                            dve.tensor_reduce(ssv[:, t], z[:, 0:GMLP].rearrange("p (h d) -> p h d", d=HEAD),
                                              AX.X, ALU.add).then_inc(v_ss, 1)
                    if u == 4:
                        for t in range(ST):
                            dve.wait_ge(v_r, tiles + (t + 1))
                            heads = v[:, t].rearrange("p (h d) -> p h d", d=HEAD)
                            dve.tensor_tensor(heads, heads, rv[:, t].unsqueeze(2).broadcast_to((P, HEADS, HEAD)),
                                              ALU.mult).then_inc(v_done, 1)
                        dve.wait_ge(v_ss, tiles + (ST + 1))
                    if u >= 8 and which == 0:
                        lower_y(4 + g - 1, yb, ys + 2 * g)
                    if u >= 4 and which == 1:
                        dve.wait_ge(unit_used, used + (u + 1))
                        dve.wait_ge(c_done, groups + (g + 2))
                        dve.wait_ge(halo_kept, groups + (g + 1))
                        dve.tensor_copy(z[:, 0:2], halo[:, g]).then_inc(z_halo, 1)
                        dve.tensor_tensor(z[:, 2:], bank[:, 5], c_sb[:], ALU.mult).then_inc(z_done, 1)
                        dve.wait_ge(z_halo, groups + (g + 1))
                        dve.wait_ge(z_done, groups + (g + 2))
                        dve.wait_ge(y_sq, ys + (2 * g + 1))
                        dve.tensor_scalar(ya[:], z[:, 2:], col("conv_w", 8 + g), None, ALU.mult).then_inc(conv0, 1)
                        dve.wait_ge(conv0, groups + (g + 1))
                        dve.scalar_tensor_tensor(ya[:], z[:, 1:SUPER + 1], col("conv_w", 4 + g), ya[:],
                                                 ALU.mult, ALU.add).then_inc(conv1, 1)
                        dve.wait_ge(conv1, groups + (g + 1))
                        dve.scalar_tensor_tensor(ya[:], z[:, 0:SUPER], col("conv_w", g), ya[:],
                                                 ALU.mult, ALU.add).then_inc(conv2, 1)
                        dve.tensor_copy(halo[:, g], z[:, SUPER:]).then_inc(halo_kept, 1)
                    if u >= 4 and which == 2:
                        dve.wait_ge(unit_used, used + (u + 1))
                        dve.wait_ge(conv2, groups + (g + 1))
                        dve.tensor_tensor(ya[:], bank[:, 6], ya[:], ALU.mult).then_inc(ya_done, 1)
                    if u >= 4 and which == 3:
                        if is_first(i) and g == 0:
                            dve.wait_ge(const_in, 16 * HEADS)
                        lower_y(g, ya, ys + (2 * g + 1))
                        dve.wait_ge(s_ps, groups + (g + 2))
                        dve.wait_ge(y_sq, ys + (2 * g + 2))
                        dve.scalar_tensor_tensor(
                            yb[:].rearrange("p (t n) -> p t n", n=P), bank[:, g % 2].rearrange("p (t n) -> p t n", n=P),
                            col("g_v", g), bias[:, g].unsqueeze(1).broadcast_to((P, ST, CHUNK)),
                            ALU.mult, ALU.add).then_inc(t_done, 1)
                if not last:
                    turn_x(tiles_next, 0)
                lower_y(7, yb, ys + 8)
                n = snap(dve, i + 1)
                dve.wait_ge(ssy_ps, n + 1)
                dve.tensor_copy(ssy[:], bank[:, 0, 0:2 * ST]).then_inc(ssy_done, 1)
                dve.wait_ge(ry_done, n)
                for t in range(ST):
                    if not last:
                        if t:
                            turn_x(tiles_next, t)
                        if t < 2:
                            scale_x(tiles_next, t + 2)
                    res16 = snap(dve, (tiles + t) * 16 + 16)
                    for part in range(2):
                        k = 2 * t + part
                        dve.wait_ge(o_ps, ys + (k + 2))
                        if part == 0:
                            dve.wait_ge(res_in, res16)
                        else:
                            dve.wait_ge(o_done, ys + (k + 3))
                        pair = PAIR[k % 3]
                        dve.scalar_tensor_tensor(
                            xres[:], bank[:, pair:pair + 2].rearrange("p b n -> p (b n)"),
                            ry[:, part * ST + t:part * ST + t + 1], xres[:], ALU.mult, ALU.add).then_inc(o_done, 1)
                    if t == 2 and not last:
                        split_unit(units_next, 0)
                        split_unit(units_next, 1)

            dve.memset(halo[:], 0.0).then_inc(halo_zero, 1)
            dve.wait_ge(halo_zero, 1)
            dve.sem_inc(lo_done, 2)
            dve.sem_inc(z_done, 1)
            dve.sem_inc(ya_done, 1)
            dve.sem_inc(t_done, 2)
            dve.sem_inc(v_ss, 1)
            dve.sem_inc(halo_kept, 1)
            dve.sem_inc(hT_lo_done, 1)
            dve.sem_inc(o_done, 3)
            dve.sem_inc(x_scaled, 2)
            for t in range(ST):
                scale_x(0, t)
                if t >= 1:
                    turn_x(0, t - 1)
            turn_x(0, 3)
            dve.wait_ge(ws_turned, 1)
            dve.tensor_copy(wsT[:], bank[:, 0:2].rearrange("p b (h n) -> p (b h) n", n=CHUNK)).then_inc(ws_copied, 1)
            dve.wait_ge(gains_turned, 1)
            dve.tensor_copy(keep.cols[:], bank[:, 7, 0:GAIN_ROWS]).then_inc(gains_kept, 1)
            split_unit(0, 0)
            split_unit(0, 1)
            steps(dve, step)

        @block.tensor
        def _(pe):
            def turn_x(tiles, t):
                pe.wait_ge(x_scaled, tiles + (t + 3))
                pe.wait_ge(hT_hi_done, tiles + (t + 1))
                pe.wait_ge(hT_lo_done, tiles + (t + 1))
                for k in range(KD):
                    mm = pe.transpose(bank[:, 2 + k // 4, (k % 4) * P:(k % 4 + 1) * P],
                                      xin[:, t % 2, k * P:(k + 1) * P], keep.ident[:])
                mm.then_inc(xT_ps, 1)

            def step(i, last):
                units = snap(pe, i * UNITS)
                groups = snap(pe, i * 4)
                ys = snap(pe, i * 8)
                tiles = snap(pe, i * ST)
                tiles_next = snap(pe, i * ST + ST)
                pe.wait_ge(o_done, ys + 1)
                pe.wait_ge(hT_hi_done, tiles + (ST + 1))
                pe.wait_ge(hT_lo_done, tiles + (ST + 1))
                for u in range(UNITS):
                    pe.wait_ge(hi_done, units + (u + 3))
                    pe.wait_ge(lo_done, units + (u + 3))
                    g, which = divmod(u - 4, 4)
                    hi, lo = as_unit(w_hi, u), as_unit(w_lo, u)
                    if u < 4:
                        for kk in range(2):
                            for t in range(ST):
                                k, cols = 2 * u + kk, slice(t * P, (t + 1) * P)
                                mm = product(pe, bank[:, t], hT_hi[:, k, cols], hT_lo[:, k, cols],
                                             hi[:, kk], lo[:, kk], k == 0, k == KD - 1)
                        mm.then_inc(unit_used, 1)
                        continue
                    if u == 4:
                        pe.wait_ge(o_done, ys + 3)
                    pe.wait_ge((c_done, z_done, ya_done, u_done)[which], groups + (g + 1))
                    for k in range(KD):
                        mm = product(pe, bank[:, 4 + which], hi[:, k], lo[:, k], hT_hi[:, k], hT_lo[:, k],
                                     k == 0, k == KD - 1)
                    mm.then_inc(unit_used, 1)
                    if which == 3:
                        pe.wait_ge(v_done, tiles + ST)
                        pe.wait_ge(t_done, groups + (g + 1))
                        for t in range(ST):
                            for hh in range(2):
                                h = 2 * g + hh
                                mm = pe.matmul(bank[hh * HEAD:(hh + 1) * HEAD, g % 2, t * P:(t + 1) * P],
                                               v[:, t, h * HEAD:(h + 1) * HEAD], wsT[:, h], start=True, stop=True)
                        mm.then_inc(s_ps, 1)
                if not last:
                    turn_x(tiles_next, 0)

                def out_part(t, part):
                    cols = slice(t * P, (t + 1) * P)
                    k = 2 * t + part
                    pair = PAIR[k % 3]
                    pe.wait_ge(o_done, ys + (k + 1))
                    for c in range(4 * part, 4 * part + 4):
                        for n_half in range(2):
                            w = slice(n_half * 512, (n_half + 1) * 512)
                            mm = product(pe, bank[:, pair + n_half], yT_hi[:, c, cols], yT_lo[:, c, cols],
                                         wo_hi[:, c, w], wo_lo[:, c, w], c % 4 == 0, c % 4 == 3)
                    mm.then_inc(o_ps, 1)

                if is_first(i):
                    pe.wait_ge(wo_lo_done, KD)
                pe.wait_ge(y_hi, ys + 7)
                pe.wait_ge(y_lo, ys + 7)
                out_part(0, 0)
                pe.wait_ge(y_sum, ys + 9)
                for part, total in enumerate((sum_a, sum_b)):
                    for t in range(ST):
                        mm = pe.matmul(bank[:, 0, part * ST + t:part * ST + t + 1], total[:, t * P:(t + 1) * P],
                                       keep.ones[:, 0:1], start=True, stop=True)
                mm.then_inc(ssy_ps, 1)
                n = snap(pe, i + 1)
                pe.wait_ge(y_hi, ys + 8)
                pe.wait_ge(y_lo, ys + 8)
                out_part(0, 1)
                for t in range(1, ST):
                    if not last:
                        turn_x(tiles_next, t)
                    if t == 1:
                        pe.wait_ge(ssy_done, n)
                    for part in range(2):
                        out_part(t, part)

            pe.sem_inc(unit_used, 2)
            pe.sem_inc(xT_ps, 2)
            pe.sem_inc(s_ps, 1)
            pe.sem_inc(ssy_ps, 1)
            pe.sem_inc(o_ps, 1)
            pe.wait_ge(ident_ready, 1)
            pe.wait_ge(zeroed, 2)
            for t in range(ST):
                turn_x(0, t)
            pe.wait_ge(ws_in, 16)
            for h in range(HEADS):
                mm = pe.transpose(bank[:, h // 4, (h % 4) * P:(h % 4 + 1) * P], v[:, h // 4, (h % 4) * P:(h % 4 + 1) * P],
                                  keep.ident[:])
            mm.then_inc(ws_turned, 1)
            pe.wait_ge(rows_in, 16 * len(COLS))
            pe.transpose(bank[:, 7, 0:GAIN_ROWS], rows[:], keep.ident[0:GAIN_ROWS, 0:GAIN_ROWS]).then_inc(gains_turned, 1)
            pe.wait_ge(gains_kept, 1)
            pe.wait_ge(ws_copied, 1)
            pe.wait_ge(ws_masked, 1)
            steps(pe, step)


def folding(nc, keep, ins, fold):
    MT = MEM // P
    DC = XDIM // P
    with ExitStack() as ctx:
        sb = lambda n, s, d=F32: ctx.enter_context(nc.sbuf_tensor(n, s, d))
        sem = semaphores(nc, ctx)
        bank = ctx.enter_context(nc.psum_tensor("fold_ps", [P, 8, 512], F32))
        raw = sb("fold_raw", [P, 2, 2048])
        w_hi = sb("fold_w_hi", [P, 2, 2048], F32R)
        w_lo = sb("fold_w_lo", [P, 2, 2048], F32R)
        memT_hi = sb("memT_hi", [P, KD, MEM], F32R)
        memT_lo = sb("memT_lo", [P, KD, MEM], F32R)
        kT_hi, kT_lo = sb("kT_hi", [P, DC, MEM], F32R), sb("kT_lo", [P, DC, MEM], F32R)
        vT_hi, vT_lo = sb("vT_hi", [P, DC, MEM], F32R), sb("vT_lo", [P, DC, MEM], F32R)
        gain = sb("gain_mem", [P, D])
        ssm, rm, half = sb("ssm", [P, MT]), sb("rm", [P, MT]), sb("fold_half", [P, MT])

        mem_in, gain_mem_in = [sem(f"mem_in{t}") for t in range(MT)], sem("g_mem_in")
        mem_sq, mem_ms, mem_r, mem_scaled = [sem(n) for n in (
            "mem_sq", "mem_ms", "mem_r", "mem_scaled")]
        mem_ps, mem_hi, mem_lo, half_set = [sem(n) for n in ("mem_ps", "mem_hi", "mem_lo", "half_set")]
        k_in, v_in, q_in, o_in = [sem(n) for n in ("k_in", "v_in", "q_in", "o_in")]
        k_hi, k_lo, v_hi, v_lo, o_hi, o_lo = [sem(n) for n in ("k_hi", "k_lo", "v_hi", "v_lo", "wo_hi_d", "wo_lo_d")]
        k_ps, q_ps, v_ps, a_ps, b_ps = [sem(n) for n in ("k_ps", "q_ps", "v_ps_f", "a_ps", "b_ps")]
        qT_h, qT_l, kT_h, kT_l, vT_h, vT_l = [sem(n) for n in ("qT_h", "qT_l", "kT_h", "kT_l", "vT_h", "vT_l")]
        a_hi, a_lo, b_hi, b_lo = [sem(n) for n in ("a_hi", "a_lo", "b_hi", "b_lo")]
        block = ctx.enter_context(nc.Block())
        col = lambda i: keep.cols[:, COLS["g_xattn"] + i:COLS["g_xattn"] + i + 1]
        mem_raw = raw[:, 1].rearrange("p (t n) -> p t n", t=MT)
        CHUNKS = (0, 1, 4, 5, 6, 7, 2, 3)

        def heads(engine, step):
            with engine.Fori(0, XHEADS - 1) as h:
                step(h, False)
            step(XHEADS - 1, True)

        @block.sync
        def _(sp):
            for t in range(MT):
                sp.dma_start(mem_raw[:, t], ins["mem"][0, t * P:(t + 1) * P, :]).then_inc(mem_in[t], 16)
            sp.dma_start(gain[:], ins["g_mem"].broadcast_to((P, D))).then_inc(gain_mem_in, 16)
            by_k = lambda w, h: ins[w][0, :, bass.ds(h * XDIM, XDIM)].rearrange("(k p) n -> p k n", p=P)

            def load_k(h):
                sp.dma_start(raw[:, 0].rearrange("p (k n) -> p k n", k=KD), by_k("w_k", h)).then_inc(k_in, 16)

            def load_v(h):
                sp.dma_start(raw[:, 1].rearrange("p (k n) -> p k n", k=KD), by_k("w_v", h)).then_inc(v_in, 16)

            load_k(0)
            sp.wait_ge(mem_ps, 1)
            load_v(0)

            def step(h, last):
                n = snap(sp, h + 1)
                sp.wait_ge(k_lo, n)
                sp.dma_start(raw[:, 0].rearrange("p (k n) -> p k n", k=KD), by_k("w_q", h)).then_inc(q_in, 16)
                sp.wait_ge(v_lo, n)
                sp.dma_start(raw[:, 1].rearrange("p (c n) -> p c n", c=DC),
                             ins["w_o"][0, bass.ds(h * XDIM, XDIM), :].rearrange("(c p) n -> p c n", p=P)).then_inc(o_in, 16)
                if not last:
                    sp.wait_ge(q_ps, n)
                    load_k(h + 1)
                    sp.wait_ge(o_lo, n)
                    load_v(h + 1)

            heads(sp, step)

        @block.gpsimd
        def _(pool):
            pool.memset(half[:], -0.5).then_inc(half_set, 1)
            pool.wait_ge(mem_sq, MT)
            pool.tensor_scalar(rm[:], ssm[:], 1.0 / D, EPS, ALU.mult, ALU.add).then_inc(mem_ms, 1)
            pool.wait_ge(mem_ms, 1)
            pool.wait_ge(half_set, 1)
            pool.tensor_tensor(rm[:], rm[:], half[:], ALU.pow).then_inc(mem_r, 1)

        @block.scalar
        def _(act):
            for t in range(MT):
                act.wait_ge(mem_in[t], 16)
                act.activation(memT_lo[:, 4 * t:4 * t + 4, :].rearrange("p k n -> p (k n)"), mem_raw[:, t], ACT.Square,
                               accum_out=ssm[:, t:t + 1]).then_inc(mem_sq, 1)
            act.wait_ge(k_in, 16)
            act.activation(w_hi[:, 0], raw[:, 0], ACT.Copy).then_inc(k_hi, 1)
            act.wait_ge(mem_ps, 1)
            act.activation(memT_hi[:], bank[:, 0:4].rearrange("p b (k n) -> p (b k) n", n=MEM), ACT.Copy).then_inc(mem_hi, 1)

            def split_k(h):
                act.wait_ge(k_in, snap(act, h * 16 + 16))
                act.wait_ge(a_ps, snap(act, h + 1))
                act.activation(w_hi[:, 0], raw[:, 0], ACT.Copy).then_inc(k_hi, 1)

            def split_v(h):
                act.wait_ge(v_in, snap(act, h * 16 + 16))
                act.wait_ge(b_ps, snap(act, h + 1))
                act.activation(w_hi[:, 1], raw[:, 1], ACT.Copy).then_inc(v_hi, 1)

            def step(h, last):
                n = snap(act, h + 1)
                n1 = snap(act, h + 2)
                n16 = snap(act, h * 16 + 16)
                act.wait_ge(k_ps, n)
                act.activation(kT_hi[:], bank[:, 4].rearrange("p (c n) -> p c n", n=MEM), ACT.Copy).then_inc(kT_h, 1)
                act.wait_ge(q_ps, n)
                act.activation(w_hi[:, 0], bank[:, 0:4].rearrange("p b n -> p (b n)"), ACT.Copy).then_inc(qT_h, 1)
                act.wait_ge(v_ps, n)
                act.activation(vT_hi[:], bank[:, 5].rearrange("p (c n) -> p c n", n=MEM), ACT.Copy).then_inc(vT_h, 1)
                act.wait_ge(o_in, n16)
                act.activation(w_hi[:, 1], raw[:, 1], ACT.Copy).then_inc(o_hi, 1)
                act.wait_ge(a_ps, n1)
                if not last:
                    split_k(h + 1)
                for i in CHUNKS:
                    mm = act.activation(fold.a_hi[:, i, bass.ds(h * MEM, MEM)], bank[:, 4 + i // 2, (i % 2) * MEM:(i % 2 + 1) * MEM],
                                        ACT.Copy, scale=col(i))
                    if i % 2:
                        mm.then_inc(a_hi, 1)
                act.wait_ge(b_ps, n1)
                act.activation(fold.b_hi[:, bass.ds(h * MT, MT), :].rearrange("p m n -> p (m n)"),
                               bank[:, 0:4].rearrange("p b n -> p (b n)"), ACT.Copy).then_inc(b_hi, 1)
                if not last:
                    split_v(h + 1)

            split_v(0)
            heads(act, step)

        @block.vector
        def _(dve):
            dve.sem_inc(a_lo, 4)
            dve.sem_inc(b_lo, 1)
            dve.wait_ge(mem_r, 1)
            dve.wait_ge(gain_mem_in, 16)
            for t in range(MT):
                dve.scalar_tensor_tensor(mem_raw[:, t], mem_raw[:, t], rm[:, t:t + 1], gain[:],
                                         ALU.mult, ALU.mult).then_inc(mem_scaled, 1)
            dve.wait_ge(k_hi, 1)
            dve.tensor_tensor(w_lo[:, 0], raw[:, 0], f32(w_hi[:, 0]), ALU.subtract).then_inc(k_lo, 1)
            dve.wait_ge(mem_hi, 1)
            dve.tensor_tensor(memT_lo[:], bank[:, 0:4].rearrange("p b (k n) -> p (b k) n", n=MEM), f32(memT_hi[:]),
                              ALU.subtract).then_inc(mem_lo, 1)

            def low(out, of, high, after, n, done):
                dve.wait_ge(after, n)
                return dve.tensor_tensor(out, of, f32(high), ALU.subtract).then_inc(done, 1)

            def step(h, last):
                n = snap(dve, h + 1)
                low(kT_lo[:], bank[:, 4].rearrange("p (c n) -> p c n", n=MEM), kT_hi[:], kT_h, n, kT_l)
                low(w_lo[:, 0], bank[:, 0:4].rearrange("p b n -> p (b n)"), w_hi[:, 0], qT_h, n, qT_l)
                low(vT_lo[:], bank[:, 5].rearrange("p (c n) -> p c n", n=MEM), vT_hi[:], vT_h, n, vT_l)
                low(w_lo[:, 1], raw[:, 1], w_hi[:, 1], o_hi, n, o_lo)
                if not last:
                    low(w_lo[:, 0], raw[:, 0], w_hi[:, 0], k_hi, snap(dve, h + 2), k_lo)
                for at, i in enumerate(CHUNKS):
                    here = bass.ds(h * MEM, MEM)
                    if i % 2 == 0:
                        dve.wait_ge(a_hi, snap(dve, h * 4 + at // 2 + 1))
                    mm = dve.scalar_tensor_tensor(fold.a_lo[:, i, here], bank[:, 4 + i // 2, (i % 2) * MEM:(i % 2 + 1) * MEM],
                                                  col(i), f32(fold.a_hi[:, i, here]), ALU.mult, ALU.subtract)
                    if i % 2:
                        mm.then_inc(a_lo, 1)
                here = bass.ds(h * MT, MT)
                low(fold.b_lo[:, here, :].rearrange("p m n -> p (m n)"), bank[:, 0:4].rearrange("p b n -> p (b n)"),
                    fold.b_hi[:, here, :].rearrange("p m n -> p (m n)"), b_hi, n, b_lo)
                if not last:
                    low(w_lo[:, 1], raw[:, 1], w_hi[:, 1], v_hi, snap(dve, h + 2), v_lo)

            low(w_lo[:, 1], raw[:, 1], w_hi[:, 1], v_hi, 1, v_lo)
            heads(dve, step)

        @block.tensor
        def _(pe):
            pe.sem_inc(a_ps, 1)
            pe.sem_inc(b_ps, 1)
            pe.wait_ge(mem_scaled, MT)
            for k in range(KD):
                for t in range(MT):
                    c = k * MEM + t * P
                    mm = pe.transpose(bank[:, c // 512, c % 512:c % 512 + P], mem_raw[:, t, k * P:(k + 1) * P], keep.ident[:])
            mm.then_inc(mem_ps, 1)
            pe.wait_ge(mem_lo, 1)
            wide = lambda tile, b: tile[:, b].rearrange("p (k n) -> p k n", k=KD)

            def step(h, last):
                n = snap(pe, h + 1)
                n16 = snap(pe, h * 16 + 16)

                def project(b, out, ready, done):
                    pe.wait_ge(ready, n)
                    for c in range(DC):
                        for k in range(KD):
                            cols = slice(c * P, (c + 1) * P)
                            mm = product(pe, bank[:, out, c * MEM:(c + 1) * MEM], wide(w_hi, b)[:, k, cols],
                                         wide(w_lo, b)[:, k, cols], memT_hi[:, k], memT_lo[:, k], k == 0, k == KD - 1)
                    mm.then_inc(done, 1)

                pe.wait_ge(a_lo, snap(pe, h * 4 + 1))
                project(0, 4, k_lo, k_ps)
                pe.wait_ge(q_in, n16)
                pe.wait_ge(b_lo, n)
                for c in range(DC):
                    for k in range(KD):
                        mm = pe.transpose(bank[:, 2 * c + k // 4, (k % 4) * P:(k % 4 + 1) * P],
                                          wide(raw, 0)[:, k, c * P:(c + 1) * P], keep.ident[:])
                mm.then_inc(q_ps, 1)
                pe.wait_ge(a_lo, snap(pe, h * 4 + 4))
                project(1, 5, v_lo, v_ps)
                pe.wait_ge(kT_l, n)
                pe.wait_ge(qT_l, n)
                for k in CHUNKS:
                    if k == 2:
                        pe.wait_ge(vT_l, n)
                    for c in range(DC):
                        cols = slice(c * D + k * P, c * D + (k + 1) * P)
                        mm = product(pe, bank[:, 4 + k // 2, (k % 2) * MEM:(k % 2 + 1) * MEM], w_hi[:, 0, cols], w_lo[:, 0, cols],
                                     kT_hi[:, c], kT_lo[:, c], c == 0, c == DC - 1)
                mm.then_inc(a_ps, 1)
                pe.wait_ge(o_lo, n)
                for t in range(MT):
                    for nh in range(2):
                        for c in range(DC):
                            cols = slice(c * D + nh * 512, c * D + (nh + 1) * 512)
                            mm = product(pe, bank[:, 2 * t + nh], vT_hi[:, c, t * P:(t + 1) * P], vT_lo[:, c, t * P:(t + 1) * P],
                                         w_hi[:, 1, cols], w_lo[:, 1, cols], c == 0, c == DC - 1)
                mm.then_inc(b_ps, 1)

            heads(pe, step)


def xattn(nc, keep, ins, fold, x1, x2, h3):
    with ExitStack() as ctx:
        sb = lambda n, s, d=F32: ctx.enter_context(nc.sbuf_tensor(n, s, d))
        sem = semaphores(nc, ctx)
        bank = ctx.enter_context(nc.psum_tensor("att_ps", [P, 8, 512], F32))
        turned, scored, mixed, prob_ps = (bank[:, b:b + 2].rearrange("p b n -> p (b n)") for b in (0, 2, 4, 6))
        by_k = lambda ap: ap.rearrange("p (k n) -> p k n", n=P)
        xa, xb = sb("xa", [P, D]), sb("xb", [P, D])
        square = sb("att_square", [P, 2, D], BF16)
        xT_hi, xT_lo = sb("xT_hi", [P, KD, P], F32R), sb("xT_lo", [P, KD, P], F32R)
        pT_hi, pT_lo = sb("pT_hi", [P, KD, P], F32R), sb("pT_lo", [P, KD, P], F32R)
        prob = sb("prob", [P, XHEADS * MEM])
        h3_sb = sb("h3_sb", [P, D])
        h3T = sb("h3T", [P, KD, P])
        wr = sb("w_router", [P, KD, GROUPS + EXPERTS])
        ss1, rs1, ss3, r3, half = [sb(n, [P, 1]) for n in ("ss1", "rs1", "ss3", "r3", "att_half")]
        top, shift, total, inv = [sb(n, [P, XHEADS]) for n in ("top", "shift", "total", "inv")]

        wr_in, wr_ready, half_set = sem("wr_in"), sem("wr_ready"), sem("att_half_set")
        xa_in, xb_in, x2_out, h3_out = [sem(n) for n in ("xa_in", "xb_in", "x2_out", "h3_out")]
        sq1, ms1, ms1b, r1_done, sq3, ms3, r3_done = [sem(n) for n in (
            "sq1", "ms1", "ms1b", "r1_done", "sq3", "ms3", "r3_done")]
        t1_ps, xT_h, xT_l, s_ps, max_done, shift_done, exp_done, inv_done, prob_done = [sem(n) for n in (
            "t1_ps", "xT_h", "xT_l", "att_s_ps", "max_done", "shift_done", "exp_done", "inv_done", "prob_done")]
        p_ps, pT_h, pT_l, o_ps, x2_done, h3_done, t3_ps, h3T_done, l_ps, logit_done = [sem(n) for n in (
            "p_ps", "pT_h", "pT_l", "att_o_ps", "x2_done", "h3_done", "t3_ps", "h3T_done", "l_ps", "logit_done")]
        passed, sp_passed = sem("att_pool_passed"), sem("att_sp_passed")
        block = ctx.enter_context(nc.Block())
        W = GROUPS + EXPERTS

        def steps(engine, step):
            step(0)
            step(1)
            with engine.Fori(2, TILES - 1) as i:
                step(i)
            step(TILES - 1)
            step(TILES)

        def has(i, offset):
            return not isinstance(i, int) or 0 <= i + offset < TILES

        @block.sync
        def _(sp):
            sp.dma_start(xa[:], x1[0:P, :]).then_inc(xa_in, 16)
            sp.dma_start(wr[:, :, 0:GROUPS], ins["w_grp"][0].rearrange("(k p) n -> p k n", p=P)).then_inc(wr_in, 16)
            sp.dma_start(wr[:, :, GROUPS:], ins["w_rt"][0].rearrange("(k p) n -> p k n", p=P)).then_inc(wr_in, 16)

            def step(i):
                if has(i, 1):
                    row, n1, n2 = snap(sp, (i + 1) * P), snap(sp, i + 1), snap(sp, i + 2)
                    wait_apart(sp, sp_passed, (t1_ps, n1))
                    wait_apart(sp, sp_passed, (sq1, n2))
                    sp.dma_start(xa[:], x1[bass.ds(row, P), :]).then_inc(xa_in, 16)
                if has(i, -1):
                    row = snap(sp, (i - 1) * P)
                    stored = snap(sp, i * 16)
                    sp.dma_start(xb[:], x1[bass.ds(row, P), :]).then_inc(xb_in, 16)
                    sp.wait_ge(x2_done, snap(sp, i * 1))
                    sp.dma_start(x2[bass.ds(row, P), :], xb[:]).then_inc(x2_out, 16)
                    sp.wait_ge(h3_done, snap(sp, i + 1))
                    sp.dma_start(h3[bass.ds(row, P), :], h3_sb[:]).then_inc(h3_out, 16)
                    wait_apart(sp, sp_passed, (x2_out, stored))

            steps(sp, step)
            sp.wait_ge(h3_out, 16 * TILES)

        @block.gpsimd
        def _(pool):
            pool.memset(half[:], -0.5).then_inc(half_set, 1)
            pool.wait_ge(half_set, 1)

            def root1(j):
                n1, n2 = snap(pool, j + 1), snap(pool, j + 2)
                wait_apart(pool, passed, (sq1, n2), (exp_done, n1))
                pool.tensor_scalar(rs1[:], ss1[:], 1.0 / D, EPS, ALU.mult, ALU.add).then_inc(ms1, 1)
                pool.wait_ge(ms1, n2)
                pool.tensor_tensor(rs1[:], rs1[:], half[:], ALU.pow).then_inc(ms1b, 1)
                wait_apart(pool, passed, (ms1b, n1))
                pool.tensor_scalar(rs1[:], rs1[:], float(XDIM) ** -0.5, None, ALU.mult).then_inc(r1_done, 1)

            def root3(j):
                n1, n2 = snap(pool, j + 1), snap(pool, j + 2)
                wait_apart(pool, passed, (sq3, n2), (h3_done, n1))
                pool.tensor_scalar(r3[:], ss3[:], 1.0 / D, EPS, ALU.mult, ALU.add).then_inc(ms3, 1)
                pool.wait_ge(ms3, n2)
                pool.tensor_tensor(r3[:], r3[:], half[:], ALU.pow).then_inc(r3_done, 1)

            def step(i):
                if has(i, 1):
                    root1(i + 1)
                if has(i, -1):
                    root3(i - 1)

            pool.sem_inc(ms1, 1)
            pool.sem_inc(ms3, 1)
            root1(0)
            steps(pool, step)

        @block.scalar
        def _(act):
            def square1(j):
                act.wait_ge(xa_in, snap(act, j * 16 + 16))
                act.wait_ge(ms1, snap(act, j + 1))
                act.wait_ge(sq1, snap(act, j + 1))
                act.activation(square[:, 0], xa[:], ACT.Square, accum_out=ss1[:]).then_inc(sq1, 1)

            def exps(j):
                n1 = snap(act, j + 1)
                act.wait_ge(shift_done, n1)
                act.wait_ge(p_ps, n1)
                act.wait_ge(inv_done, n1)
                for h in range(XHEADS):
                    cols = slice(h * MEM, (h + 1) * MEM)
                    e = act.activation(prob[:, cols], scored[:, cols], ACT.Exp, bias=shift[:, h:h + 1], scale=rs1[:],
                                       accum_out=total[:, h:h + 1])
                e.then_inc(exp_done, 1)

            def turn1(j):
                act.wait_ge(t1_ps, snap(act, j + 1))
                act.activation(xT_hi[:], by_k(turned), ACT.Copy).then_inc(xT_h, 1)

            def step(i):
                if has(i, 1):
                    square1(i + 1)
                if has(i, 0):
                    exps(i)
                if has(i, 1):
                    turn1(i + 1)
                if has(i, -2):
                    act.wait_ge(t3_ps, snap(act, i - 1))
                    act.activation(h3T[:], by_k(prob_ps), ACT.Copy).then_inc(h3T_done, 1)
                if has(i, -1):
                    act.wait_ge(x2_done, snap(act, i * 1))
                    act.wait_ge(ms3, snap(act, i * 1))
                    act.wait_ge(sq3, snap(act, i * 1))
                    act.activation(square[:, 1], xb[:], ACT.Square, accum_out=ss3[:]).then_inc(sq3, 1)
                if has(i, 0):
                    act.wait_ge(p_ps, snap(act, i + 2))
                    act.activation(pT_hi[:], by_k(prob_ps), ACT.Copy).then_inc(pT_h, 1)

            act.sem_inc(sq1, 1)
            act.sem_inc(sq3, 1)
            act.sem_inc(exp_done, 1)
            act.sem_inc(h3T_done, 2)
            square1(0)
            turn1(0)
            steps(act, step)
            act.wait_ge(t3_ps, TILES)
            act.activation(h3T[:], by_k(prob_ps), ACT.Copy).then_inc(h3T_done, 1)

        @block.vector
        def _(dve):
            def turn1(j):
                dve.wait_ge(xT_h, snap(dve, j + 1))
                dve.tensor_tensor(xT_lo[:], by_k(turned), f32(xT_hi[:]), ALU.subtract).then_inc(xT_l, 1)

            def keep_logits(j):
                dve.wait_ge(l_ps, snap(dve, j + 1))
                dve.tensor_copy(keep.logits[:, bass.ds(j, 1), :], scored[:, 0:W].unsqueeze(1)).then_inc(logit_done, 1)

            def step(i):
                n1, n2 = snap(dve, i + 1), snap(dve, i + 2)
                if has(i, 0):
                    dve.wait_ge(s_ps, n1)
                    dve.tensor_reduce(top[:], scored.rearrange("p (h m) -> p h m", m=MEM), AX.X, ALU.max).then_inc(max_done, 1)
                    dve.wait_ge(max_done, n1)
                    dve.wait_ge(r1_done, n1)
                    dve.tensor_scalar(shift[:], top[:], rs1[:], -1.0, ALU.mult, ALU.mult).then_inc(shift_done, 1)
                if has(i, 1):
                    turn1(i + 1)
                if has(i, 0):
                    dve.wait_ge(exp_done, n2)
                    dve.reciprocal(inv[:], total[:]).then_inc(inv_done, 1)
                    dve.wait_ge(inv_done, n2)
                    heads = prob[:].rearrange("p (h m) -> p h m", m=MEM)
                    dve.tensor_tensor(heads, heads, inv[:].unsqueeze(2).broadcast_to((P, XHEADS, MEM)),
                                      ALU.mult).then_inc(prob_done, 1)
                if has(i, -1):
                    dve.wait_ge(o_ps, snap(dve, i * 1))
                    dve.wait_ge(xb_in, snap(dve, i * 16))
                    dve.tensor_tensor(xb[:], mixed, xb[:], ALU.add).then_inc(x2_done, 1)
                if has(i, -2):
                    keep_logits(i - 2)
                if has(i, 0):
                    dve.wait_ge(pT_h, n1)
                    dve.tensor_tensor(pT_lo[:], by_k(prob_ps), f32(pT_hi[:]), ALU.subtract).then_inc(pT_l, 1)
                if has(i, -1):
                    dve.wait_ge(r3_done, snap(dve, i * 1))
                    dve.wait_ge(x2_done, snap(dve, i * 1))
                    if has(i, -2):
                        dve.wait_ge(h3_out, snap(dve, i * 16 - 16))
                        dve.wait_ge(t3_ps, snap(dve, i - 1))
                    dve.tensor_scalar(h3_sb[:], xb[:], r3[:], None, ALU.mult).then_inc(h3_done, 1)

            dve.sem_inc(xT_l, 1)
            dve.sem_inc(inv_done, 1)
            dve.sem_inc(pT_l, 1)
            dve.sem_inc(h3_done, 1)
            dve.sem_inc(logit_done, 3)
            turn1(0)
            dve.wait_ge(wr_in, 32)
            gain = keep.cols[:, COLS["g_ffn"]:COLS["g_ffn"] + KD]
            dve.tensor_tensor(wr[:], wr[:], gain.unsqueeze(2).broadcast_to((P, KD, W)), ALU.mult).then_inc(wr_ready, 1)
            steps(dve, step)
            keep_logits(TILES - 1)

        @block.tensor
        def _(pe):
            def turn(out, of, done):
                for k in range(KD):
                    mm = pe.transpose(out[:, k * P:(k + 1) * P], of[:, k * P:(k + 1) * P], keep.ident[:])
                mm.then_inc(done, 1)

            def turn1(j):
                pe.wait_ge(xa_in, snap(pe, j * 16 + 16))
                pe.wait_ge(xT_l, snap(pe, j + 1))
                turn(turned, xa, t1_ps)

            def times(out, a_hi, a_lo, b_hi, b_lo, done):
                for k in range(KD):
                    for nh in range(2):
                        cols = slice(nh * 512, (nh + 1) * 512)
                        mm = product(pe, out[:, cols], a_hi[:, k], a_lo[:, k], b_hi[:, k, cols], b_lo[:, k, cols],
                                     k == 0, k == KD - 1)
                mm.then_inc(done, 1)

            def turn3(j):
                pe.wait_ge(h3_done, snap(pe, j + 2))
                pe.wait_ge(pT_l, snap(pe, j + 3) if has(j, 1) else TILES + 1)
                turn(prob_ps, h3_sb, t3_ps)

            def route(j):
                pe.wait_ge(wr_ready, 1)
                pe.wait_ge(h3T_done, snap(pe, j + 3))
                pe.wait_ge(exp_done, snap(pe, j + 4) if has(j, 2) else TILES + 1)
                for k in range(KD):
                    mm = pe.matmul(scored[:, 0:W], h3T[:, k], wr[:, k], start=(k == 0), stop=(k == KD - 1))
                mm.then_inc(l_ps, 1)

            def step(i):
                if has(i, 0):
                    pe.wait_ge(xT_l, snap(pe, i + 2))
                    pe.wait_ge(exp_done, snap(pe, i + 1))
                    pe.wait_ge(logit_done, snap(pe, i + 1))
                    times(scored, xT_hi, xT_lo, fold.a_hi, fold.a_lo, s_ps)
                if has(i, 1):
                    turn1(i + 1)
                if has(i, -2):
                    turn3(i - 2)
                if has(i, -1):
                    pe.wait_ge(pT_l, snap(pe, i + 1))
                    if has(i, -2):
                        pe.wait_ge(x2_done, snap(pe, i - 1))
                    times(mixed, pT_hi, pT_lo, fold.b_hi, fold.b_lo, o_ps)
                if has(i, -2):
                    route(i - 2)
                if has(i, 0):
                    pe.wait_ge(prob_done, snap(pe, i + 1))
                    pe.wait_ge(pT_l, snap(pe, i + 1))
                    pe.wait_ge(h3T_done, snap(pe, i + 1))
                    turn(prob_ps, prob, p_ps)

            pe.sem_inc(p_ps, 1)
            turn1(0)
            steps(pe, step)
            pe.wait_ge(logit_done, TILES + 2)
            turn3(TILES - 1)
            route(TILES - 1)


class Routed:

    SECOND, NEXT, PREVIOUS, ORDER, ROW = 0, 1, 2, 3, 10
    EXPERT, FOLLOWING, GOES_ON = 0, 5, 10

    def __init__(self, nc, ctx):
        sb = lambda n, s, d=F32: ctx.enter_context(nc.sbuf_tensor(n, s, d))
        self.tokens = sb("block_tokens", [P, LISTED], U32)
        self.rows = sb("token_rows", [P, 2, TILES], U32)
        self.gates = sb("gates", [P, 2, TILES])
        self.plan = sb("plan", [1, 2, SLOTS + 1], I32)
        self.slots = sb("active_slots", [1, 1], I32)


GU, DN = KD, DE // P
UNITS = GU + DN


class Staged:

    def __init__(self, nc, ctx):
        sb = lambda n, d=F32: ctx.enter_context(nc.sbuf_tensor(n, [P, UNITS, 1024], d))
        self.raw, self.hi, self.lo = sb("moe_raw"), sb("moe_w_hi", F32R), sb("moe_w_lo", F32R)
        self.index = [ctx.enter_context(nc.sbuf_tensor(f"token_index_{b}", [P, 1], U32)) for b in "AB"]
        self.tokens = [ctx.enter_context(nc.sbuf_tensor(f"moe_x_{b}", [P, D], F32)) for b in "AB"]


def gate_up_source(ins, expert, k):
    return [ins[w][0, bass.ds(expert, 1), k * P:(k + 1) * P, :].rearrange("e p n -> (e p) n") for w in ("w_gate", "w_up")]


def routing(nc, keep, ins, routed, staged, h3):
    W = GROUPS + EXPERTS
    S1 = SLOTS + 1
    PAIRS = 2 * TILES
    FAR = 3.0e38
    with ExitStack() as ctx:
        sb = lambda n, s, d=F32: ctx.enter_context(nc.sbuf_tensor(n, s, d))
        sem = semaphores(nc, ctx)
        bank = ctx.enter_context(nc.psum_tensor("route_ps", [P, 8, 512], F32))
        bias = keep.bias
        logits = keep.logits
        grp = sb("grp", [P, TILES, 8])
        grp_top, grp_at = sb("grp_top", [P, TILES, 8]), sb("grp_at", [P, TILES, 8], U32)
        grp_exp, grp_sum = sb("grp_exp", [P, TILES, GROUPS]), sb("grp_sum", [P, TILES])
        grp_id = sb("grp_id", [P, TILES])
        mask, far = sb("mask", [P, TILES, GROUPS]), sb("far", [P, TILES, GROUPS])
        inside = sb("inside", [P, TILES, EXPERTS])
        exp_top, exp_at = sb("exp_top", [P, TILES, 8]), sb("exp_at", [P, TILES, 8], U32)
        ids = sb("ids", [P, 2, TILES])
        gap, ratio, den = sb("gap", [P, TILES]), sb("ratio", [P, TILES]), sb("den", [P, TILES])
        chosen = sb("chosen", [P, 2, TILES, EXPERTS])
        both = sb("both", [P, TILES, EXPERTS], BF16)
        PAD_T = TILES // 2
        so_far = sb("so_far", [P, 2, PAD_T + TILES + 1, EXPERTS], BF16)
        last = (TILES - 1).bit_length() % 2
        picked = sb("picked", [P, 2, TILES, EXPERTS])
        before = sb("before", [P, TILES, EXPERTS])
        count_i, slots_i = sb("count_i", [P, EXPERTS], I32), sb("slots_i", [P, EXPERTS], I32)
        PAD_E = EXPERTS // 2
        held = sb("held", [P, 2, EXPERTS])
        sums = sb("held_sums", [P, 2, 2, PAD_E + EXPERTS])
        starts = sb("starts", [P, 2, EXPERTS])
        dest, dest_i = sb("dest", [P, 2, TILES]), sb("dest_i", [P, 2, TILES], I32)
        part_i, part = sb("part_i", [P, 2, 2, TILES], I32), sb("part", [P, 2, 2, TILES], BF16)
        part_f = sb("part_f", [P, 2, TILES])
        place = sb("place", [P, PAIRS, P], BF16)
        blocks = sb("blocks", [P, 3, PAIRS, LISTED], BF16)
        iota_e = sb("iota_e", [P, EXPERTS])
        iota_p = sb("iota_p", [P, 1])
        iota_r = sb("iota_r", [P, P], BF16)
        earlier, ones_b = sb("earlier", [P, P], BF16), sb("ones_b", [P, P], BF16)
        list_f = sb("list_f", [P, LISTED])
        slot = sb("slot", [S1, 3])
        ended, expert = sb("ended", [S1, 3, EXPERTS]), sb("slot_expert", [S1, 3])
        spans = sb("spans", [P, 2, EXPERTS])
        at_slot, at_sum = sb("at_slot", [S1, 2, 3, EXPERTS]), sb("at_sum", [S1, 2, 3])
        second, second_b = sb("second", [S1, 3]), sb("second_b", [S1, 3], BF16)
        row, words = sb("row_before", [S1, 1]), sb("words", [S1, 2])

        made, chain = sem("pool_made"), sem("route_chain")
        index_ready, gathered = sem("first_index_ready"), sem("first_gathered")
        hits_ready, weighted = sem("hits_ready"), sem("blocks_weighted")
        staged_in = [sem(f"staged_in{k}") for k in range(GU)]
        scaled, staged_hi, staged_lo = sem("staged_scaled"), sem("staged_hi"), sem("staged_lo")
        second_ready, ordered, words_ready, words_turned = [sem(n) for n in (
            "second_ready", "ordered", "words_ready", "words_turned")]
        grp_ready, grp_exped, gap_ready, ratio_ready = [sem(n) for n in ("grp_ready", "grp_exped", "gap_ready", "ratio_ready")]
        both_ready, counted, blocks_ready, listed = [sem(n) for n in ("both_ready", "counted", "blocks_ready", "listed")]
        block = ctx.enter_context(nc.Block())

        @block.sync
        def _(sp):
            for k in range(GU):
                for half, source in enumerate(gate_up_source(ins, 0, k)):
                    sp.dma_start(staged.raw[:, k, half * DE:(half + 1) * DE], source).then_inc(staged_in[k], 16)

        @block.gpsimd
        def _(pool):
            pool.iota(iota_e[:], pattern=[[1, EXPERTS]], base=0, channel_multiplier=0,
                      allow_small_or_imprecise_dtypes=True).then_inc(made, 1)
            pool.iota(iota_p[:], pattern=[[0, 1]], base=0, channel_multiplier=1,
                      allow_small_or_imprecise_dtypes=True).then_inc(made, 1)
            pool.iota(iota_r[:], pattern=[[1, P]], base=0, channel_multiplier=0,
                      allow_small_or_imprecise_dtypes=True).then_inc(made, 1)
            pool.iota(slot[:], pattern=[[1, 3]], base=-1, channel_multiplier=1,
                      allow_small_or_imprecise_dtypes=True).then_inc(made, 1)
            pool.memset(ones_b[:], 1.0).then_inc(made, 1)
            pool.memset(so_far[:], 0.0).then_inc(made, 1)
            pool.memset(sums[:], 0.0).then_inc(made, 1)
            pool.wait_ge(made, 7)
            pool.affine_select(out=earlier[:], in_=ones_b[:], compare_op=ALU.is_gt, fill=0.0, base=0,
                               pattern=[[1, P]], channel_multiplier=-1).then_inc(made, 1)
            for k in range(GU):
                pool.wait_ge(staged_hi, k + 1)
                pool.tensor_tensor(staged.lo[:, k], staged.raw[:, k], f32(staged.hi[:, k]), ALU.subtract).then_inc(staged_lo, 1)
            pool.wait_ge(index_ready, 1)
            pool.indirect_dma_start(out=staged.tokens[0][:], out_offset=None, in_=h3[:, :],
                                    in_offset=bass.IndirectOffsetOnAxis(ap=staged.index[0][:, :1], axis=0)).then_inc(gathered, 16)
            pool.wait_ge(gathered, 16)

        @block.scalar
        def _(act):
            for k in range(GU):
                if k == GU // 2:
                    act.wait_ge(grp_ready, 1)
                    act.activation(grp_exp[:], grp_exp[:], ACT.Exp).then_inc(grp_exped, 1)
                gain = keep.cols[:, COLS["g_ffn"] + k:COLS["g_ffn"] + k + 1]
                act.wait_ge(staged_in[k], 32)
                act.activation(staged.raw[:, k], staged.raw[:, k], ACT.Copy, scale=gain).then_inc(scaled, 1)
                act.wait_ge(scaled, k + 1)
                act.activation(staged.hi[:, k], staged.raw[:, k], ACT.Copy).then_inc(staged_hi, 1)
            act.wait_ge(gap_ready, 1)
            act.activation(ratio[:], gap[:], ACT.Exp).then_inc(ratio_ready, 1)
            act.wait_ge(hits_ready, 1)
            of_tile = lambda k, t: blocks[:, k].rearrange("p (c t) b -> p c t b", c=2)[:, :, t]
            for t in range(TILES):
                mm = act.activation(of_tile(2, t), of_tile(0, t), ACT.Copy, scale=float(t))
            mm.then_inc(weighted, 1)

        @block.tensor
        def _(pe):
            pe.wait_ge(made, 8)
            pe.wait_ge(both_ready, 1)
            flat = lambda tile: tile.rearrange("p t e -> p (t e)")
            pe.matmul(bank[:, 1, 0:EXPERTS], ones_b[:], so_far[:, last, PAD_T + TILES], start=True, stop=True)
            pe.matmul(bank[:, 0], earlier[:], flat(both[:]), start=True, stop=False)
            pe.matmul(bank[:, 0], ones_b[:], flat(so_far[:, last, PAD_T:PAD_T + TILES]), start=False, stop=True).then_inc(counted, 1)
            pe.wait_ge(blocks_ready, 1)
            pe.wait_ge(weighted, 1)
            for j in range(PAIRS):
                mm = pe.matmul(bank[:, 2, 0:2 * LISTED].rearrange("p (k b) -> p k b", k=2), place[:, j], blocks[:, 1:3, j],
                               start=(j == 0), stop=(j == PAIRS - 1))
            mm.then_inc(listed, 1)
            pe.wait_ge(second_ready, 1)
            pe.matmul(bank[0:S1, 3, 0:1], earlier[0:S1, 0:S1], second_b[:, 0:1], start=True, stop=True).then_inc(ordered, 1)
            pe.wait_ge(words_ready, 1)
            for k in range(2):
                mm = pe.transpose(bank[0:1, 4, k * S1:(k + 1) * S1], words[:, k:k + 1], keep.ident[0:S1, 0:S1])
            mm.then_inc(words_turned, 1)

        @block.vector
        def _(dve):
            steps = [0]

            def link(instruction):
                steps[0] += 1
                instruction.then_inc(chain, 1)
                dve.wait_ge(chain, steps[0])

            def copy(out, of):
                link(dve.tensor_copy(out, of))

            def bcast(ap, axis, shape):
                return ap.unsqueeze(axis).broadcast_to(shape)

            link(dve.tensor_tensor(logits[:], logits[:], bcast(bias[:], 1, (P, TILES, W)), ALU.add))
            link(dve.memset(grp[:], -FAR))
            copy(grp[:, :, 0:GROUPS], logits[:, :, 0:GROUPS])
            for t in range(TILES):
                mm = dve.max(grp_top[:, t], grp[:, t])
            link(mm)
            for t in range(TILES):
                mm = dve.max_index(grp_at[:, t], grp_top[:, t], grp[:, t])
            link(mm)
            dve.tensor_tensor(grp_exp[:], logits[:, :, 0:GROUPS], grp_top[:, :, 0:1].broadcast_to((P, TILES, GROUPS)),
                              ALU.subtract).then_inc(grp_ready, 1)
            copy(grp_id[:], grp_at[:, :, 0])
            dve.wait_ge(made, 8)
            link(dve.tensor_tensor(mask[:], bcast(iota_e[:, 0:GROUPS], 1, (P, TILES, GROUPS)),
                                   bcast(grp_id[:], 2, (P, TILES, GROUPS)), ALU.is_equal))
            link(dve.tensor_scalar(far[:], mask[:], -1.0, FAR, ALU.add, ALU.mult))
            in_order = inside[:].rearrange("p t (e g) -> p t e g", g=GROUPS)
            spread = lambda m: bcast(m[:], 2, (P, TILES, PER_GROUP, GROUPS))
            link(dve.tensor_tensor(in_order, logits[:, :, GROUPS:].rearrange("p t (g e) -> p t e g", g=GROUPS),
                                   spread(far), ALU.add))
            for t in range(TILES):
                mm = dve.max(exp_top[:, t], inside[:, t])
            link(mm)
            for t in range(TILES):
                mm = dve.max_index(exp_at[:, t], exp_top[:, t], inside[:, t])
            link(mm)
            dve.tensor_tensor(gap[:], exp_top[:, :, 1], exp_top[:, :, 0], ALU.subtract).then_inc(gap_ready, 1)
            for c in range(2):
                copy(ids[:, c], exp_at[:, :, c])
            for c in range(2):
                link(dve.tensor_tensor(chosen[:, c], bcast(iota_e[:], 1, (P, TILES, EXPERTS)),
                                       bcast(ids[:, c], 2, (P, TILES, EXPERTS)), ALU.is_equal))
            link(dve.tensor_tensor(both[:], chosen[:, 0], chosen[:, 1], ALU.add))
            copy(so_far[:, 0, PAD_T + 1:], both[:])
            at, step = 0, 1
            while step < TILES:
                added = dve.tensor_tensor(so_far[:, 1 - at, PAD_T + 1:], so_far[:, at, PAD_T + 1:],
                                          so_far[:, at, PAD_T + 1 - step:PAD_T + 1 + TILES - step], ALU.add)
                at, step = 1 - at, 2 * step
                if step < TILES:
                    link(added)
            added.then_inc(both_ready, 1)
            dve.wait_ge(grp_exped, 1)
            link(dve.tensor_reduce(grp_sum[:], grp_exp[:], AX.X, ALU.add))
            dve.wait_ge(ratio_ready, 1)
            link(dve.tensor_scalar(den[:], ratio[:], 1.0, None, ALU.add))
            link(dve.tensor_tensor(den[:], den[:], grp_sum[:], ALU.mult))
            link(dve.reciprocal(routed.gates[:, 0], den[:]))
            link(dve.tensor_tensor(routed.gates[:, 1], routed.gates[:, 0], ratio[:], ALU.mult))

            dve.wait_ge(counted, 1)
            copy(held[:, 1], bank[:, 1, 0:EXPERTS])
            link(dve.tensor_scalar(count_i[:], held[:, 1], float(SLOT - 1), None, ALU.add))
            link(dve.tensor_scalar(slots_i[:], count_i[:], 8, None, ALU.arith_shift_right))
            link(dve.tensor_scalar(held[:, 0], slots_i[:], 1.0, None, ALU.max))
            copy(sums[:, 0, :, PAD_E:], held[:])
            at, step = 0, 1
            while step < EXPERTS:
                link(dve.tensor_tensor(sums[:, 1 - at, :, PAD_E:], sums[:, at, :, PAD_E:],
                                       sums[:, at, :, PAD_E - step:PAD_E + EXPERTS - step], ALU.add))
                at, step = 1 - at, 2 * step
            end = sums[:, at, 0, PAD_E:]
            link(dve.tensor_tensor(starts[:], sums[:, at, :, PAD_E:], held[:], ALU.subtract))
            link(dve.scalar_tensor_tensor(before[:], bcast(starts[:, 0], 1, (P, TILES, EXPERTS)), float(SLOT),
                                          bank[:, 0].rearrange("p (t e) -> p t e", e=EXPERTS), ALU.mult, ALU.add))
            flat2 = lambda tile: tile[:].rearrange("p c t e -> p (c t) e")
            flat_s = lambda tile: tile[:].rearrange("p c t -> p (c t)")
            for c in range(2):
                link(dve.tensor_tensor(picked[:, c], chosen[:, c], before[:], ALU.mult))
            link(dve.tensor_reduce(flat_s(dest), flat2(picked), AX.X, ALU.add))
            copy(dest_i[:], dest[:])
            link(dve.tensor_scalar(part_i[:, 0], dest_i[:], P - 1, None, ALU.bitwise_and))
            link(dve.tensor_scalar(part_i[:, 1], dest_i[:], 7, None, ALU.arith_shift_right))
            copy(part[:], part_i[:])
            col = lambda k: part[:, k].rearrange("p c t -> p (c t)")
            dve.tensor_tensor(blocks[:, 0], bcast(iota_r[:, 0:LISTED], 1, (P, PAIRS, LISTED)),
                              bcast(col(1), 2, (P, PAIRS, LISTED)), ALU.is_equal).then_inc(hits_ready, 1)
            dve.wait_ge(hits_ready, 1)
            dve.tensor_scalar(blocks[:, 1], blocks[:, 0], iota_p[:], None, ALU.mult)
            dve.tensor_tensor(place[:], bcast(iota_r[:], 1, (P, PAIRS, P)), bcast(col(0), 2, (P, PAIRS, P)),
                              ALU.is_equal).then_inc(blocks_ready, 1)

            three = (S1, 3, EXPERTS)
            link(dve.tensor_tensor(ended[:], bcast(end[0:S1], 1, three), bcast(slot[:], 2, three), ALU.is_le))
            link(dve.tensor_reduce(expert[:], ended[:], AX.X, ALU.add))
            link(dve.tensor_scalar(expert[:], expert[:], float(EXPERTS - 1), None, ALU.min))
            link(dve.tensor_tensor(ended[:], bcast(iota_e[0:S1], 1, three), bcast(expert[:], 2, three), ALU.is_equal))
            link(dve.scalar_tensor_tensor(spans[:, 0], starts[:, 0], float(SLOT), held[:, 1], ALU.mult, ALU.add))
            link(dve.scalar_tensor_tensor(spans[:, 1], starts[:, 0], -float(SLOT), starts[:, 1], ALU.mult, ALU.add))
            for k in range(2):
                link(dve.tensor_tensor(at_slot[:, k], ended[:], bcast(spans[0:S1, k], 1, three), ALU.mult))
            link(dve.tensor_reduce(at_sum[:].rearrange("p k j -> p (k j)"), at_slot[:].rearrange("p k j e -> p (k j) e"), AX.X, ALU.add))
            link(dve.scalar_tensor_tensor(second[:], slot[:], -float(SLOT), at_sum[:, 0], ALU.mult, ALU.add))
            link(dve.tensor_scalar(second[:], second[:], float(P), None, ALU.is_gt))
            link(dve.scalar_tensor_tensor(second[:], slot[:], 0.0, second[:], ALU.is_ge, ALU.mult))
            dve.tensor_copy(second_b[:], second[:]).then_inc(second_ready, 1)
            link(dve.scalar_tensor_tensor(row[:], slot[:, 0:1], float(SLOT), at_sum[:, 1, 0:1], ALU.mult, ALU.add))
            link(dve.tensor_scalar(row[:], row[:], 0.0, float(2 * SEQ), ALU.max, ALU.min))
            link(dve.tensor_scalar(words[:, 0:1], second[:, 1:2], float(1 << Routed.SECOND), None, ALU.mult))

            def field(k, bit, of):
                link(dve.scalar_tensor_tensor(words[:, k:k + 1], of, float(1 << bit), words[:, k:k + 1], ALU.mult, ALU.add))

            field(0, Routed.NEXT, second[:, 2:3])
            field(0, Routed.PREVIOUS, second[:, 0:1])
            field(0, Routed.ROW, row[:])
            copy(words[:, 1:2], expert[:, 1:2])
            field(1, Routed.FOLLOWING, expert[:, 2:3])
            link(dve.tensor_tensor(row[:], end[0:S1, EXPERTS - 1:EXPERTS], slot[:, 2:3], ALU.is_gt))
            field(1, Routed.GOES_ON, row[:])
            link(dve.tensor_scalar(words[:, 0:1], words[:, 0:1], float(1 << Routed.ORDER), None, ALU.add))
            dve.wait_ge(ordered, 1)
            dve.scalar_tensor_tensor(words[:, 0:1], bank[0:S1, 3, 0:1], float(1 << Routed.ORDER), words[:, 0:1],
                                     ALU.mult, ALU.add).then_inc(words_ready, 1)
            copy(routed.slots[:], end[0:1, EXPERTS - 1:EXPERTS])
            dve.wait_ge(listed, 1)
            copy(list_f[:], bank[:, 2, LISTED:2 * LISTED])
            link(dve.scalar_tensor_tensor(list_f[:], list_f[:], float(P), bank[:, 2, 0:LISTED], ALU.mult, ALU.add))
            dve.tensor_copy(staged.index[0][:], list_f[:, 0:1]).then_inc(index_ready, 1)
            copy(routed.tokens[:], list_f[:])
            link(dve.tensor_tensor(flat2(picked), flat2(chosen), bcast(spans[:, 1], 1, (P, PAIRS, EXPERTS)), ALU.mult))
            link(dve.tensor_reduce(flat_s(part_f), flat2(picked), AX.X, ALU.add))
            link(dve.tensor_tensor(dest[:], dest[:], part_f[:], ALU.add))
            copy(routed.rows[:], dest[:])
            dve.wait_ge(words_turned, 1)
            copy(routed.plan[:], bank[0:1, 4, 0:2 * S1].rearrange("p (k s) -> p k s", k=2))


def moe(nc, keep, ins, routed, staged, h3, y):
    EARLY = GU - 1
    CHECKED = 4
    w_down = ins["w_down"]
    raw, w_hi, w_lo, index, tokens = staged.raw, staged.hi, staged.lo, staged.index, staged.tokens
    with ExitStack() as ctx:
        sb = lambda n, s, d=F32: ctx.enter_context(nc.sbuf_tensor(n, s, d))
        sem = semaphores(nc, ctx)
        bank = ctx.enter_context(nc.psum_tensor("moe_ps", [P, 8, 512], F32))
        pair = lambda b: bank[:, b:b + 2].rearrange("p b n -> p (b n)")
        by_chunk = lambda ap: ap.rearrange("p (k n) -> p k n", n=P)
        xT_hi = [sb(f"moe_xT_hi_{b}", [P, KD, P], F32R) for b in "AB"]
        xT_lo = [sb(f"moe_xT_lo_{b}", [P, KD, P], F32R) for b in "AB"]
        silu = [sb(f"silu_{b}", [P, DE]) for b in "AB"]
        hid = [sb(f"hidden_{b}", [P, DE]) for b in "AB"]
        hT_hi = [sb(f"hidT_hi_{b}", [P, DN, P], F32R) for b in "AB"]
        hT_lo = [sb(f"hidT_lo_{b}", [P, DN, P], F32R) for b in "AB"]
        y_sb = [sb(f"y_sb_{b}", [P, D]) for b in "AB"]

        raw_in = [sem(f"moe_raw_in{b}") for b in range(UNITS)]
        hi_done, lo_done = sem("moe_hi_done"), sem("moe_lo_done")
        gu_used, down_used = sem("gu_used"), sem("down_used")
        y_set, index_ready, pool_passed = sem("y_set"), [sem(f"index_ready_{b}") for b in "AB"], sem("moe_pool_passed")
        sp_passed = sem("moe_sp_passed")
        gathered = [sem(f"gathered_{b}") for b in "AB"]
        x_ps = [sem(f"x_ps_{b}") for b in "AB"]
        xT_h = [sem(f"moe_xT_h_{b}") for b in "AB"]
        xT_l = [sem(f"moe_xT_l_{b}") for b in "AB"]
        gu_ps, down_ps = sem("gu_ps"), sem("down_ps")
        silu_done = [sem(f"silu_done_{b}") for b in "AB"]
        hid_done = [sem(f"hid_done_{b}") for b in "AB"]
        hid_ps = [sem(f"hid_ps_{b}") for b in "AB"]
        hT_h = [sem(f"hidT_h_{b}") for b in "AB"]
        hT_l = [sem(f"hidT_l_{b}") for b in "AB"]
        y_kept = [sem(f"y_kept_{b}") for b in "AB"]
        y_out = [sem(f"y_out_{b}") for b in "AB"]
        block = ctx.enter_context(nc.Block())
        gain = lambda k: keep.cols[:, COLS["g_ffn"] + k:COLS["g_ffn"] + k + 1]

        def word(engine, slot, k=0):
            return engine.value_load(routed.plan[0:1, k, bass.ds(slot, 1)], min_val=0, max_val=(1 << 24) - 1)

        def field(engine, of, first, width=1):
            return snap(engine, (of >> first) & ((1 << width) - 1))

        class Blocks:

            def __init__(self, engine, plan):
                self.has_b, self.next_b, self.had_b = (
                    field(engine, plan, f) for f in (Routed.SECOND, Routed.NEXT, Routed.PREVIOUS))
                self.before = field(engine, plan, Routed.ORDER, 6)
                self.here = snap(engine, self.before + self.had_b)
                self.next = snap(engine, self.here + self.has_b)

        def slots_of(engine):
            return engine.value_load(routed.slots[0:1, 0:1], min_val=EXPERTS, max_val=SLOTS)

        def steps(engine, step):
            step(0, word(engine, 0))
            with engine.Fori(1, EXPERTS) as i:
                step(i, word(engine, i))
            slots = slots_of(engine)
            with engine.Fori(0, -(-(SLOTS - EXPERTS) // CHECKED)) as c:
                base = snap(engine, c * CHECKED + EXPERTS)
                with engine.If(slots > base):
                    with engine.Fori(0, CHECKED) as r:
                        i = snap(engine, base + r)
                        with engine.If(slots > i):
                            i = i.with_bounds(min_val=EXPERTS, max_val=SLOTS - 1)
                            step(i, word(engine, i))

        def behind(engine):
            slots = slots_of(engine)
            return slots, word(engine, slots)

        def staging(u):
            return (GU + u) % UNITS

        def arrived(i, u):
            return i * 32 + 32

        def split(i, u):
            return i * UNITS + (GU + u + 1)

        @block.sync
        def _(sp):
            def load_gu(expert, k, b):
                for half, source in enumerate(gate_up_source(ins, expert, k)):
                    sp.dma_start(raw[:, b, half * DE:(half + 1) * DE], source).then_inc(raw_in[b], 16)

            def step(i, plan):
                experts = word(sp, i, 1)
                own, following = (snap(sp, field(sp, experts, f, 2) * PER_GROUP + field(sp, experts, f + 2, 3))
                                  for f in (Routed.EXPERT, Routed.FOLLOWING))
                goes_on = field(sp, experts, Routed.GOES_ON)

                def wait_free(u):
                    if not isinstance(i, int):
                        wait_apart(sp, sp_passed, (lo_done, split(i - 1, u)))

                with sp.If(goes_on == 1):
                    for k in range(GU):
                        wait_free(k)
                        load_gu(following, k, staging(k))
                with sp.Else():
                    for k in range(GU):
                        wait_free(k)
                        sp.sem_inc(raw_in[staging(k)], 32)
                for k in range(DN):
                    wait_free(GU + k)
                    for half in range(2):
                        cols = slice(half * 512, (half + 1) * 512)
                        sp.dma_start(raw[:, staging(GU + k), cols],
                                     w_down[0, bass.ds(own, 1), k * P:(k + 1) * P, cols].rearrange("e p n -> (e p) n")
                                     ).then_inc(raw_in[staging(GU + k)], 16)

            steps(sp, step)

        @block.gpsimd
        def _(pool):
            def gather(slot, b, count):
                pool.tensor_copy(index[b][:], routed.tokens[:, bass.ds(slot * 2 + b, 1)]).then_inc(index_ready[b], 1)
                wait_apart(pool, pool_passed, (index_ready[b], count))
                pool.indirect_dma_start(out=tokens[b][:], out_offset=None, in_=h3[:, :],
                                        in_offset=bass.IndirectOffsetOnAxis(ap=index[b][:, :1], axis=0)).then_inc(gathered[b], 16)

            def step(i, plan):
                blocks = Blocks(pool, plan)
                next_b, b_next = blocks.next_b, blocks.next
                wait_apart(pool, pool_passed, (x_ps[0], i + 1))
                gather(i + 1, 0, i + 1)
                with pool.If(next_b == 1):
                    wait_apart(pool, pool_passed, (x_ps[1], b_next))
                    gather(i + 1, 1, b_next)
                if not isinstance(i, int):
                    store(i, blocks, plan)

            def store(i, blocks, plan):
                row = field(pool, plan, Routed.ROW, 13).with_bounds(min_val=0, max_val=2 * SEQ)
                wait_apart(pool, pool_passed, (y_out[0], i * 16))
                wait_apart(pool, pool_passed, (y_out[1], blocks.before * 16))
                wait_apart(pool, pool_passed, (y_kept[0], i + 1))
                pool.dma_start(y[bass.ds(row, P), :], y_sb[0][:]).then_inc(y_out[0], 16)
                with pool.If(blocks.had_b == 1):
                    wait_apart(pool, pool_passed, (y_kept[1], blocks.before + 1))
                    pool.dma_start(y[bass.ds(row + P, P), :], y_sb[1][:]).then_inc(y_out[1], 16)

            with pool.If(field(pool, word(pool, 0), Routed.SECOND) == 1):
                gather(0, 1, 1)
            for b in range(2):
                pool.memset(y_sb[b][:], 0.0).then_inc(y_set, 1)
            pool.wait_ge(y_set, 2)
            for b in range(2):
                pool.dma_start(y[2 * SEQ + b * P:2 * SEQ + (b + 1) * P, :], y_sb[b][:]).then_inc(y_out[b], 16)
            steps(pool, step)
            slots, plan = behind(pool)
            blocks = Blocks(pool, plan)
            store(slots, blocks, plan)
            wait_apart(pool, pool_passed, (y_out[0], slots * 16 + 16))
            wait_apart(pool, pool_passed, (y_out[1], blocks.here * 16))

        @block.tensor
        def _(pe):
            def turn(of, out, done):
                for k in range(of.shape[-1] // P):
                    mm = pe.transpose(out[:, k * P:(k + 1) * P], of[:, k * P:(k + 1) * P], keep.ident[:])
                mm.then_inc(done, 1)

            def gate_up(i, b, last):
                for k in range(GU):
                    if b == 0:
                        if not isinstance(i, int):
                            pe.wait_ge(lo_done, snap(pe, split(i - 1, k)))
                    for half in range(2):
                        cols = slice(half * DE, (half + 1) * DE)
                        mm = product(pe, bank[:, 2 + 2 * b + half], xT_hi[b][:, k], xT_lo[b][:, k],
                                     w_hi[:, k, cols], w_lo[:, k, cols], k == 0, k == GU - 1)
                    if last:
                        mm.then_inc(gu_used, 1)
                if not last:
                    mm.then_inc(gu_ps, 1)

            def down(i, b, last, final):
                for k in range(DN):
                    if b == 0:
                        pe.wait_ge(lo_done, snap(pe, i * UNITS + GU if final else split(i - 1, GU + k)))
                    for half in range(2):
                        cols = slice(half * 512, (half + 1) * 512)
                        mm = product(pe, bank[:, (0, 6)[b] + half], hT_hi[b][:, k], hT_lo[b][:, k],
                                     w_hi[:, GU + k, cols], w_lo[:, GU + k, cols], k == 0, k == DN - 1)
                    if last:
                        mm.then_inc(down_used, 1)
                if not last:
                    mm.then_inc(down_ps, 1)

            def turn_hidden(i, had_b, b_here):
                pe.wait_ge(hid_done[0], snap(pe, i * 1))
                pe.wait_ge(hid_done[1], b_here)
                turn(hid[0], bank[:, 4], hid_ps[0])
                with pe.If(had_b == 1):
                    turn(hid[1], bank[:, 5], hid_ps[1])

            def turn_tokens(slot, b_before, has_b, b_until):
                if not (isinstance(slot, int) and slot == 0):
                    pe.wait_ge(gathered[0], snap(pe, slot * 16))
                pe.wait_ge(y_kept[1], snap(pe, b_before))
                turn(tokens[0], pair(6), x_ps[0])
                with pe.If(has_b == 1):
                    pe.wait_ge(gathered[1], snap(pe, b_until * 16))
                    pe.wait_ge(hid_done[1], snap(pe, b_until))
                    turn(tokens[1], pair(4), x_ps[1])

            def finish(i, had_b, b_done, final=False):
                pe.wait_ge(hT_l[0], snap(pe, i * 1))
                pe.wait_ge(hT_l[1], snap(pe, b_done))
                pe.wait_ge(y_kept[0], snap(pe, i * 1))
                with pe.If(had_b == 1):
                    down(i, 0, False, final)
                    if not final:
                        pe.wait_ge(xT_l[0], snap(pe, i + 2))
                    down(i, 1, True, final)
                with pe.Else():
                    down(i, 0, True, final)

            def step(i, plan):
                blocks = Blocks(pe, plan)
                has_b, b_here, b_next, b_before = blocks.has_b, blocks.here, blocks.next, blocks.before
                had_b = None if isinstance(i, int) else blocks.had_b
                pe.wait_ge(xT_l[1], b_next)
                if had_b is not None:
                    turn_hidden(i, had_b, b_here)
                    pe.wait_ge(hid_done[0], snap(pe, i * 1))
                pe.wait_ge(xT_l[0], snap(pe, i + 1))
                with pe.If(has_b == 1):
                    gate_up(i, 0, False)
                    if had_b is not None:
                        pe.wait_ge(hT_l[0], snap(pe, i * 1))
                        pe.wait_ge(hT_l[1], b_here)
                    gate_up(i, 1, True)
                with pe.Else():
                    gate_up(i, 0, True)
                if had_b is not None:
                    pe.wait_ge(hT_l[0], snap(pe, i * 1))
                    pe.wait_ge(hT_l[1], b_here)
                turn_tokens(i + 1, b_before, blocks.next_b, b_next)
                if had_b is not None:
                    finish(i, had_b, b_here)

            pe.sem_inc(x_ps[1], 1)
            turn_tokens(0, 1, field(pe, word(pe, 0), Routed.SECOND), 1)
            steps(pe, step)
            slots, plan = behind(pe)
            blocks = Blocks(pe, plan)
            turn_hidden(slots, blocks.had_b, blocks.here)
            finish(slots, blocks.had_b, blocks.here, final=True)

        @block.scalar
        def _(act):
            def high(i, u):
                b = staging(u)
                act.wait_ge(raw_in[b], snap(act, arrived(i, u)))
                if u < GU:
                    act.wait_ge(gu_used, snap(act, i * GU + (u + 1)))
                elif not isinstance(i, int):
                    act.wait_ge(down_used, snap(act, i * DN - (DN - 1 - (u - GU))))
                act.activation(w_hi[:, u], raw[:, b], ACT.Copy, scale=gain(u) if u < GU else 1.0).then_inc(hi_done, 1)

            def gate(i, b, after, count):
                act.wait_ge(after, snap(act, count))
                act.activation(silu[b][:], bank[:, 2 + 2 * b], ACT.Silu).then_inc(silu_done[b], 1)

            def turned_hidden(i, had_b, b_before):
                act.wait_ge(hid_ps[0], snap(act, i * 1))
                act.activation(hT_hi[0][:], by_chunk(bank[:, 4]), ACT.Copy).then_inc(hT_h[0], 1)
                with act.If(had_b == 1):
                    act.wait_ge(hid_ps[1], snap(act, b_before))
                    act.activation(hT_hi[1][:], by_chunk(bank[:, 5]), ACT.Copy).then_inc(hT_h[1], 1)

            def turned_tokens(slot, b, count):
                act.wait_ge(x_ps[b], snap(act, count))
                act.activation(xT_hi[b][:], by_chunk(pair((6, 4)[b])), ACT.Copy).then_inc(xT_h[b], 1)

            def turn_next(slot, next_b, b_next):
                turned_tokens(slot, 0, slot + 1)
                with act.If(next_b == 1):
                    turned_tokens(slot, 1, b_next + 1)

            def result(b, after, count, stored):
                act.wait_ge(after, snap(act, count))
                act.wait_ge(y_out[b], snap(act, stored * 16))
                act.activation(y_sb[b][:], pair((0, 6)[b]), ACT.Copy).then_inc(y_kept[b], 1)

            def results(i, blocks):
                with act.If(blocks.had_b == 1):
                    result(0, down_ps, blocks.before, i * 1)
                    result(1, down_used, i * DN, blocks.before)
                with act.Else():
                    result(0, down_used, i * DN, i * 1)

            def step(i, plan):
                blocks = Blocks(act, plan)
                has_b, b_here, had_b, b_before = blocks.has_b, blocks.here, blocks.had_b, blocks.before
                first = isinstance(i, int)
                if not first:
                    turned_hidden(i, had_b, b_before)
                with act.If(has_b == 1):
                    gate(i, 0, gu_ps, b_here)
                    for u in range(EARLY):
                        high(i, u)
                    gate(i, 1, gu_used, i * GU + GU)
                with act.Else():
                    for u in range(EARLY):
                        high(i, u)
                    gate(i, 0, gu_used, i * GU + GU)
                turn_next(i + 1, blocks.next_b, blocks.next)
                for u in range(EARLY, UNITS):
                    high(i, u)
                if not first:
                    results(i, blocks)

            act.sem_inc(hi_done, GU)
            act.sem_inc(y_kept[0], 1)
            act.sem_inc(y_kept[1], 1)
            turn_next(0, field(act, word(act, 0), Routed.SECOND), 1)
            steps(act, step)
            slots, plan = behind(act)
            blocks = Blocks(act, plan)
            turned_hidden(slots, blocks.had_b, blocks.before)
            results(slots, blocks)

        @block.vector
        def _(dve):
            def low(i, u):
                b = staging(u)
                dve.wait_ge(hi_done, snap(dve, split(i, u)))
                if u < GU:
                    dve.scalar_tensor_tensor(w_lo[:, u], raw[:, b], gain(u), f32(w_hi[:, u]),
                                             ALU.mult, ALU.subtract).then_inc(lo_done, 1)
                else:
                    dve.tensor_tensor(w_lo[:, u], raw[:, b], f32(w_hi[:, u]), ALU.subtract).then_inc(lo_done, 1)

            def gated(i, b, silu_count):
                dve.wait_ge(silu_done[b], snap(dve, silu_count))
                if b == 0:
                    if not isinstance(i, int):
                        dve.wait_ge(hid_ps[0], snap(dve, i * 1))
                dve.tensor_tensor(hid[b][:], silu[b][:], bank[:, 3 + 2 * b], ALU.mult).then_inc(hid_done[b], 1)

            def turned_hidden(i, had_b, b_before):
                dve.wait_ge(hT_h[0], snap(dve, i * 1))
                dve.tensor_tensor(hT_lo[0][:], by_chunk(bank[:, 4]), f32(hT_hi[0][:]), ALU.subtract).then_inc(hT_l[0], 1)
                with dve.If(had_b == 1):
                    dve.wait_ge(hT_h[1], snap(dve, b_before))
                    dve.tensor_tensor(hT_lo[1][:], by_chunk(bank[:, 5]), f32(hT_hi[1][:]), ALU.subtract).then_inc(hT_l[1], 1)

            def turned_tokens(slot, b, count):
                dve.wait_ge(xT_h[b], snap(dve, count))
                dve.tensor_tensor(xT_lo[b][:], by_chunk(pair((6, 4)[b])), f32(xT_hi[b][:]), ALU.subtract).then_inc(xT_l[b], 1)

            def turn_next(slot, next_b, b_next):
                turned_tokens(slot, 0, slot + 1)
                with dve.If(next_b == 1):
                    turned_tokens(slot, 1, b_next)

            def step(i, plan):
                blocks = Blocks(dve, plan)
                has_b, b_here, had_b, b_before = blocks.has_b, blocks.here, blocks.had_b, blocks.before
                first = isinstance(i, int)
                if not first:
                    turned_hidden(i, had_b, b_before)
                with dve.If(has_b == 1):
                    gated(i, 0, i + 1)
                    for u in range(EARLY):
                        low(i, u)
                    gated(i, 1, b_here)
                with dve.Else():
                    for u in range(EARLY):
                        low(i, u)
                    gated(i, 0, i + 1)
                turn_next(i + 1, blocks.next_b, blocks.next)
                for u in range(EARLY, UNITS):
                    low(i, u)

            dve.sem_inc(lo_done, GU)
            dve.sem_inc(hid_done[1], 1)
            dve.sem_inc(hT_l[1], 1)
            dve.sem_inc(xT_l[1], 1)
            turn_next(0, field(dve, word(dve, 0), Routed.SECOND), 1)
            steps(dve, step)
            slots, plan = behind(dve)
            blocks = Blocks(dve, plan)
            turned_hidden(slots, blocks.had_b, blocks.before)


def combine(nc, keep, ins, routed, x2, y, out):
    BUFS = 4
    STEPS = TILES // BUFS
    with ExitStack() as ctx:
        sb = lambda n, s, d=F32: ctx.enter_context(nc.sbuf_tensor(n, s, d))
        sem = semaphores(nc, ctx)
        index = [[sb(f"row_index{b}{c}", [P, 1], U32) for c in range(2)] for b in range(BUFS)]
        ys = [[sb(f"y_row{b}{c}", [P, D]) for c in range(2)] for b in range(BUFS)]
        xs = [sb(f"x_tile{b}", [P, D]) for b in range(BUFS)]
        outs = [sb(f"out_tile{b}", [P, D]) for b in range(BUFS)]
        square = sb("final_square", [P, D], BF16)
        gain = sb("gain_final", [P, D])
        ss, r, half = sb("final_ss", [P, BUFS]), sb("final_r", [P, BUFS]), sb("final_half", [P, 1])
        gain_in, half_set, passed = sem("gain_in"), sem("final_half_set"), sem("final_pool_passed")
        x_in = [sem(f"final_x_in{b}") for b in range(BUFS)]
        y_in = [sem(f"final_y_in{b}") for b in range(BUFS)]
        stored = [sem(f"final_stored{b}") for b in range(BUFS)]
        index_ready, added, summed, squared = [sem(n) for n in ("row_index_ready", "added", "summed", "squared")]
        mean_ready, root_ready, scaled = sem("mean_ready"), sem("root_ready"), sem("scaled")
        block = ctx.enter_context(nc.Block())

        def steps(engine, step):
            step(0)
            with engine.Fori(1, STEPS - 1) as j:
                step(j)
            step(STEPS - 1)

        def is_last(j):
            return isinstance(j, int) and j == STEPS - 1

        def is_first(j):
            return isinstance(j, int) and j == 0

        @block.sync
        def _(sp):
            def load(j, b):
                row = snap(sp, j * (BUFS * P) + b * P)
                sp.dma_start(xs[b][:], x2[bass.ds(row, P), :]).then_inc(x_in[b], 16)

            def step(j):
                for b in range(BUFS):
                    row = snap(sp, j * (BUFS * P) + b * P)
                    sp.wait_ge(scaled, snap(sp, j * BUFS + (b + 1)))
                    sp.dma_start(out[0, bass.ds(row, P), :], outs[b][:]).then_inc(stored[b], 16)
                    if not is_last(j):
                        load(j + 1, b)

            for b in range(BUFS):
                load(0, b)
            sp.dma_start(gain[:], ins["g_final"].unsqueeze(0).broadcast_to((P, D))).then_inc(gain_in, 16)
            steps(sp, step)
            for b in range(BUFS):
                sp.wait_ge(stored[b], 16 * (STEPS))

        @block.gpsimd
        def _(pool):
            def gather(j, b):
                for c in range(2):
                    pool.tensor_copy(index[b][c][:], routed.rows[:, c, bass.ds(j * BUFS + b, 1)]).then_inc(index_ready, 1)
                wait_apart(pool, passed, (index_ready, j * (2 * BUFS) + (2 * b + 2)))
                for c in range(2):
                    pool.indirect_dma_start(out=ys[b][c][:], out_offset=None, in_=y[:, :],
                                            in_offset=bass.IndirectOffsetOnAxis(ap=index[b][c][:, :1], axis=0)).then_inc(y_in[b], 16)

            def step(j):
                for b in range(BUFS):
                    n = j * BUFS + (b + 1)
                    if not is_last(j):
                        wait_apart(pool, passed, (summed, n))
                        gather(j + 1, b)
                    wait_apart(pool, passed, (squared, n))
                    if not is_first(j):
                        wait_apart(pool, passed, (scaled, n - BUFS))
                    pool.tensor_scalar(r[:, b:b + 1], ss[:, b:b + 1], 1.0 / D, EPS, ALU.mult, ALU.add).then_inc(mean_ready, 1)
                    pool.wait_ge(mean_ready, snap(pool, n))
                    pool.tensor_tensor(r[:, b:b + 1], r[:, b:b + 1], half[:], ALU.pow).then_inc(root_ready, 1)

            pool.memset(half[:], -0.5).then_inc(half_set, 1)
            pool.wait_ge(half_set, 1)
            for b in range(BUFS):
                gather(0, b)
            steps(pool, step)

        @block.scalar
        def _(act):
            def step(j):
                for b in range(BUFS):
                    n = j * BUFS + (b + 1)
                    act.wait_ge(summed, snap(act, n))
                    if not (is_first(j) and b == 0):
                        act.wait_ge(squared, snap(act, n - 1))
                    if not is_first(j):
                        act.wait_ge(mean_ready, snap(act, n - BUFS))
                    act.activation(square[:], xs[b][:], ACT.Square, accum_out=ss[:, b:b + 1]).then_inc(squared, 1)

            steps(act, step)

        @block.vector
        def _(dve):
            def step(j):
                for b in range(BUFS):
                    n = j * BUFS + (b + 1)
                    gate = lambda c: routed.gates[:, c, bass.ds(j * BUFS + b, 1)]
                    dve.wait_ge(x_in[b], snap(dve, j * 16 + 16))
                    dve.wait_ge(y_in[b], snap(dve, j * 32 + 32))
                    dve.scalar_tensor_tensor(xs[b][:], ys[b][0][:], gate(0), xs[b][:], ALU.mult, ALU.add).then_inc(added, 1)
                    dve.wait_ge(added, snap(dve, n))
                    dve.scalar_tensor_tensor(xs[b][:], ys[b][1][:], gate(1), xs[b][:], ALU.mult, ALU.add).then_inc(summed, 1)
                for b in range(BUFS):
                    n = j * BUFS + (b + 1)
                    dve.wait_ge(summed, snap(dve, n))
                    dve.wait_ge(root_ready, snap(dve, n))
                    if not is_first(j):
                        dve.wait_ge(stored[b], snap(dve, j * 16))
                    dve.scalar_tensor_tensor(outs[b][:], xs[b][:], r[:, b:b + 1], gain[:], ALU.mult, ALU.mult).then_inc(scaled, 1)

            dve.wait_ge(gain_in, 16)
            steps(dve, step)


def hybrid_layer_kernel(nc, out, **ins):
    dram = lambda name, rows: nc.dram_tensor(name, (rows, D), F32, kind="Internal").ap()
    x1, x2, h3 = dram("x1", SEQ), dram("x2", SEQ), dram("h3", SEQ)
    y = dram("y_rows", 2 * SEQ + SLOT)
    with ExitStack() as ctx:
        keep = Kept(nc, ctx)
        mixer(nc, keep, ins, x1)
        with Fold(nc) as fold:
            folding(nc, keep, ins, fold)
            xattn(nc, keep, ins, fold, x1, x2, h3)
        routed = Routed(nc, ctx)
        with ExitStack() as moe_ctx:
            staged = Staged(nc, moe_ctx)
            routing(nc, keep, ins, routed, staged, h3)
            moe(nc, keep, ins, routed, staged, h3, y)
        combine(nc, keep, ins, routed, x2, y, out)


_INS = ["x", "mem", "g_mix", "w_in", "conv_w", "g_v", "w_s", "b_s", "g_out_conv", "g_out_gmlp", "w_out",
        "g_xattn", "g_mem", "w_q", "w_k", "w_v", "w_o", "g_ffn", "w_grp", "b_grp", "w_rt", "b_rt",
        "w_gate", "w_up", "w_down", "g_final"]


def kernel(**inputs):
    import numpy as _np
    import concourse.bacc as _bacc
    from concourse import mybir as _mybir
    from concourse.bass_utils import run_bass_kernel_spmd as _run

    nc = _bacc.Bacc("TRN2", target_bir_lowering=False, num_devices=1)
    arrays, args = {}, {}
    for name in _INS:
        a = _np.ascontiguousarray(inputs[name])
        arrays[f"in_{name}_dram"] = a
        args[name] = nc.dram_tensor(f"in_{name}_dram", a.shape, _mybir.dt.from_np(a.dtype), kind="ExternalInput").ap()
    out = nc.dram_tensor("out_0_dram", (1, SEQ, D), F32, kind="ExternalOutput").ap()
    hybrid_layer_kernel(nc, out, **args)
    r = _run(nc, [arrays], core_ids=[0])
    return r.results[0]["out_0_dram"]
```
